# Optimizing a Trainium2 kernel written in Bass

```python
import math
import jax, jax.numpy as jnp
from jax import lax
import numpy as np

D_MODEL = 1024
BATCH = 1
SEQ = 256
DEPTH = 2

N_AB = (DEPTH + 1) // 2
N_RET = DEPTH // 2

CONV_GROUPS = 8
CONV_WIDTH = D_MODEL // 2
CONV_K = 3
MLA_HEADS = 8
MLA_NOPE = 64
MLA_ROPE = 32
MLA_V = 64
MLA_Q_RANK = 256
MLA_KV_RANK = 128
MLA_WIDTH = MLA_HEADS * MLA_V
Q_BLOCK = 128
ROPE_BASE = 10000.0
AB_IN = 3 * CONV_WIDTH + MLA_Q_RANK + MLA_KV_RANK + MLA_ROPE
AB_OUT = CONV_WIDTH + MLA_WIDTH
AB_SPLITS = (CONV_WIDTH, 2 * CONV_WIDTH, 3 * CONV_WIDTH,
             3 * CONV_WIDTH + MLA_Q_RANK, 3 * CONV_WIDTH + MLA_Q_RANK + MLA_KV_RANK)
RET_HEADS = 8
RET_DK = D_MODEL // RET_HEADS
RET_DV = 2 * RET_DK
RET_CHUNK = 128
RET_IN = 2 * RET_HEADS * RET_DK + 2 * RET_HEADS * RET_DV
RET_SPLITS = (RET_HEADS * RET_DK, 2 * RET_HEADS * RET_DK, 2 * RET_HEADS * RET_DK + RET_HEADS * RET_DV)
N_GROUPS = 4
EXPERTS_PER_GROUP = 8
N_EXPERTS = N_GROUPS * EXPERTS_PER_GROUP
TOP_K = 2
D_EXPERT = 256
LN_EPS = 1e-5
RMS_EPS = 1e-6
DEEPNORM_ALPHA = (2 * DEPTH) ** 0.25
DEEPNORM_BETA = (8 * DEPTH) ** -0.25

kernel_name = 'hybrid_conv_mla_retention_hmoe'

def layer_norm(x, g, b):
    xf = x.astype(jnp.float32)
    mu = jnp.mean(xf, axis=-1, keepdims=True)
    var = jnp.mean(jnp.square(xf - mu), axis=-1, keepdims=True)
    y = (xf - mu) * lax.rsqrt(var + LN_EPS)
    return (y * g.astype(jnp.float32) + b.astype(jnp.float32)).astype(x.dtype)

def rms_norm(x, g):
    xf = x.astype(jnp.float32)
    y = xf * lax.rsqrt(jnp.mean(jnp.square(xf), axis=-1, keepdims=True) + RMS_EPS)
    return (y * g.astype(jnp.float32)).astype(x.dtype)

def rope_tables(positions, dim):
    inv = ROPE_BASE ** (-jnp.arange(0, dim, 2, dtype=jnp.float32) / dim)
    ang = positions.astype(jnp.float32)[..., None] * inv
    return jnp.cos(ang), jnp.sin(ang)

def apply_rope(x, cos, sin):
    xf = x.astype(jnp.float32)
    half = x.shape[-1] // 2
    x1, x2 = xf[..., :half], xf[..., half:]
    c, s = cos[:, :, None, :], sin[:, :, None, :]
    return jnp.concatenate([x1 * c - x2 * s, x2 * c + x1 * s], axis=-1).astype(x.dtype)

def adaln(c, w, b):
    m = jax.nn.silu(c) @ w + b
    shift, scale, gate = jnp.split(m, 3, axis=-1)
    return shift, scale, gate

def modulate(x, shift, scale):
    return x * (1.0 + scale[:, None, :]) + shift[:, None, :]

def short_conv_mix(a_x, a_b, a_c, conv_w):
    u = a_c * a_x
    s = u.shape[1]
    up = jnp.pad(u, ((0, 0), (CONV_K - 1, 0), (0, 0)))
    y = conv_w[0] * up[:, 0:s]
    for j in range(1, CONV_K):
        y = y + conv_w[j] * up[:, j:j + s]
    return a_b * y

def causal_attention_blocks(q, k, v):
    b, s, h, dqk = q.shape
    nb = s // Q_BLOCK
    scale = dqk ** -0.5
    qb = q.reshape(b, nb, Q_BLOCK, h, dqk).transpose(1, 0, 2, 3, 4)
    k_idx = jnp.arange(s)

    def one_block(args):
        i, qi = args
        sc = jnp.einsum('bqhd,bkhd->bhqk', qi, k).astype(jnp.float32) * scale
        q_idx = i * Q_BLOCK + jnp.arange(Q_BLOCK)
        sc = jnp.where(k_idx[None, :] <= q_idx[:, None], sc, -jnp.inf)
        p = jax.nn.softmax(sc, axis=-1).astype(v.dtype)
        return jnp.einsum('bhqk,bkhd->bqhd', p, v)

    o = lax.map(one_block, (jnp.arange(nb), qb))
    return o.transpose(1, 0, 2, 3, 4).reshape(b, s, h, v.shape[-1])

def mla_mix(q_c, kv_c, k_r, q_norm_g, kv_norm_g, w_uq, w_ukv, cos, sin):
    b, s, _ = q_c.shape
    q = (rms_norm(q_c, q_norm_g) @ w_uq).reshape(b, s, MLA_HEADS, MLA_NOPE + MLA_ROPE)
    q = jnp.concatenate([q[..., :MLA_NOPE], apply_rope(q[..., MLA_NOPE:], cos, sin)], axis=-1)
    kv = (rms_norm(kv_c, kv_norm_g) @ w_ukv).reshape(b, s, MLA_HEADS, MLA_NOPE + MLA_V)
    k_nope, v = kv[..., :MLA_NOPE], kv[..., MLA_NOPE:]
    k_rope = apply_rope(k_r[:, :, None, :], cos, sin)
    k = jnp.concatenate([k_nope, jnp.broadcast_to(k_rope, (b, s, MLA_HEADS, MLA_ROPE))], axis=-1)
    o = causal_attention_blocks(q, k, v)
    return o.reshape(b, s, MLA_WIDTH)

def ab_mixer(h, w_in, conv_w, q_norm_g, kv_norm_g, w_uq, w_ukv, w_out, cos, sin):
    p = h @ w_in
    a_x, a_b, a_c, q_c, kv_c, k_r = jnp.split(p, AB_SPLITS, axis=-1)
    y_a = short_conv_mix(a_x, a_b, a_c, conv_w)
    y_b = mla_mix(q_c, kv_c, k_r, q_norm_g, kv_norm_g, w_uq, w_ukv, cos, sin)
    return jnp.concatenate([y_a, y_b], axis=-1) @ w_out

def chunkwise_retention(q, k, v):
    b, s, h, dk = q.shape
    dv = v.shape[-1]
    nc = s // RET_CHUNK
    lg = jnp.log1p(-jnp.exp2(-5.0 - jnp.arange(h, dtype=jnp.float32)))
    n = jnp.arange(RET_CHUNK, dtype=jnp.float32)
    diff = n[:, None] - n[None, :]
    inner_decay = jnp.where(diff >= 0, jnp.exp(lg[:, None, None] * jnp.maximum(diff, 0.0)), 0.0)
    q_decay = jnp.exp(lg[:, None] * (n + 1.0))
    k_decay = jnp.exp(lg[:, None] * (RET_CHUNK - 1.0 - n))
    chunk_decay = jnp.exp(lg * RET_CHUNK)

    def to_chunks(t):
        return t.astype(jnp.float32).reshape(b, nc, RET_CHUNK, h, -1).transpose(1, 0, 3, 2, 4)

    def step(state, inp):
        qc, kc, vc = inp
        sc = jnp.einsum('bhnd,bhmd->bhnm', qc, kc) * inner_decay
        o = jnp.einsum('bhnm,bhme->bhne', sc, vc) \
            + jnp.einsum('bhnd,bhde->bhne', qc * q_decay[..., None], state)
        state = chunk_decay[:, None, None] * state \
            + jnp.einsum('bhmd,bhme->bhde', kc * k_decay[..., None], vc)
        return state, o

    state0 = jnp.zeros((b, h, dk, dv), jnp.float32)
    _, o = lax.scan(step, state0, (to_chunks(q), to_chunks(k), to_chunks(v)))
    return o.transpose(1, 0, 3, 2, 4).reshape(b, s, h, dv)

def head_group_norm(o, g):
    mu = jnp.mean(o, axis=-1, keepdims=True)
    var = jnp.mean(jnp.square(o - mu), axis=-1, keepdims=True)
    y = (o - mu) * lax.rsqrt(var + LN_EPS)
    return y * g.astype(jnp.float32).reshape(RET_HEADS, RET_DV)

def retention_mixer(h, w_in, gn_g, w_out, cos, sin):
    b, s, _ = h.shape
    p = h @ w_in
    q, k, v, g = jnp.split(p, RET_SPLITS, axis=-1)
    q = apply_rope(q.reshape(b, s, RET_HEADS, RET_DK), cos, sin)
    k = apply_rope(k.reshape(b, s, RET_HEADS, RET_DK), cos, sin) * (RET_DK ** -0.5)
    v = v.reshape(b, s, RET_HEADS, RET_DV)
    o = head_group_norm(chunkwise_retention(q, k, v), gn_g).astype(h.dtype)
    y = jax.nn.silu(g) * o.reshape(b, s, RET_HEADS * RET_DV)
    return y @ w_out

def hier_moe(h, rg_w, rg_b, re_w, re_b, w_gate, w_up, w_down):
    b, s, d = h.shape
    hf = h.reshape(-1, d)
    g_prob = jax.nn.softmax((hf @ rg_w + rg_b).astype(jnp.float32), axis=-1)
    g_p, g_idx = lax.top_k(g_prob, 1)
    e_logits = (hf @ re_w + re_b).astype(jnp.float32).reshape(-1, N_GROUPS, EXPERTS_PER_GROUP)
    e_sel = jnp.take_along_axis(e_logits, g_idx[:, :, None], axis=1)[:, 0]
    e_prob = jax.nn.softmax(e_sel, axis=-1)
    e_p, e_idx = lax.top_k(e_prob, TOP_K)
    w = g_p * e_p / jnp.sum(e_p, axis=-1, keepdims=True)
    ids = g_idx * EXPERTS_PER_GROUP + e_idx
    combine = jnp.einsum('tk,tke->te', w, jax.nn.one_hot(ids, N_EXPERTS, dtype=jnp.float32))

    def expert_step(acc, params):
        wg, wu, wd, cw = params
        y = (jax.nn.silu(hf @ wg) * (hf @ wu)) @ wd
        return acc + cw[:, None] * y.astype(jnp.float32), None

    acc, _ = lax.scan(expert_step, jnp.zeros(hf.shape, jnp.float32),
                      (w_gate, w_up, w_down, combine.T))
    return acc.astype(h.dtype).reshape(b, s, d)

def setup_inputs(seed: int = 0) -> dict:
    key = jax.random.key(seed)
    ks = jax.random.split(key, 32)
    f32 = jnp.float32
    nrm = lambda k, shp, sc: jax.random.normal(k, shp, f32) * sc
    D = D_MODEL
    x = nrm(ks[0], (BATCH, SEQ, D), 1.0)
    c = nrm(ks[1], (BATCH, D), 1.0)
    positions = jnp.broadcast_to(jnp.arange(SEQ, dtype=jnp.int32)[None, :], (BATCH, SEQ))
    return {
        'x': x,
        'c': c,
        'positions': positions,
        'ada_mix_w': nrm(ks[2], (DEPTH, D, 3 * D), 0.2 * D ** -0.5),
        'ada_mix_b': nrm(ks[3], (DEPTH, 3 * D), 0.01),
        'ln_mix_g': 1.0 + nrm(ks[4], (DEPTH, D), 0.01),
        'ln_mix_b': nrm(ks[5], (DEPTH, D), 0.01),
        'ab_w_in': nrm(ks[6], (N_AB, D, AB_IN), D ** -0.5),
        'ab_conv_w': nrm(ks[7], (N_AB, CONV_K, CONV_WIDTH), CONV_K ** -0.5),
        'ab_q_norm_g': 1.0 + nrm(ks[8], (N_AB, MLA_Q_RANK), 0.01),
        'ab_kv_norm_g': 1.0 + nrm(ks[9], (N_AB, MLA_KV_RANK), 0.01),
        'ab_w_uq': nrm(ks[10], (N_AB, MLA_Q_RANK, MLA_HEADS * (MLA_NOPE + MLA_ROPE)), MLA_Q_RANK ** -0.5),
        'ab_w_ukv': nrm(ks[11], (N_AB, MLA_KV_RANK, MLA_HEADS * (MLA_NOPE + MLA_V)), MLA_KV_RANK ** -0.5),
        'ab_w_out': nrm(ks[12], (N_AB, AB_OUT, D), DEEPNORM_BETA * AB_OUT ** -0.5),
        'ret_w_in': nrm(ks[13], (N_RET, D, RET_IN), D ** -0.5),
        'ret_gn_g': 1.0 + nrm(ks[14], (N_RET, RET_HEADS * RET_DV), 0.01),
        'ret_w_out': nrm(ks[15], (N_RET, RET_HEADS * RET_DV, D), DEEPNORM_BETA * (RET_HEADS * RET_DV) ** -0.5),
        'ada_ffn_w': nrm(ks[16], (DEPTH, D, 3 * D), 0.2 * D ** -0.5),
        'ada_ffn_b': nrm(ks[17], (DEPTH, 3 * D), 0.01),
        'ln_ffn_g': 1.0 + nrm(ks[18], (DEPTH, D), 0.01),
        'ln_ffn_b': nrm(ks[19], (DEPTH, D), 0.01),
        'moe_rg_w': nrm(ks[20], (DEPTH, D, N_GROUPS), D ** -0.5),
        'moe_rg_b': nrm(ks[21], (DEPTH, N_GROUPS), 0.01),
        'moe_re_w': nrm(ks[22], (DEPTH, D, N_EXPERTS), D ** -0.5),
        'moe_re_b': nrm(ks[23], (DEPTH, N_EXPERTS), 0.01),
        'moe_w_gate': nrm(ks[24], (DEPTH, N_EXPERTS, D, D_EXPERT), D ** -0.5),
        'moe_w_up': nrm(ks[25], (DEPTH, N_EXPERTS, D, D_EXPERT), D ** -0.5),
        'moe_w_down': nrm(ks[26], (DEPTH, N_EXPERTS, D_EXPERT, D), DEEPNORM_BETA * D_EXPERT ** -0.5),
    }

def reference(x, c, positions, ada_mix_w, ada_mix_b, ln_mix_g, ln_mix_b,
              ab_w_in, ab_conv_w, ab_q_norm_g, ab_kv_norm_g, ab_w_uq, ab_w_ukv, ab_w_out,
              ret_w_in, ret_gn_g, ret_w_out,
              ada_ffn_w, ada_ffn_b, ln_ffn_g, ln_ffn_b,
              moe_rg_w, moe_rg_b, moe_re_w, moe_re_b, moe_w_gate, moe_w_up, moe_w_down):
    cos_m, sin_m = rope_tables(positions, MLA_ROPE)
    cos_r, sin_r = rope_tables(positions, RET_DK)
    for l in range(DEPTH):
        shift, scale, gate = adaln(c, ada_mix_w[l], ada_mix_b[l])
        h = modulate(x, shift, scale)
        if l % 2 == 0:
            i = l // 2
            y = ab_mixer(h, ab_w_in[i], ab_conv_w[i], ab_q_norm_g[i], ab_kv_norm_g[i],
                         ab_w_uq[i], ab_w_ukv[i], ab_w_out[i], cos_m, sin_m)
        else:
            i = l // 2
            y = retention_mixer(h, ret_w_in[i], ret_gn_g[i], ret_w_out[i], cos_r, sin_r)
        x = layer_norm(DEEPNORM_ALPHA * x + (1.0 + gate[:, None, :]) * y, ln_mix_g[l], ln_mix_b[l])
        shift, scale, gate = adaln(c, ada_ffn_w[l], ada_ffn_b[l])
        h = modulate(x, shift, scale)
        y = hier_moe(h, moe_rg_w[l], moe_rg_b[l], moe_re_w[l], moe_re_b[l],
                     moe_w_gate[l], moe_w_up[l], moe_w_down[l])
        x = layer_norm(DEEPNORM_ALPHA * x + (1.0 + gate[:, None, :]) * y, ln_ffn_g[l], ln_ffn_b[l])
    return x


_drawn_inputs = setup_inputs


def setup_inputs(seed=0):
    import zlib

    import numpy as np

    out = dict(_drawn_inputs(seed))
    spreads = {}
    factors = {'ada_mix_b': 3.686,
     'ln_mix_g': 2.976,
     'ab_q_norm_g': 8.0,
     'ab_kv_norm_g': 8.0,
     'ret_gn_g': 8.0,
     'ada_ffn_b': 3.609,
     'ln_ffn_g': 3.369,
     'ln_ffn_b': 2.995,
     'moe_rg_b': 8.0,
     'moe_re_b': 8.0}
    for name, (base, spread) in spreads.items():
        noise = np.random.default_rng([zlib.crc32(name.encode()), seed]).standard_normal(out[name].shape)
        drawn = base * np.exp(spread * noise) if base else spread * noise
        out[name] = __import__('jax').numpy.asarray(drawn.astype(out[name].dtype))
    for name, factor in factors.items():
        out[name] = (out[name] * factor).astype(out[name].dtype)
    return out
```

```python
from contextlib import ExitStack

import numpy as np

import concourse.bass as bass
from concourse import mybir

ALU = mybir.AluOpType
ACT = mybir.ActivationFunctionType
AX = mybir.AxisListType
F32 = mybir.dt.float32
I32 = mybir.dt.int32
U32 = mybir.dt.uint32

P = 128
D = 1024
SEQ = 256
TT = SEQ // P
KD = D // P
DEPTH = 2
SUBLAYERS = 2 * DEPTH
ALPHA = float(2 * DEPTH) ** 0.25
LN_EPS, RMS_EPS = 1e-5, 1e-6
HALF = 512

CONV = 512
CT = CONV // P
QR, KVR, ROPE, NOPE, HV, HEADS = 256, 128, 32, 64, 64, 8
LOWRANK = QR + KVR + ROPE
QK = NOPE + ROPE
MLA_SCALE = float(QK) ** -0.5

RH, DK, DV = 8, 128, 256
RQ = RH * DK
RV = RH * DV
RET_CHUNKS = (2 * RQ + 2 * RV) // HALF

GROUPS, PER_GROUP = 4, 8
EXPERTS = GROUPS * PER_GROUP
FE = 256
KF = FE // P
SLOTS = 64
PAIRS = EXPERTS // 2

C_ID, C_ONE, C_UP, C_MASK = 0, 128, 256, 384
C_SLOT = 768
C_EXP = C_SLOT + SLOTS
C_INVM = C_EXP + EXPERTS
C_INVR = C_INVM + ROPE // 2
C_N = C_INVR + DK // 2

TWO_PI = 2 * np.pi
PI_A = float(np.float32(6.28125))
PI_B = float(np.float32(np.float64(TWO_PI) - 6.28125))
PI_C = float(np.float32(TWO_PI - 6.28125 - np.float64(np.float32(TWO_PI - 6.28125))))
ROUND = float(1.5 * 2 ** 23)
SIN_MAX = 3.1415925


def shape_constants():
    t = np.zeros((P, C_N), np.float32)
    t[:, C_ID:C_ID + P] = np.eye(P)
    t[:, C_ONE:C_ONE + P] = 1.0
    t[:, C_UP:C_UP + P] = np.triu(np.ones((P, P)), 1)
    causal = np.where(np.arange(P)[None, :] <= np.arange(P)[:, None], 0.0, -1e30)
    t[:, C_MASK:C_MASK + P] = causal
    t[:, C_MASK + 2 * P:C_MASK + 3 * P] = causal
    t[:, C_SLOT:C_SLOT + SLOTS] = np.arange(SLOTS)
    t[:, C_EXP:C_EXP + EXPERTS] = np.arange(EXPERTS)
    for at, dim in ((C_INVM, ROPE), (C_INVR, DK)):
        inv = np.float32(10000.0) ** (-np.arange(0, dim, 2, dtype=np.float32) / np.float32(dim))
        t[:, at:at + dim // 2] = inv
    lg = np.log1p(-np.exp2(-5.0 - np.arange(RH)))
    lag = np.arange(SEQ)[None, :] - np.arange(P)[:, None]
    decay = np.where(lag[:, None, :] >= 0, np.exp(lg[None, :, None] * np.maximum(lag, 0)[:, None, :]), 0.0)
    decay = decay * DK ** -0.5
    return t, np.ascontiguousarray(decay.astype(np.float32).reshape(P, RH * SEQ))


class Chain:

    def __init__(self, eng, sem):
        self.eng, self.sem, self.n, self.moving = eng, sem, 0, None

    def value(self):
        return self.n if self.moving is None else self.moving + self.n

    def step(self, ins):
        self.n += 1
        ins.then_inc(self.sem, 1)

    def hold(self):
        self.eng.wait_ge(self.sem, self.value())

    def link(self, ins):
        self.step(ins)
        self.hold()

    def enter(self, i, per):
        self.before, self.per = self.n, per
        self.moving, self.n = self.before + per * i, 0

    def again(self):
        assert self.n == self.per, (self.n, self.per)

    def leave(self, times):
        self.moving, self.n = None, self.before + self.per * times


def build(nc, a, out):
    ctx = ExitStack()
    with ctx:
        def sb(name, shape, dt=F32):
            return ctx.enter_context(nc.sbuf_tensor(name, shape, dt))

        def sem(name):
            return ctx.enter_context(nc.semaphore(name))

        W = sb("W", [P, 24576])
        M = sb("M", [P, 16384])
        acc_b = sb("acc_b", [P, 3 * D])
        x = sb("x", [P, TT, D])
        hT = sb("hT", [P, KD, SEQ])
        gate = sb("gate", [P, D])
        ln_g = sb("ln_g", [P, D])
        ln_b = sb("ln_b", [P, D])
        cst = sb("cst", [P, C_N])
        router_w = sb("router_w", [P, KD, GROUPS + EXPERTS])
        router_b = sb("router_b", [1, GROUPS + EXPERTS])
        gains = sb("gains", [P, 31])
        gn_g, q_g, kv_g = gains[:, 0:16], gains[:, 16:18], gains[:, 18:19]
        conv_w = gains[:, 19:31].rearrange("p (j c) -> p j c", j=3)
        gain_rows = acc_b[0:31, 0:P]
        pos_i = acc_b[0:TT, P:2 * P].bitcast(I32)
        pos_r = acc_b[0:TT, 2 * P:3 * P]
        bias_c = sb("bias_c", [P, SUBLAYERS, 2, KD])
        mod_c = sb("mod_c", [P, 2, KD])
        c_in = sb("c_in", [P, KD])
        c_silu = sb("c_silu", [P, KD])
        pos_f = sb("pos_f", [P, TT])
        trig_m = sb("trig_m", [P, 2, TT, ROPE // 2])
        trig_r = sb("trig_r", [P, 2, TT, DK // 2])
        stats = sb("stats", [P, TT, 2, 6])
        mv = sb("mv", [P, TT, 2])
        std = sb("std", [P, TT])
        rstd = sb("rstd", [P, TT])
        over = sb("over", [1, 1], I32)
        over_f = sb("over_f", [P, 1])
        PS = ctx.enter_context(nc.psum_tensor("PS", [P, 8, HALF], F32))

        ident = cst[:, C_ID:C_ID + P]
        ones = cst[:, C_ONE:C_ONE + P]
        upper = cst[:, C_UP:C_UP + P]
        acc_a = M[:, 13312:16384]
        ada_buf = [M[:, 7168 + 3072 * j:7168 + 3072 * (j + 1)] for j in range(2)]
        sums = [acc_a, acc_b[:, :], acc_a, acc_b[:, :]]
        y_acc = M[:, 0:2048].rearrange("p (t d) -> p t d", t=TT)

        in_ld = sem("in_ld")
        pos_rows = sem("pos_rows")
        columns_ps = sem("columns_ps")
        ada_ld = [sem("ada_ld0"), sem("ada_ld1")]
        c_silu_ready = sem("c_silu_ready")
        ada_used = sem("ada_used")
        bias_ld = sem("bias_ld")
        ln_ld = sem("ln_ld")
        cols_ps = sem("cols_ps")
        cols_ready = sem("cols_ready")
        gate_ps = sem("gate_ps")
        gate_ready = sem("gate_ready")
        xT_ps = sem("xT_ps")
        hT_even = sem("hT_even")
        hT_odd = sem("hT_odd")
        var_ready = sem("var_ready")
        std_ready = sem("std_ready")
        x_ready = sem("x_ready")
        y_ps = sem("y_ps")
        dve_chain = sem("dve_chain")
        act_chain = sem("act_chain")
        angle_ready = sem("angle_ready")
        trig_ready = sem("trig_ready")
        lowrank_ld = sem("lowrank_ld")
        convw_ld = [sem(f"conv_ld{j}") for j in range(3)]
        upw_ld = sem("upw_ld")
        out_ld = [sem(f"out_ld{j}") for j in range(4)]
        lowrank_ps = sem("lowrank_ps")
        lowrank_sb = sem("lowrank_sb")
        square_ready = sem("square_ready")
        ms_ready = sem("ms_ready")
        rms_ready = sem("rms_ready")
        lowrank_n = sem("lowrank_n")
        lowT_ps = sem("lowT_ps")
        lowT_ready = sem("lowT_ready")
        conv_ps = sem("conv_ps")
        conv_x_sb = sem("conv_x_sb")
        conv_done = sem("conv_done")
        up_ps = sem("up_ps")
        up_q_sb = sem("up_q_sb")
        up_k_sb = sem("up_k_sb")
        qk_ready = sem("qk_ready")
        qkT_ps = sem("qkT_ps")
        qkT_ready = sem("qkT_ready")
        score_ps = sem("score_ps")
        shift_ready = sem("shift_ready")
        prob_ready = sem("prob_ready")
        probT_ps = sem("probT_ps")
        probT_ready = sem("probT_ready")
        head_ps = sem("head_ps")
        head_sb = sem("head_sb")
        oT_ps = sem("oT_ps")
        oT_ready = sem("oT_ready")
        ret_ld = [sem(f"ret_ld{j}") for j in range(4)]
        decay_ld = sem("decay_ld")
        ret_ps = sem("ret_ps")
        ret_sb = sem("ret_sb")
        rope_ready = sem("rope_ready")
        retT_ps = sem("retT_ps")
        retT_ready = sem("retT_ready")
        rscore_ps = sem("rscore_ps")
        decayed = sem("decayed")
        rhead_ps = sem("rhead_ps")
        rhead_sb = sem("rhead_sb")
        rvar_ready = sem("rvar_ready")
        rstd_ready = sem("rstd_ready")
        ret_y = sem("ret_y")
        ryT_ps = sem("ryT_ps")
        ryT_ready = sem("ryT_ready")
        rw_ld = sem("rw_ld")
        logit_ps = sem("logit_ps")
        gdiff_ready = sem("gdiff_ready")
        gexp_ready = sem("gexp_ready")
        ediff_ready = sem("ediff_ready")
        eexp_ready = sem("eexp_ready")
        mask_ready = sem("mask_ready")
        rank_ps = sem("rank_ps")
        route_ready = sem("route_ready")
        gu_ld = [sem("gu_ld0"), sem("gu_ld1")]
        down_ld = [sem("down_ld0"), sem("down_ld1")]
        sel_ready = sem("sel_ready")
        gath_ps = sem("gath_ps")
        gath_sb = sem("gath_sb")
        gu_ps = sem("gu_ps")
        silu_ready = sem("silu_ready")
        act_ready = sem("act_ready")
        turn_ps = sem("turn_ps")
        turn_sb = sem("turn_sb")
        down_ps = sem("down_ps")
        down_sb = sem("down_sb")
        scat_ps = sem("scat_ps")
        acc_done = sem("acc_done")
        dense = [{n: sem(f"dense{l}_{n}") for n in
                  ("ld", "gu", "silu", "act", "turn", "turned", "down", "added")} for l in range(DEPTH)]
        out_st = sem("out_st")

        n_in = [0]

        block = ctx.enter_context(nc.Block())
        rows8 = lambda w: w.rearrange("(p k) n -> p k n", k=KD)

        w_low = W[:, 0:KD * LOWRANK].rearrange("p (k n) -> p k n", k=KD)
        at = KD * LOWRANK
        w_conv = [W[:, at + 4096 * j:at + 4096 * (j + 1)].rearrange("p (k n) -> p k n", k=KD) for j in range(3)]
        at += 3 * 4096
        w_uq = W[:, at:at + 1536].rearrange("p (k n) -> p k n", k=QR // P)
        w_ukv = W[:, at + 1536:at + 2560]
        w_out0 = W[:, 0:8192].rearrange("p (k n) -> p k n", k=KD)
        at += 2560
        qT0 = W[0:QK, at:at + 2048].rearrange("p (h t) -> p h t", h=HEADS)
        kT0 = W[0:QK, at + 2048:at + 4096].rearrange("p (h t) -> p h t", h=HEADS)
        k_sb = W[:, at + 4096:at + 5632].rearrange("p (t h c) -> p t h c", t=TT, h=HEADS)
        prob = W[:, at + 5632:at + 6400].rearrange("p (b c) -> p b c", b=2)
        assert at + 6400 == 24576
        low = M[:, 0:832].rearrange("p (t c) -> p t c", t=TT)
        conv_x = M[:, 832:1856].rearrange("p (c t) -> p c t", c=CT)
        score = M[:, 832:1600].rearrange("p (b c) -> p b c", b=2)
        conv_u = M[:, 1856:1856 + CT * (SEQ + 2)].rearrange("p (c t) -> p c t", c=CT)
        yT0 = M[:, 2888:4936].rearrange("p (k t) -> p k t", k=KD)
        lowT = M[:, 4936:5704].rearrange("p (k t) -> p k t", k=3)
        probT = M[:, 5704:6472].rearrange("p (b c) -> p b c", b=2)
        soft = M[:, 6472:6600]
        low_sq = M[:, 6600:6856]
        q_sb = acc_a[:, 0:1536].rearrange("p (t h c) -> p t h c", t=TT, h=HEADS)
        v_sb = acc_a[:, 1536:2560].rearrange("p (t h c) -> p t h c", t=TT, h=HEADS)
        hflat = hT[:, :, :].rearrange("p k t -> p (k t)")
        o_sb = hflat[:, 0:1024].rearrange("p (t c) -> p t c", t=TT)
        rope_t = [hflat[:, 1024 + 256 * j:1280 + 256 * j] for j in range(4)]

        w_ret = [W[:, 4096 * j:4096 * (j + 1)].rearrange("p (k n) -> p k n", k=KD) for j in range(4)]
        w_out1 = W[:, 0:16384].rearrange("p (k n) -> p k n", k=RV // P)
        rope_r = [W[:, 20480 + 512 * j:20992 + 512 * j].rearrange("p (h c) -> p h c", h=RH) for j in range(4)]
        decay = W[:, 22528:24576].rearrange("p (h t) -> p h t", h=RH)
        v1 = M[:, 0:4096].rearrange("p (t c) -> p t c", t=TT)
        g1 = M[:, 4096:8192].rearrange("p (t c) -> p t c", t=TT)
        qkT1 = [M[:, 8192 + 2048 * j:10240 + 2048 * j].rearrange("p (h t) -> p h t", h=RH) for j in range(2)]
        raw1 = M[:, 12288:14336].rearrange("p (t h c) -> p t h c", t=TT, h=RH)
        turned1 = M[:, 14336:16384].rearrange("p (t h c) -> p t h c", t=TT, h=RH)
        o1 = M[:, 12288:16384].rearrange("p (t c) -> p t c", t=TT)
        yT1 = M[:, 8192:12288].rearrange("p (k t) -> p k t", k=RV // P)
        sT1 = hflat[:, 0:768].rearrange("p (b c) -> p b c", b=2)
        rstat = hflat[:, 768:864].rearrange("p (t h c) -> p t h c", t=TT, h=RH)
        rmv = hflat[:, 864:896].rearrange("p (t h c) -> p t h c", t=TT, h=RH)
        rsd = hflat[:, 896:912].rearrange("p (t h) -> p t h", t=TT)
        rrs = hflat[:, 912:928].rearrange("p (t h) -> p t h", t=TT)

        w_gu = [W[:, 12288 * b:12288 * b + 8192].rearrange("p (u e k f) -> p u e k f", u=2, e=2, k=KD) for b in range(2)]
        w_down = [W[:, 12288 * b + 8192:12288 * (b + 1)].rearrange("p (e k n) -> p e k n", e=2, k=KF) for b in range(2)]
        xselT = M[:, 2048:3072].rearrange("p (k s) -> p k s", k=KD)
        y_sel = M[:, 3072:4096]
        sel = [M[:, 4096 + 256 * b:4352 + 256 * b].rearrange("p (t e s) -> p t e s", t=TT, e=2) for b in range(2)]
        sel_w = [M[:, 4608 + 256 * b:4864 + 256 * b].rearrange("p (t e s) -> p t e s", t=TT, e=2) for b in range(2)]
        turn = [M[:, 5120 + 512 * b:5632 + 512 * b] for b in range(2)]
        silu_sb = M[:, 6144:6400]
        act_sb = M[:, 6400:6656]
        r = M[:, 6656:7168]
        rank = r[:, 0:64].rearrange("p (t e) -> p t e", t=TT)
        cw = r[:, 64:128].rearrange("p (t e) -> p t e", t=TT)
        cw_over = r[:, 128:192].rearrange("p (t e) -> p t e", t=TT)
        mask = r[:, 192:256].rearrange("p (t e) -> p t e", t=TT)
        eq2 = r[:, 256:320].rearrange("p (t e) -> p t e", t=TT)
        g_pad = r[:, 320:336].rearrange("p (t e) -> p t e", t=TT)
        mx = r[:, 336:352].rearrange("p (t e) -> p t e", t=TT)
        mi = r[:, 352:368].bitcast(U32).rearrange("p (t e) -> p t e", t=TT)
        d4 = r[:, 368:376].rearrange("p (t e) -> p t e", t=TT)
        oh4 = r[:, 376:384].rearrange("p (t e) -> p t e", t=TT)
        e_sel = r[:, 384:400].rearrange("p (t e) -> p t e", t=TT)
        e_prod = r[:, 400:464].rearrange("p (t j g) -> p t j g", t=TT, j=PER_GROUP)
        g_sum = r[:, 464:466]
        g_p = r[:, 466:468].rearrange("p (t e) -> p t e", t=TT)
        g_i = r[:, 468:470].rearrange("p (t e) -> p t e", t=TT)
        g_8 = r[:, 470:472].rearrange("p (t e) -> p t e", t=TT)
        e_d = r[:, 472:474].rearrange("p (t e) -> p t e", t=TT)
        e_x = r[:, 474:476].rearrange("p (t e) -> p t e", t=TT)
        w_1 = r[:, 476:478].rearrange("p (t e) -> p t e", t=TT)
        w_2 = r[:, 478:480].rearrange("p (t e) -> p t e", t=TT)
        e_id = r[:, 480:484].rearrange("p (t e) -> p t e", t=TT)
        den = r[:, 484:486].rearrange("p (t e) -> p t e", t=TT)
        GATH, GU, DOWN, SCAT, TURN = (0, 1), 2, (3, 4), (5, 6), 7

        ada_w = [a["ada_mix_w"][0], a["ada_ffn_w"][0], a["ada_mix_w"][1], a["ada_ffn_w"][1]]
        ada_b = [a["ada_mix_b"][0], a["ada_ffn_b"][0], a["ada_mix_b"][1], a["ada_ffn_b"][1]]
        lng_d = [a["ln_mix_g"][0], a["ln_ffn_g"][0], a["ln_mix_g"][1], a["ln_ffn_g"][1]]
        lnb_d = [a["ln_mix_b"][0], a["ln_ffn_b"][0], a["ln_mix_b"][1], a["ln_ffn_b"][1]]
        wg_d = a["moe_w_gate"].rearrange("l e (p k) f -> (l e) p (k f)", k=KD)
        wu_d = a["moe_w_up"].rearrange("l e (p k) f -> (l e) p (k f)", k=KD)
        wd_d = a["moe_w_down"].rearrange("l e (p k) n -> (l e) p (k n)", k=KF)
        IN_LOADS = 12

        @block.sync
        def _(sp):
            def load_ada(s, k, n):
                if n >= 2:
                    sp.wait_ge(ada_used, n - 1)
                sp.dma_start(ada_buf[n % 2], rows8(ada_w[s])[:, k, :]).then_inc(ada_ld[n % 2], 16)

            def load_rows(s):
                if s:
                    sp.wait_ge(x_ready, 2 * s)
                sp.dma_start(ln_g[0:1, :], ada_b[s][2 * D:3 * D].unsqueeze(0)).then_inc(bias_ld, 16)

            def load_ln(s):
                sp.wait_ge(gate_ps, s + 1)
                sp.dma_start(ln_g[:, :], lng_d[s].partition_broadcast(P)).then_inc(ln_ld, 16)
                sp.dma_start(ln_b[:, :], lnb_d[s].partition_broadcast(P)).then_inc(ln_ld, 16)

            def load_experts(l, i, b, moving=None):
                q = PAIRS * l + i
                e = EXPERTS * l + 2 * i
                pair = bass.ds(e, 2)
                if not (isinstance(i, int) and i < 2):
                    sp.wait_ge(gu_ps, q - 1)
                elif l:
                    sp.wait_ge(y_ps, 2 * (2 * l - 1) + 2)
                sp.dma_start(w_gu[b][:, 0], wg_d[pair].rearrange("e p n -> p e n")).then_inc(gu_ld[b], 16)
                sp.dma_start(w_gu[b][:, 1], wu_d[pair].rearrange("e p n -> p e n")).then_inc(gu_ld[b], 16)
                if not (isinstance(i, int) and i < 2):
                    sp.wait_ge(down_ps, 2 * (q - 1))
                sp.dma_start(w_down[b], wd_d[pair].rearrange("e p n -> p e n")).then_inc(down_ld[b], 16)

            def load_router(l):
                if l:
                    sp.wait_ge(logit_ps, l)
                sp.dma_start(router_w[:, :, 0:GROUPS], rows8(a["moe_rg_w"][l])).then_inc(rw_ld, 16)
                sp.dma_start(router_w[:, :, GROUPS:], rows8(a["moe_re_w"][l])).then_inc(rw_ld, 16)
                sp.dma_start(router_b[:, 0:GROUPS], a["moe_rg_b"][l].unsqueeze(0)).then_inc(rw_ld, 16)
                sp.dma_start(router_b[:, GROUPS:], a["moe_re_b"][l].unsqueeze(0)).then_inc(rw_ld, 16)

            def dense_loads(l):
                d = dense[l]
                sp.wait_ge(route_ready, l + 1)
                sp.wait_ge(down_ps, 2 * PAIRS * (l + 1))
                flag = sp.value_load(over[0:1, 0:1])
                with sp.If(flag > 0):
                    def load(e):
                        one = bass.ds(e + EXPERTS * l, 1)
                        sp.dma_start(w_gu[0][:, 0, 0:1], wg_d[one].rearrange("e p n -> p e n")).then_inc(d["ld"], 16)
                        sp.dma_start(w_gu[0][:, 1, 0:1], wu_d[one].rearrange("e p n -> p e n")).then_inc(d["ld"], 16)
                        sp.dma_start(w_down[0][:, 0:1], wd_d[one].rearrange("e p n -> p e n")).then_inc(d["ld"], 16)

                    load(0)
                    with sp.Fori(1, EXPERTS) as e:
                        sp.wait_ge(d["added"], 4 * e)
                        load(e)
                    sp.wait_ge(d["added"], 4 * EXPERTS)

            for dst, src in (
                (c_in[:, :], a["c"][0].rearrange("(p k) -> p k", k=KD)),
                (cst[:, :], a["table"]),
                (x[:, :, :], a["x"][0].rearrange("(t p) d -> p t d", p=P)),
                (pos_i, a["positions"][0].rearrange("(t p) -> t p", p=P)),
                (gain_rows[0:16, :], a["ret_gn_g"][0].rearrange("(k p) -> k p", p=P)),
                (gain_rows[16:18, :], a["ab_q_norm_g"][0].rearrange("(k p) -> k p", p=P)),
                (gain_rows[18:19, :], a["ab_kv_norm_g"][0].rearrange("(k p) -> k p", p=P)),
                (gain_rows[19:31, :], a["ab_conv_w"][0].rearrange("j (c p) -> (j c) p", p=P)),
            ):
                sp.dma_start(dst, src).then_inc(in_ld, 16)
                n_in[0] += 1
            for s in range(SUBLAYERS):
                sp.dma_start(bias_c[:, s, :, :],
                             ada_b[s][0:2 * D].rearrange("(u p k) -> p u k", u=2, k=KD)).then_inc(in_ld, 16)
                n_in[0] += 1
            assert n_in[0] == IN_LOADS
            load_rows(0)
            for k in range(KD):
                load_ada(0, k, k)
            w_in = rows8(a["ab_w_in"][0])
            sp.dma_start(w_low, w_in[:, :, 3 * CONV:]).then_inc(lowrank_ld, 16)
            for j, c in enumerate((0, 2, 1)):
                sp.dma_start(w_conv[j], w_in[:, :, CONV * c:CONV * (c + 1)]).then_inc(convw_ld[j], 16)
            sp.dma_start(w_uq, a["ab_w_uq"][0].rearrange("(k p) n -> p k n", p=P)).then_inc(upw_ld, 16)
            sp.dma_start(w_ukv, a["ab_w_ukv"][0]).then_inc(upw_ld, 16)
            load_router(0)
            load_ln(0)
            for k in range(KD):
                load_ada(1, k, KD + k)
            sp.wait_ge(conv_ps, 6)
            sp.dma_start(w_out0, a["ab_w_out"][0].rearrange("(k p) n -> p k n", p=P)).then_inc(out_ld[0], 16)
            load_rows(1)
            sp.wait_ge(y_ps, 2)
            load_experts(0, 0, 0)
            load_experts(0, 1, 1)
            load_ln(1)
            with sp.Fori(1, PAIRS // 2) as j:
                for b in range(2):
                    load_experts(0, 2 * j + b, b)
                for u, s in enumerate((2, 3)):
                    sp.wait_ge(ada_used, 2 * KD + 2 * (j - 1) + u - 1)
                    sp.dma_start(ada_buf[u], rows8(ada_w[s])[:, bass.ds(j - 1, 1), :]).then_inc(ada_ld[u], 16)
            for u, s in enumerate((2, 3)):
                load_ada(s, KD - 1, 2 * KD + 2 * (KD - 1) + u)
            dense_loads(0)
            load_router(1)
            load_rows(2)
            w_in = rows8(a["ret_w_in"][0])
            sp.wait_ge(down_ps, 2 * PAIRS)
            for c in range(RET_CHUNKS):
                if c >= 4:
                    sp.wait_ge(ret_ps, 2 * (c - 3))
                sp.dma_start(w_ret[c % 4], w_in[:, :, HALF * c:HALF * (c + 1)]).then_inc(ret_ld[c % 4], 16)
                if c == 0:
                    sp.dma_start(W[:, 22528:24576], a["decay"]).then_inc(decay_ld, 16)
                if c == 3:
                    load_ln(2)
            w_o = a["ret_w_out"][0].rearrange("(k p) n -> p k n", p=P)
            for j in range(4):
                sp.wait_ge(ret_ps, 2 * (RET_CHUNKS - 3 + j))
                sp.dma_start(w_out1[:, 4 * j:4 * j + 4, :], w_o[:, 4 * j:4 * j + 4, :]).then_inc(out_ld[j], 16)
            load_rows(3)
            load_experts(1, 0, 0)
            load_experts(1, 1, 1)
            load_ln(3)
            with sp.Fori(1, PAIRS // 2) as j:
                for b in range(2):
                    load_experts(1, 2 * j + b, b)
            dense_loads(1)
            for t in range(TT):
                sp.wait_ge(x_ready, 2 * (SUBLAYERS - 1) + t + 1)
                sp.dma_start(out[0, P * t:P * (t + 1), :], x[:, t, :]).then_inc(out_st, 16)
            sp.wait_ge(out_st, 16 * TT)

        @block.scalar
        def _(act):
            ch = Chain(act, act_chain)

            def h_banks(s):
                for bank in (1, 3):
                    act.wait_ge(xT_ps, 4 * s + bank + 1)
                    act.wait_ge(cols_ready, s + 1)
                    for k in (2 * bank, 2 * bank + 1):
                        ins = act.activation(hT[:, k, :], PS[:, bank, 256 * (k % 2):256 * (k % 2) + 256], ACT.Identity,
                                             bias=mod_c[:, 0, k:k + 1], scale=mod_c[:, 1, k:k + 1])
                    ins.then_inc(hT_odd, 1)

            def norm_std(s):
                for t in range(TT):
                    act.wait_ge(var_ready, 2 * s + t + 1)
                    act.activation(std[:, t:t + 1], mv[:, t, 1:2], ACT.Sqrt).then_inc(std_ready, 1)

            def router(l):
                act.wait_ge(gdiff_ready, l + 1)
                act.activation(d4, d4, ACT.Exp).then_inc(gexp_ready, 1)
                act.wait_ge(ediff_ready, l + 1)
                act.activation(e_x, e_d, ACT.Exp).then_inc(eexp_ready, 1)

            def gathered(l, q):
                for g in range(2):
                    act.wait_ge(gath_ps, 2 * q + g + 1)
                    for k in range(4 * g, 4 * g + 4):
                        ins = act.activation(xselT[:, k, :], PS[:, GATH[g], P * (k % 4):P * (k % 4) + P], ACT.Identity,
                                             bias=mod_c[:, 0, k:k + 1], scale=mod_c[:, 1, k:k + 1])
                    ins.then_inc(gath_sb, 1)

            def pair(l, i, last=False):
                q = PAIRS * l + i
                act.wait_ge(gu_ps, q + 1)
                act.activation(silu_sb, PS[:, GU, 0:FE], ACT.Silu).then_inc(silu_ready, 1)
                if not last:
                    gathered(l, q + 1)
                for h in range(2):
                    act.wait_ge(down_ps, 2 * q + h + 1)
                    act.activation(y_sel[:, HALF * h:HALF * (h + 1)], PS[:, DOWN[h], :], ACT.Copy).then_inc(down_sb, 1)

            def experts(l):
                gathered(l, PAIRS * l)
                with act.Fori(0, PAIRS // 2 - 1) as j:
                    for b in range(2):
                        pair(l, 2 * j + b)
                pair(l, PAIRS - 2)
                pair(l, PAIRS - 1, last=True)
                d = dense[l]
                act.wait_ge(route_ready, l + 1)
                flag = act.value_load(over[0:1, 0:1])
                with act.If(flag > 0):
                    with act.Fori(0, EXPERTS) as e:
                        for t in range(TT):
                            act.wait_ge(d["gu"], 2 * e + t + 1)
                            act.activation(silu_sb, PS[:, GU, 0:FE], ACT.Silu).then_inc(d["silu"], 1)

            act.wait_ge(in_ld, 16 * IN_LOADS)
            act.activation(c_silu[:, :], c_in[:, :], ACT.Silu).then_inc(c_silu_ready, 1)
            act.wait_ge(angle_ready, 4)
            act.activation(trig_m[:, :, :, :], trig_m[:, :, :, :], ACT.Sin)
            act.activation(trig_r[:, :, :, :], trig_r[:, :, :, :], ACT.Sin).then_inc(trig_ready, 1)

            h_banks(0)
            for t in range(TT):
                act.wait_ge(lowrank_sb, t + 1)
                act.activation(low_sq, low[:, t, 0:QR], ACT.Square, accum_out=soft[:, 2 * t:2 * t + 1]).then_inc(square_ready, 1)
                ch.step(act.activation(M[:, 6856:6984], low[:, t, QR:QR + KVR], ACT.Square,
                                       accum_out=soft[:, 2 * t + 1:2 * t + 2]))
                ch.hold()
            act.wait_ge(square_ready, TT)
            act.wait_ge(ms_ready, 2)
            act.activation(soft[:, 8:12], soft[:, 4:8], ACT.Sqrt).then_inc(rms_ready, 1)
            act.wait_ge(conv_ps, 2)
            for h in range(2):
                act.activation(conv_x[:, 2 * h:2 * h + 2, :].rearrange("p c t -> p (c t)"), PS[:, 2 + h, :],
                               ACT.Copy).then_inc(conv_x_sb, 1)
            for t in range(TT):
                for h in range(2):
                    act.wait_ge(up_ps, 2 * t + h + 1)
                    act.activation(q_sb[:, t, 4 * h:4 * h + 4, :],
                                   PS[:, 2 * t + h, 0:4 * QK].rearrange("p (h c) -> p h c", h=4), ACT.Copy).then_inc(up_q_sb, 1)
            for t in range(TT):
                for h in range(2):
                    act.wait_ge(up_ps, 4 + 2 * t + h + 1)
                    src = PS[:, 4 + 2 * t + h, :].rearrange("p (h c) -> p h c", h=4)
                    act.activation(k_sb[:, t, 4 * h:4 * h + 4, 0:NOPE], src[:, :, 0:NOPE], ACT.Copy).then_inc(up_k_sb, 1)
                    act.activation(v_sb[:, t, 4 * h:4 * h + 4, :], src[:, :, NOPE:], ACT.Copy).then_inc(up_k_sb, 1)
            for h in range(HEADS):
                b = h % 2
                act.wait_ge(shift_ready, h + 1)
                if h >= 2:
                    act.wait_ge(probT_ps, h - 1)
                act.activation(prob[:, b, 0:P], score[:, b, 0:P], ACT.Exp, bias=soft[:, 16 + 2 * h:17 + 2 * h],
                               scale=MLA_SCALE, accum_out=soft[:, 32 + 2 * h:33 + 2 * h]).then_inc(prob_ready, 1)
                act.activation(prob[:, b, P:3 * P], score[:, b, P:3 * P], ACT.Exp, bias=soft[:, 17 + 2 * h:18 + 2 * h],
                               scale=MLA_SCALE, accum_out=soft[:, 33 + 2 * h:34 + 2 * h]).then_inc(prob_ready, 1)
            norm_std(0)

            h_banks(1)
            router(0)
            experts(0)
            norm_std(1)

            h_banks(2)
            for c in range(RET_CHUNKS):
                kind = c // 2
                for t in range(TT):
                    n = 2 * c + t
                    act.wait_ge(ret_ps, n + 1)
                    bank = PS[:, n % 4, :]
                    if kind < 2:
                        if kind == 1 and c == 2:
                            act.wait_ge(rope_ready, 2)
                        dst = raw1[:, t, 4 * (c % 2):4 * (c % 2) + 4, :].rearrange("p h c -> p (h c)")
                        act.activation(dst, bank, ACT.Copy).then_inc(ret_sb, 1)
                    elif c < 8:
                        act.activation(v1[:, t, HALF * (c - 4):HALF * (c - 3)], bank, ACT.Copy).then_inc(ret_sb, 1)
                    else:
                        act.activation(g1[:, t, HALF * (c - 8):HALF * (c - 7)], bank, ACT.Silu).then_inc(ret_sb, 1)
            for h in range(RH):
                act.wait_ge(rhead_ps, h + 1)
                for t in range(TT):
                    act.activation(o1[:, t, DV * h:DV * (h + 1)], PS[:, 4 + h % 2, DV * t:DV * (t + 1)],
                                   ACT.Copy).then_inc(rhead_sb, 1)
            act.wait_ge(rvar_ready, 1)
            act.activation(rsd, rsd, ACT.Sqrt).then_inc(rstd_ready, 1)
            norm_std(2)

            h_banks(3)
            router(1)
            experts(1)
            norm_std(3)

        @block.tensor
        def _(pe):
            def adaln(s):
                acc = sums[s]
                pe.wait_ge(ada_used, (KD, 2 * KD, 4 * KD, 4 * KD)[s])
                for u in range(2):
                    part = acc[:, D * u:D * (u + 1)].rearrange("q (p k) -> q k p", k=KD)
                    for k in range(KD):
                        ins = pe.matmul(PS[:, 4, KD * u + k:KD * u + k + 1], part[:, k, :], ones[:, 0:1],
                                        start=True, stop=True)
                ins.then_inc(cols_ps, 1)
                pe.wait_ge(bias_ld, 16 * (s + 1))
                for h in range(2):
                    pe.matmul(PS[:, 5 + h, :], ones, acc[:, 2 * D + HALF * h:2 * D + HALF * (h + 1)], start=True, stop=False)
                    ins = pe.matmul(PS[:, 5 + h, :], ones[0:1, :], ln_g[0:1, HALF * h:HALF * (h + 1)], start=False, stop=True)
                ins.then_inc(gate_ps, 1)

            def turn_x(s):
                if s:
                    pe.wait_ge(x_ready, 2 * s)
                xk = x[:, :, :].rearrange("q t (p k) -> q t k p", k=KD)
                for k in range(KD):
                    for t in range(TT):
                        at = 256 * (k % 2) + P * t
                        ins = pe.transpose(PS[:, k // 2, at:at + P], xk[:, t, k, :], ident)
                    if k % 2:
                        ins.then_inc(xT_ps, 1)

            def h_ready(s):
                pe.wait_ge(hT_even, 2 * (s + 1))
                pe.wait_ge(hT_odd, 2 * (s + 1))

            def router(l):
                h_ready(2 * l + 1)
                pe.wait_ge(gate_ready, 2 * l + 2)
                pe.wait_ge(rw_ld, 64 * (l + 1))
                for t in range(TT):
                    o = PS[:, 4, 64 * t:64 * t + GROUPS + EXPERTS]
                    for k in range(KD):
                        pe.matmul(o, hT[:, k, P * t:P * (t + 1)], router_w[:, k, :], start=(k == 0), stop=False)
                    ins = pe.matmul(o, ones[0:1, :], router_b[0:1, :], start=False, stop=True)
                ins.then_inc(logit_ps, 1)
                pe.wait_ge(mask_ready, l + 1)
                pe.matmul(PS[:, 5, 0:32], upper, mask[:, 0, :], start=True, stop=True)
                pe.matmul(PS[:, 5, 32:64], ones, mask[:, 0, :], start=True, stop=False)
                pe.matmul(PS[:, 5, 32:64], upper, mask[:, 1, :], start=False, stop=True)
                pe.matmul(PS[:, 5, 64:96], ones, mask[:, 0, :], start=True, stop=False)
                pe.matmul(PS[:, 5, 64:96], ones, mask[:, 1, :], start=False, stop=True).then_inc(rank_ps, 1)

            xk_all = x[:, :, :].rearrange("q t (p k) -> q t k p", k=KD)

            def gather(q, b):
                pe.wait_ge(sel_ready, q + 1)
                for g in range(2):
                    for k in range(4 * g, 4 * g + 4):
                        o = PS[:, GATH[g], P * (k % 4):P * (k % 4) + P]
                        for t in range(TT):
                            ins = pe.matmul(o, xk_all[:, t, k, :], sel[b][:, t].rearrange("p e s -> p (e s)"),
                                            start=(t == 0), stop=(t == TT - 1))
                    ins.then_inc(gath_ps, 1)

            def scatter(q, b):
                pe.wait_ge(down_sb, 2 * (q + 1))
                for t in range(TT):
                    for h in range(2):
                        c = 2 * t + h
                        if not (isinstance(q, int) and 4 * q + c < 2):
                            pe.wait_ge(acc_done, 4 * q + c - 1)
                        pe.matmul(PS[:, SCAT[c % 2], :], turn[b][:, 2 * P + P * t:2 * P + P * (t + 1)],
                                  y_sel[:, HALF * h:HALF * (h + 1)], start=True, stop=True).then_inc(scat_ps, 1)

            def pair(l, i, b, first=False, last=False):
                q = PAIRS * l + i
                pe.wait_ge(gath_sb, 2 * (q + 1))
                pe.wait_ge(gu_ld[b], 32 * (PAIRS // 2 * l + 1) + 16 * (i - b))
                if not (isinstance(q, int) and q == 0):
                    pe.wait_ge(act_ready, q)
                for k in range(KD):
                    for e in range(2):
                        o = PS[64 * e:64 * e + 64, GU, :].rearrange("p (u f) -> p u f", u=2)
                        ins = pe.matmul(o, xselT[:, k, 64 * e:64 * e + 64], w_gu[b][:, :, e, k, :],
                                        start=(k == 0), stop=(k == KD - 1))
                ins.then_inc(gu_ps, 1)
                if not last:
                    gather(q + 1, 1 - b)
                pe.wait_ge(act_ready, q + 1)
                if not (isinstance(q, int) and q == 0):
                    pe.wait_ge(turn_sb, q)
                for k in range(KF):
                    pe.transpose(PS[:, TURN, P * k:P * (k + 1)], act_sb[:, P * k:P * (k + 1)], ident)
                for t in range(TT):
                    ins = pe.transpose(PS[:, TURN, 2 * P + P * t:2 * P + P * (t + 1)],
                                       sel_w[b][:, t].rearrange("p e s -> p (e s)"), ident)
                ins.then_inc(turn_ps, 1)
                if not first:
                    scatter(q - 1, 1 - b)
                pe.wait_ge(turn_sb, q + 1)
                pe.wait_ge(down_ld[b], 16 * (PAIRS // 2 * l + 1) + 8 * (i - b))
                pe.wait_ge(down_sb, 2 * q)
                for h in range(2):
                    for k in range(KF):
                        for e in range(2):
                            ins = pe.matmul(PS[64 * e:64 * e + 64, DOWN[h], :], turn[b][:, P * k + 64 * e:P * k + 64 * e + 64],
                                            w_down[b][:, e, k, HALF * h:HALF * (h + 1)], start=(k == 0), stop=(k == KF - 1))
                    ins.then_inc(down_ps, 1)

            def experts(l):
                gather(PAIRS * l, 0)
                pair(l, 0, 0, first=True)
                pair(l, 1, 1)
                with pe.Fori(1, PAIRS // 2 - 1) as j:
                    for b in range(2):
                        pair(l, 2 * j + b, b)
                pair(l, PAIRS - 2, 0)
                pair(l, PAIRS - 1, 1, last=True)
                scatter(PAIRS * (l + 1) - 1, 1)
                d = dense[l]
                pe.wait_ge(acc_done, 4 * PAIRS * (l + 1))
                flag = pe.value_load(over[0:1, 0:1])
                with pe.If(flag > 0):
                    with pe.Fori(0, EXPERTS) as e:
                        pe.wait_ge(d["ld"], 48 * e + 48)
                        for t in range(TT):
                            for k in range(KD):
                                ins = pe.matmul(PS[:, GU, :].rearrange("p (u f) -> p u f", u=2), hT[:, k, P * t:P * (t + 1)],
                                                w_gu[0][:, :, 0, k, :], start=(k == 0), stop=(k == KD - 1))
                            ins.then_inc(d["gu"], 1)
                            pe.wait_ge(d["act"], 2 * e + t + 1)
                            for k in range(KF):
                                ins = pe.transpose(PS[:, TURN, P * k:P * (k + 1)], act_sb[:, P * k:P * (k + 1)], ident)
                            ins.then_inc(d["turn"], 1)
                            pe.wait_ge(d["turned"], 2 * e + t + 1)
                            for h in range(2):
                                for k in range(KF):
                                    ins = pe.matmul(PS[:, DOWN[h], :], turn[0][:, P * k:P * (k + 1)],
                                                    w_down[0][:, 0, k, HALF * h:HALF * (h + 1)], start=(k == 0), stop=(k == KF - 1))
                            ins.then_inc(d["down"], 1)
                            pe.wait_ge(d["added"], 4 * e + 2 * t + 2)

            pe.wait_ge(in_ld, 16 * IN_LOADS)
            pe.transpose(PS[:, 7, 0:31], gain_rows, ident[0:31, 0:31])
            pe.wait_ge(pos_rows, 1)
            pe.transpose(PS[:, 7, 32:34], pos_r, ident[0:TT, 0:TT]).then_inc(columns_ps, 1)
            adaln(0)
            turn_x(0)
            h_ready(0)
            pe.wait_ge(lowrank_ld, 16)
            for t in range(TT):
                for k in range(KD):
                    ins = pe.matmul(PS[:, t, 0:LOWRANK], hT[:, k, P * t:P * (t + 1)], w_low[:, k, :],
                                    start=(k == 0), stop=(k == KD - 1))
                ins.then_inc(lowrank_ps, 1)
            pe.wait_ge(gate_ready, 1)
            for j in range(3):
                pe.wait_ge(convw_ld[j], 16)
                for c in range(CT):
                    o = PS[:, 2 + 2 * j + c // 2, 256 * (c % 2):256 * (c % 2) + 256]
                    for k in range(KD):
                        ins = pe.matmul(o, w_conv[j][:, k, P * c:P * (c + 1)], hT[:, k, :], start=(k == 0), stop=(k == KD - 1))
                    if c % 2:
                        ins.then_inc(conv_ps, 1)
            pe.wait_ge(lowrank_n, TT)
            for k in range(3):
                for t in range(TT):
                    at = 256 * (k % 2) + P * t
                    ins = pe.transpose(PS[:, k // 2, at:at + P], low[:, t, P * k:P * (k + 1)], ident)
            ins.then_inc(lowT_ps, 1)
            pe.wait_ge(lowT_ready, 1)
            pe.wait_ge(upw_ld, 32)
            pe.wait_ge(conv_x_sb, 2)
            for t in range(TT):
                for h in range(2):
                    for k in range(2):
                        ins = pe.matmul(PS[:, 2 * t + h, 0:4 * QK], lowT[:, k, P * t:P * (t + 1)], w_uq[:, k, 4 * QK * h:4 * QK * (h + 1)],
                                        start=(k == 0), stop=(k == 1))
                    ins.then_inc(up_ps, 1)
            pe.wait_ge(conv_done, 1)
            for t in range(TT):
                for h in range(2):
                    pe.matmul(PS[:, 4 + 2 * t + h, :], lowT[:, 2, P * t:P * (t + 1)], w_ukv[:, HALF * h:HALF * (h + 1)],
                              start=True, stop=True).then_inc(up_ps, 1)
            pe.wait_ge(up_q_sb, 4)
            pe.wait_ge(up_k_sb, 8)
            for u, src in enumerate((q_sb, k_sb)):
                pe.wait_ge(qk_ready, u + 1)
                for h in range(HEADS):
                    for t in range(TT):
                        at = 256 * (h % 2) + P * t
                        ins = pe.transpose(PS[0:QK, 4 * u + h // 2, at:at + P], src[:, t, h, :], ident)
                    if h % 2:
                        ins.then_inc(qkT_ps, 1)
            pe.wait_ge(qkT_ready, 8)

            def scores(h):
                b = h % 2
                if h >= 2:
                    pe.wait_ge(shift_ready, h - 1)
                pe.matmul(PS[:, b, 0:P], qT0[:, h, 0:P], kT0[:, h, 0:P], start=True, stop=True)
                pe.matmul(PS[:, b, P:3 * P], qT0[:, h, P:SEQ], kT0[:, h, :], start=True, stop=True).then_inc(score_ps, 1)

            scores(0)
            for h in range(HEADS):
                b = h % 2
                if h + 1 < HEADS:
                    scores(h + 1)
                pe.wait_ge(prob_ready, 2 * (h + 1))
                if h >= 2:
                    pe.wait_ge(probT_ready, h - 1)
                for j in range(3):
                    ins = pe.transpose(PS[:, 2 + b, P * j:P * (j + 1)], prob[:, b, P * j:P * (j + 1)], ident)
                ins.then_inc(probT_ps, 1)
                pe.wait_ge(probT_ready, h + 1)
                if h >= 2:
                    pe.wait_ge(head_sb, h - 1)
                pe.matmul(PS[:, 4 + b, 0:HV], probT[:, b, 0:P], v_sb[:, 0, h, :], start=True, stop=True)
                pe.matmul(PS[:, 4 + b, HV:2 * HV], probT[:, b, P:2 * P], v_sb[:, 0, h, :], start=True, stop=False)
                pe.matmul(PS[:, 4 + b, HV:2 * HV], probT[:, b, 2 * P:3 * P], v_sb[:, 1, h, :], start=False, stop=True)\
                  .then_inc(head_ps, 1)
            pe.wait_ge(head_sb, HEADS)
            for k in range(4):
                for t in range(TT):
                    at = 256 * (k % 2) + P * t
                    ins = pe.transpose(PS[:, 6 + k // 2, at:at + P], o_sb[:, t, P * k:P * (k + 1)], ident)
            ins.then_inc(oT_ps, 1)
            pe.wait_ge(oT_ready, 1)
            pe.wait_ge(out_ld[0], 16)
            for t in range(TT):
                for h in range(2):
                    for k in range(KD):
                        ins = pe.matmul(PS[:, 2 * t + h, :], yT0[:, k, P * t:P * (t + 1)], w_out0[:, k, HALF * h:HALF * (h + 1)],
                                        start=(k == 0), stop=(k == KD - 1))
                ins.then_inc(y_ps, 1)

            adaln(1)
            turn_x(1)
            router(0)
            experts(0)

            pe.wait_ge(x_ready, 4)
            adaln(2)
            turn_x(2)
            h_ready(2)
            for c in range(RET_CHUNKS):
                pe.wait_ge(ret_ld[c % 4], 16 * (c // 4 + 1))
                for t in range(TT):
                    n = 2 * c + t
                    if n >= 4:
                        pe.wait_ge(ret_sb, n - 3)
                    for k in range(KD):
                        ins = pe.matmul(PS[:, n % 4, :], hT[:, k, P * t:P * (t + 1)], w_ret[c % 4][:, k, :],
                                        start=(k == 0), stop=(k == KD - 1))
                    ins.then_inc(ret_ps, 1)
                if c in (4, 6):
                    u = c // 2 - 2
                    pe.wait_ge(rope_ready, 2 * (u + 1))
                    if u:
                        pe.wait_ge(retT_ready, 4)
                    else:
                        pe.wait_ge(gate_ready, 3)
                    for h in range(RH):
                        for t in range(TT):
                            at = 256 * (h % 2) + P * t
                            ins = pe.transpose(PS[:, 4 + h // 2, at:at + P], turned1[:, t, h, :], ident)
                        if h % 2:
                            ins.then_inc(retT_ps, 1)
            pe.wait_ge(retT_ready, 8)
            pe.wait_ge(ret_sb, 2 * RET_CHUNKS)

            def ret_scores(h):
                b = h % 2
                if h >= 2:
                    pe.wait_ge(decayed, h - 1)
                pe.matmul(PS[:, b, 0:SEQ], qkT1[1][:, h, 0:P], qkT1[0][:, h, :], start=True, stop=True)
                pe.matmul(PS[:, b, SEQ:SEQ + P], qkT1[1][:, h, P:SEQ], qkT1[0][:, h, P:SEQ], start=True, stop=True)\
                  .then_inc(rscore_ps, 1)

            ret_scores(0)
            for h in range(RH):
                b = h % 2
                if h + 1 < RH:
                    ret_scores(h + 1)
                pe.wait_ge(decayed, h + 1)
                if h >= 2:
                    pe.wait_ge(rhead_sb, 2 * (h - 1))
                vh = v1[:, :, DV * h:DV * (h + 1)]
                pe.matmul(PS[:, 4 + b, 0:DV], sT1[:, b, 0:P], vh[:, 0, :], start=True, stop=True)
                pe.matmul(PS[:, 4 + b, DV:2 * DV], sT1[:, b, P:2 * P], vh[:, 0, :], start=True, stop=False)
                pe.matmul(PS[:, 4 + b, DV:2 * DV], sT1[:, b, 2 * P:3 * P], vh[:, 1, :], start=False, stop=True)\
                  .then_inc(rhead_ps, 1)
            for n in range(RV // P // 2):
                if n == 0:
                    pe.wait_ge(ret_y, 1)
                if n >= 4:
                    pe.wait_ge(ryT_ready, 2 * (n - 3))
                for k in (2 * n, 2 * n + 1):
                    for t in range(TT):
                        at = 256 * (k % 2) + P * t
                        ins = pe.transpose(PS[:, 4 + n % 4, at:at + P], o1[:, t, P * k:P * (k + 1)], ident)
                ins.then_inc(ryT_ps, 1)
            pe.wait_ge(ryT_ready, RV // P)
            for j in range(4):
                pe.wait_ge(out_ld[j], 16 * (2 if j == 0 else 1))
            for t in range(TT):
                for h in range(2):
                    for k in range(RV // P):
                        ins = pe.matmul(PS[:, 2 * t + h, :], yT1[:, k, P * t:P * (t + 1)], w_out1[:, k, HALF * h:HALF * (h + 1)],
                                        start=(k == 0), stop=(k == RV // P - 1))
                ins.then_inc(y_ps, 1)

            adaln(3)
            turn_x(3)
            router(1)
            experts(1)

        @block.vector
        def _(dve):
            ch = Chain(dve, dve_chain)

            def ada_sum(s, k, n):
                dve.wait_ge(ada_ld[n % 2], 16 * (n // 2 + 1))
                if k == 0:
                    dve.tensor_scalar(sums[s], ada_buf[n % 2], c_silu[:, 0:1], None, ALU.mult).then_inc(ada_used, 1)
                else:
                    dve.wait_ge(ada_used, n)
                    dve.scalar_tensor_tensor(sums[s], ada_buf[n % 2], c_silu[:, k:k + 1], sums[s], ALU.mult, ALU.add)\
                       .then_inc(ada_used, 1)

            def adaln(s):
                dve.wait_ge(cols_ps, s + 1)
                ch.link(dve.tensor_tensor(mod_c[:, :, :].rearrange("p u k -> p (u k)"), PS[:, 4, 0:2 * KD],
                                          bias_c[:, s].rearrange("p u k -> p (u k)"), ALU.add))
                dve.tensor_scalar(mod_c[:, 1, :], mod_c[:, 1, :], 1.0, None, ALU.add).then_inc(cols_ready, 1)
                dve.wait_ge(gate_ps, s + 1)
                for h in range(2):
                    ins = dve.tensor_scalar(gate[:, HALF * h:HALF * (h + 1)], PS[:, 5 + h, :], 1.0, None, ALU.add)
                ins.then_inc(gate_ready, 1)

            def h_banks(s):
                dve.wait_ge(cols_ready, s + 1)
                for bank in (0, 2):
                    dve.wait_ge(xT_ps, 4 * s + bank + 1)
                    for k in (2 * bank, 2 * bank + 1):
                        ins = dve.tensor_scalar(hT[:, k, :], PS[:, bank, 256 * (k % 2):256 * (k % 2) + 256],
                                                mod_c[:, 1, k:k + 1], mod_c[:, 0, k:k + 1], ALU.mult, ALU.add)
                    ins.then_inc(hT_even, 1)

            def layer_norm(s, y):
                z = y_acc
                dve.wait_ge(gate_ready, s + 1)
                for t in range(TT):
                    for h in range(2):
                        cut = slice(HALF * h, HALF * (h + 1))
                        ch.step(dve.tensor_tensor(z[:, t, cut], y(t, h), gate[:, cut], ALU.mult))
                    ch.hold()
                    ch.link(dve.scalar_tensor_tensor(z[:, t, :], x[:, t, :], ALPHA, z[:, t, :], ALU.mult, ALU.add))
                    for h in range(2):
                        ch.step(dve.bn_stats(stats[:, t, h, :], z[:, t, HALF * h:HALF * (h + 1)]))
                    ch.hold()
                    ch.link(dve.bn_aggr(mv[:, t, :], stats[:, t, :, :].rearrange("p h c -> p (h c)")))
                    dve.tensor_scalar(mv[:, t, 1:2], mv[:, t, 1:2], LN_EPS, None, ALU.add).then_inc(var_ready, 1)
                dve.wait_ge(ln_ld, 32 * (s + 1))
                for t in range(TT):
                    dve.wait_ge(std_ready, 2 * s + t + 1)
                    ch.link(dve.reciprocal(rstd[:, t:t + 1], std[:, t:t + 1]))
                    ch.link(dve.tensor_scalar(z[:, t, :], z[:, t, :], mv[:, t, 0:1], rstd[:, t:t + 1], ALU.subtract, ALU.mult))
                    ch.link(dve.tensor_tensor(z[:, t, :], z[:, t, :], ln_g[:, :], ALU.mult))
                    dve.tensor_tensor(x[:, t, :], z[:, t, :], ln_b[:, :], ALU.add).then_inc(x_ready, 1)

            def rope(src, dst, lo, half, cos, sin, tmp, view):
                a1, a2 = src[..., lo:lo + half], src[..., lo + half:lo + 2 * half]
                t = [view(x) for x in tmp]
                ch.hold()
                ch.step(dve.tensor_tensor(t[0], a1, cos, ALU.mult))
                ch.step(dve.tensor_tensor(t[1], a2, sin, ALU.mult))
                ch.step(dve.tensor_tensor(t[2], a2, cos, ALU.mult))
                ch.step(dve.tensor_tensor(t[3], a1, sin, ALU.mult))
                ch.hold()
                ch.step(dve.tensor_tensor(dst[..., lo:lo + half], t[0], t[1], ALU.subtract))
                return dve.tensor_tensor(dst[..., lo + half:lo + 2 * half], t[2], t[3], ALU.add)

            def router(l):
                dve.wait_ge(logit_ps, l + 1)
                lg = PS[:, 4, 0:128].rearrange("p (t c) -> p t c", t=TT)
                ch.link(dve.memset(g_pad, -3e38))
                ch.link(dve.tensor_copy(g_pad[:, :, 0:GROUPS], lg[:, :, 0:GROUPS]))
                for t in range(TT):
                    ch.step(dve.max(mx[:, t, :], g_pad[:, t, :]))
                ch.hold()
                for t in range(TT):
                    ch.step(dve.max_index(mi[:, t, :], mx[:, t, :], g_pad[:, t, :]))
                dve.tensor_tensor(d4, g_pad[:, :, 0:GROUPS], mx[:, :, 0:1].broadcast_to((P, TT, GROUPS)), ALU.subtract)\
                   .then_inc(gdiff_ready, 1)
                ch.hold()
                ch.link(dve.tensor_copy(g_i, mi[:, :, 0:1]))
                slots4 = cst[:, C_EXP:C_EXP + GROUPS].unsqueeze(1).broadcast_to((P, TT, GROUPS))
                ch.link(dve.tensor_tensor(oh4, slots4, g_i.broadcast_to((P, TT, GROUPS)), ALU.is_equal))
                for t in range(TT):
                    ch.step(dve.tensor_tensor(e_prod[:, t], lg[:, t, GROUPS:GROUPS + EXPERTS].rearrange("p (g j) -> p j g", g=GROUPS),
                                              oh4[:, t].unsqueeze(1).broadcast_to((P, PER_GROUP, GROUPS)), ALU.mult))
                ch.hold()
                ch.link(dve.tensor_reduce(e_sel, e_prod, AX.X, ALU.add))
                for t in range(TT):
                    ch.step(dve.max(mx[:, t, :], e_sel[:, t, :]))
                ch.hold()
                for t in range(TT):
                    ch.step(dve.max_index(mi[:, t, :], mx[:, t, :], e_sel[:, t, :]))
                dve.tensor_tensor(e_d, mx[:, :, 1:2], mx[:, :, 0:1], ALU.subtract).then_inc(ediff_ready, 1)
                ch.step(dve.tensor_scalar(g_8, g_i, float(PER_GROUP), None, ALU.mult))
                ch.hold()
                ch.link(dve.tensor_copy(e_id, mi[:, :, 0:2]))
                ch.link(dve.tensor_tensor(e_id, e_id, g_8.broadcast_to((P, TT, 2)), ALU.add))
                numbers = cst[:, C_EXP:C_EXP + EXPERTS].unsqueeze(1).broadcast_to((P, TT, EXPERTS))
                ch.step(dve.tensor_tensor(cw, numbers, e_id[:, :, 0:1].broadcast_to((P, TT, EXPERTS)), ALU.is_equal))
                ch.link(dve.tensor_tensor(eq2, numbers, e_id[:, :, 1:2].broadcast_to((P, TT, EXPERTS)), ALU.is_equal))
                dve.tensor_tensor(mask, cw, eq2, ALU.add).then_inc(mask_ready, 1)
                dve.wait_ge(gexp_ready, l + 1)
                ch.link(dve.tensor_reduce(g_sum, d4, AX.X, ALU.add))
                ch.link(dve.reciprocal(g_p, g_sum.rearrange("p (t e) -> p t e", t=TT)))
                dve.wait_ge(eexp_ready, l + 1)
                ch.link(dve.tensor_scalar(den, e_x, 1.0, None, ALU.add))
                ch.link(dve.reciprocal(den, den))
                ch.link(dve.tensor_tensor(w_1, g_p, den, ALU.mult))
                ch.link(dve.tensor_tensor(w_2, w_1, e_x, ALU.mult))
                ch.step(dve.tensor_tensor(cw, cw, w_1.broadcast_to((P, TT, EXPERTS)), ALU.mult))
                ch.link(dve.tensor_tensor(eq2, eq2, w_2.broadcast_to((P, TT, EXPERTS)), ALU.mult))
                ch.link(dve.tensor_tensor(cw, cw, eq2, ALU.add))
                dve.wait_ge(rank_ps, l + 1)
                flat = lambda v: v.rearrange("p t e -> p (t e)")
                ch.step(dve.tensor_reduce(over_f[:, :], PS[:, 5, 64:96], AX.X, ALU.max))
                ch.link(dve.scalar_tensor_tensor(flat(rank), PS[:, 5, 0:64], 1.0, flat(mask), ALU.add, ALU.mult))
                ch.link(dve.tensor_scalar(flat(rank), flat(rank), -1.0, None, ALU.add))
                ch.link(dve.scalar_tensor_tensor(flat(cw_over), flat(rank), float(SLOTS), flat(cw), ALU.is_ge, ALU.mult))
                dve.tensor_scalar(over[:, :], over_f[0:1, :], float(SLOTS), None, ALU.is_gt).then_inc(route_ready, 1)
                dve.wait_ge(route_ready, l + 1)

            slot_no = cst[:, C_SLOT:C_SLOT + SLOTS].unsqueeze(1).broadcast_to((P, 2, SLOTS))

            def select(i, b):
                for t in range(TT):
                    rk = rank[:, t, bass.ds(2 * i, 2)].unsqueeze(2).broadcast_to((P, 2, SLOTS))
                    ch.step(dve.tensor_tensor(sel[b][:, t], slot_no, rk, ALU.is_equal))
                ch.hold()
                for t in range(TT):
                    wt = cw[:, t, bass.ds(2 * i, 2)].unsqueeze(2).broadcast_to((P, 2, SLOTS))
                    ins = dve.tensor_tensor(sel_w[b][:, t], sel[b][:, t], wt, ALU.mult)
                ins.then_inc(sel_ready, 1)

            def accumulate(l, q, first):
                for c in range(4):
                    t, h = c // 2, c % 2
                    dve.wait_ge(scat_ps, 4 * q + c + 1)
                    cut = y_acc[:, t, HALF * h:HALF * (h + 1)]
                    if first:
                        dve.tensor_copy(cut, PS[:, SCAT[c % 2], :]).then_inc(acc_done, 1)
                    else:
                        dve.tensor_tensor(cut, cut, PS[:, SCAT[c % 2], :], ALU.add).then_inc(acc_done, 1)

            def pair(l, i, b, first=False, second=False, tail=False):
                q = PAIRS * l + i
                dve.wait_ge(silu_ready, q + 1)
                dve.tensor_tensor(act_sb.rearrange("p (k f) -> p f k", k=KF), silu_sb.rearrange("p (f k) -> p f k", k=KF),
                                  PS[:, GU, FE:2 * FE].rearrange("p (f k) -> p f k", k=KF), ALU.mult).then_inc(act_ready, 1)
                dve.wait_ge(turn_ps, q + 1)
                dve.tensor_copy(turn[b], PS[:, TURN, :]).then_inc(turn_sb, 1)
                if not first:
                    accumulate(l, q - 1, second)
                if not tail:
                    select(i + 2, b)

            def experts(l):
                select(0, 0)
                select(1, 1)
                pair(l, 0, 0, first=True)
                pair(l, 1, 1, second=True)
                if l == 0:
                    ada_sum(2, 0, 16)
                    ada_sum(3, 0, 17)
                with dve.Fori(1, PAIRS // 2 - 1) as j:
                    ch.enter(j - 1, 4)
                    for b in range(2):
                        pair(l, 2 * j + b, b)
                    if l == 0:
                        for u, s in enumerate((2, 3)):
                            dve.wait_ge(ada_ld[u], 16 * (KD + 1 + j))
                            dve.wait_ge(ada_used, 2 * KD + 2 * j + u)
                            dve.scalar_tensor_tensor(sums[s], ada_buf[u], c_silu[:, bass.ds(j, 1)], sums[s], ALU.mult, ALU.add)\
                               .then_inc(ada_used, 1)
                    ch.again()
                ch.leave(PAIRS // 2 - 2)
                pair(l, PAIRS - 2, 0, tail=True)
                pair(l, PAIRS - 1, 1, tail=True)
                if l == 0:
                    ada_sum(2, KD - 1, 30)
                    ada_sum(3, KD - 1, 31)
                accumulate(l, PAIRS * (l + 1) - 1, False)
                dve.wait_ge(acc_done, 4 * PAIRS * (l + 1))
                d = dense[l]
                flag = dve.value_load(over[0:1, 0:1])
                with dve.If(flag > 0):
                    with dve.Fori(0, EXPERTS) as e:
                        for t in range(TT):
                            n = 2 * e + t
                            dve.wait_ge(d["silu"], n + 1)
                            dve.scalar_tensor_tensor(act_sb.rearrange("p (k f) -> p f k", k=KF),
                                                     silu_sb.rearrange("p (f k) -> p f k", k=KF), cw_over[:, t, bass.ds(e, 1)],
                                                     PS[:, GU, FE:2 * FE].rearrange("p (f k) -> p f k", k=KF),
                                                     ALU.mult, ALU.mult).then_inc(d["act"], 1)
                            dve.wait_ge(d["turn"], n + 1)
                            dve.tensor_copy(turn[0][:, 0:2 * P], PS[:, TURN, 0:2 * P]).then_inc(d["turned"], 1)
                            dve.wait_ge(d["down"], n + 1)
                            for h in range(2):
                                cut = y_acc[:, t, HALF * h:HALF * (h + 1)]
                                dve.tensor_tensor(cut, cut, PS[:, DOWN[h], :], ALU.add).then_inc(d["added"], 1)
                    dve.wait_ge(d["added"], 4 * EXPERTS)

            dve.wait_ge(in_ld, 16 * IN_LOADS)
            dve.tensor_copy(pos_r, pos_i).then_inc(pos_rows, 1)
            dve.wait_ge(columns_ps, 1)
            ch.step(dve.tensor_copy(gains[:, :], PS[:, 7, 0:31]))
            ch.link(dve.tensor_copy(pos_f[:, :], PS[:, 7, 32:34]))
            tables = 0
            for trig, at, half, tmp in ((trig_m, C_INVM, ROPE // 2, M[:, 0:32]), (trig_r, C_INVR, DK // 2, M[:, 0:128])):
                n = tmp.shape[1]
                flat = [trig[:, u].rearrange("p t c -> p (t c)") for u in range(2)]
                ang, turns = M[:, 128:128 + n], M[:, 256:256 + n]
                for t in range(TT):
                    ch.step(dve.tensor_scalar(ang[:, half * t:half * (t + 1)], cst[:, at:at + half], pos_f[:, t:t + 1], None, ALU.mult))
                ch.hold()
                for u, quarter in ((0, 0.25), (1, 0.0)):
                    ch.link(dve.tensor_scalar(turns, ang, float(1 / TWO_PI), quarter, ALU.mult, ALU.add))
                    ch.link(dve.tensor_scalar(turns, turns, ROUND, None, ALU.add))
                    ch.link(dve.tensor_scalar(turns, turns, -ROUND, None, ALU.add))
                    ch.link(dve.scalar_tensor_tensor(tmp, turns, -PI_A, ang, ALU.mult, ALU.add))
                    ch.link(dve.scalar_tensor_tensor(tmp, turns, -PI_B, tmp, ALU.mult, ALU.add))
                    ch.link(dve.scalar_tensor_tensor(tmp, turns, -PI_C, tmp, ALU.mult, ALU.add))
                    ch.link(dve.tensor_scalar(tmp, tmp, float(quarter * TWO_PI), SIN_MAX, ALU.add, ALU.min))
                    dve.tensor_scalar(flat[u], tmp, -SIN_MAX, None, ALU.max).then_inc(angle_ready, 1)
                    tables += 1
                    dve.wait_ge(angle_ready, tables)
            dve.wait_ge(c_silu_ready, 1)
            for k in range(KD):
                ada_sum(0, k, k)

            adaln(0)
            h_banks(0)
            for t in range(TT):
                dve.wait_ge(lowrank_ps, t + 1)
                dve.tensor_copy(low[:, t, :], PS[:, t, 0:LOWRANK]).then_inc(lowrank_sb, 1)
            ch.step(dve.memset(conv_u[:, :, 0:2], 0.0))
            dve.wait_ge(square_ready, TT)
            dve.wait_ge(act_chain, TT)
            sq = soft[:, 0:4].rearrange("p (t c) -> p t c", t=TT)
            ms = soft[:, 4:8].rearrange("p (t c) -> p t c", t=TT)
            dve.tensor_scalar(ms[:, :, 0:1], sq[:, :, 0:1], 1.0 / QR, RMS_EPS, ALU.mult, ALU.add).then_inc(ms_ready, 1)
            dve.tensor_scalar(ms[:, :, 1:2], sq[:, :, 1:2], 1.0 / KVR, RMS_EPS, ALU.mult, ALU.add).then_inc(ms_ready, 1)
            dve.wait_ge(rms_ready, 1)
            ch.link(dve.reciprocal(soft[:, 12:16], soft[:, 8:12]))
            for t in range(TT):
                ch.step(dve.tensor_scalar(low[:, t, 0:QR], low[:, t, 0:QR], soft[:, 12 + 2 * t:13 + 2 * t], None, ALU.mult))
                dve.tensor_scalar(low[:, t, QR:QR + KVR], low[:, t, QR:QR + KVR], soft[:, 13 + 2 * t:14 + 2 * t], None,
                                  ALU.mult).then_inc(lowrank_n, 1)
            dve.wait_ge(conv_x_sb, 2)
            for c in range(CT):
                dve.wait_ge(conv_ps, 3 + c // 2)
                ch.step(dve.tensor_tensor(conv_u[:, c, 2:], conv_x[:, c, :], PS[:, 4 + c // 2, 256 * (c % 2):256 * (c % 2) + 256], ALU.mult))
            ch.hold()
            for c in range(CT):
                ch.step(dve.tensor_scalar(yT0[:, c, :], conv_u[:, c, 0:SEQ], conv_w[:, 0, c:c + 1], None, ALU.mult))
            for j in (1, 2):
                ch.hold()
                for c in range(CT):
                    ch.step(dve.scalar_tensor_tensor(yT0[:, c, :], conv_u[:, c, j:SEQ + j], conv_w[:, j, c:c + 1], yT0[:, c, :],
                                                     ALU.mult, ALU.add))
            ch.hold()
            for c in range(CT):
                dve.wait_ge(conv_ps, 5 + c // 2)
                ins = dve.tensor_tensor(yT0[:, c, :], yT0[:, c, :], PS[:, 6 + c // 2, 256 * (c % 2):256 * (c % 2) + 256], ALU.mult)
            ins.then_inc(conv_done, 1)
            dve.wait_ge(lowT_ps, 1)
            for k in range(3):
                ins = dve.tensor_scalar(lowT[:, k, :], PS[:, k // 2, 256 * (k % 2):256 * (k % 2) + 256],
                                        q_g[:, k:k + 1] if k < 2 else kv_g[:, 0:1], None, ALU.mult)
            ins.then_inc(lowT_ready, 1)
            dve.wait_ge(trig_ready, 1)
            dve.wait_ge(up_q_sb, 4)
            for t in range(TT):
                bc = lambda v: v.unsqueeze(1).broadcast_to((P, HEADS, ROPE // 2))
                view = lambda v: v[:, 128 * t:128 * t + 128].rearrange("p (h c) -> p h c", h=HEADS)
                ins = rope(q_sb[:, t], q_sb[:, t], NOPE, ROPE // 2, bc(trig_m[:, 0, t]), bc(trig_m[:, 1, t]), rope_t, view)
                if t < TT - 1:
                    ch.step(ins)
            ins.then_inc(qk_ready, 1)
            dve.wait_ge(qk_ready, 1)
            ins = rope(low[:, :, QR + KVR:], low[:, :, QR + KVR:], 0, ROPE // 2, trig_m[:, 0], trig_m[:, 1], rope_t,
                       lambda v: v[:, 0:32].rearrange("p (t c) -> p t c", t=TT))
            ch.link(ins)
            dve.wait_ge(up_k_sb, 8)
            for t in range(TT):
                ins = dve.tensor_copy(k_sb[:, t, :, NOPE:], low[:, t, QR + KVR:].unsqueeze(1).broadcast_to((P, HEADS, ROPE)))
            ins.then_inc(qk_ready, 1)
            for n in range(8):
                dve.wait_ge(qkT_ps, n + 1)
                dst = (qT0, kT0)[n // 4][:, 2 * (n % 4):2 * (n % 4) + 2, :].rearrange("p h t -> p (h t)")
                dve.tensor_copy(dst, PS[0:QK, n, :]).then_inc(qkT_ready, 1)

            def softmax_shift(h):
                b = h % 2
                dve.wait_ge(score_ps, h + 1)
                if h >= 2:
                    dve.wait_ge(prob_ready, 2 * (h - 1))
                ch.link(dve.tensor_tensor(score[:, b, :], PS[:, b, 0:3 * P], cst[:, C_MASK:C_MASK + 3 * P], ALU.add))
                at = 64 + 2 * h
                ch.step(dve.tensor_reduce(soft[:, at:at + 1], score[:, b, 0:P], AX.X, ALU.max))
                ch.link(dve.tensor_reduce(soft[:, at + 1:at + 2], score[:, b, P:3 * P], AX.X, ALU.max))
                dve.tensor_scalar(soft[:, 16 + 2 * h:18 + 2 * h], soft[:, at:at + 2], -MLA_SCALE, None, ALU.mult).then_inc(shift_ready, 1)

            softmax_shift(0)
            for h in range(HEADS):
                b = h % 2
                if h + 1 < HEADS:
                    softmax_shift(h + 1)
                dve.wait_ge(probT_ps, h + 1)
                dve.tensor_copy(probT[:, b, :], PS[:, 2 + b, 0:3 * P]).then_inc(probT_ready, 1)
                ch.link(dve.reciprocal(soft[:, 96 + 2 * h:98 + 2 * h], soft[:, 32 + 2 * h:34 + 2 * h]))
                dve.wait_ge(head_ps, h + 1)
                for t in range(TT):
                    ins = dve.tensor_scalar(o_sb[:, t, HV * h:HV * (h + 1)], PS[:, 4 + b, HV * t:HV * (t + 1)],
                                            soft[:, 96 + 2 * h + t:97 + 2 * h + t], None, ALU.mult)
                ins.then_inc(head_sb, 1)
                ada_sum(1, h, KD + h)
            dve.wait_ge(oT_ps, 1)
            for k in range(4):
                ins = dve.tensor_copy(yT0[:, 4 + k, :], PS[:, 6 + k // 2, 256 * (k % 2):256 * (k % 2) + 256])
            ins.then_inc(oT_ready, 1)
            dve.wait_ge(y_ps, 2)
            layer_norm(0, lambda t, h: PS[:, 2 * t + h, :])

            adaln(1)
            h_banks(1)
            router(0)
            experts(0)
            layer_norm(1, lambda t, h: y_acc[:, t, HALF * h:HALF * (h + 1)])

            adaln(2)
            h_banks(2)

            def ret_rope(u):
                for t in range(TT):
                    dve.wait_ge(ret_sb, 4 * u + 2 + t + 1)
                    if u:
                        dve.wait_ge(retT_ps, 4)
                    cos, sin = (trig_r[:, v, t].unsqueeze(1).broadcast_to((P, RH, DK // 2)) for v in range(2))
                    if u or t:
                        dve.wait_ge(rope_ready, 2 * u + t)
                    ins = rope(raw1[:, t], turned1[:, t], 0, DK // 2, cos, sin, rope_r, lambda v: v)
                    ins.then_inc(rope_ready, 1)

            def ret_turned(u):
                for n in range(4):
                    dve.wait_ge(retT_ps, 4 * u + n + 1)
                    dve.tensor_copy(qkT1[u][:, 2 * n:2 * n + 2, :].rearrange("p h t -> p (h t)"), PS[:, 4 + n, :])\
                       .then_inc(retT_ready, 1)

            ret_rope(0)
            ret_turned(0)
            ret_rope(1)
            ret_turned(1)
            dve.wait_ge(decay_ld, 16)
            for h in range(RH):
                b = h % 2
                dve.wait_ge(rscore_ps, h + 1)
                if h >= 2:
                    dve.wait_ge(rhead_ps, h - 1)
                dve.tensor_tensor(sT1[:, b, 0:SEQ], PS[:, b, 0:SEQ], decay[:, h, :], ALU.mult)
                dve.tensor_tensor(sT1[:, b, SEQ:SEQ + P], PS[:, b, SEQ:SEQ + P], decay[:, h, 0:P], ALU.mult).then_inc(decayed, 1)
                if h:
                    ret_stats = h - 1
                    dve.wait_ge(rhead_sb, 2 * (ret_stats + 1))
                    for t in range(TT):
                        ch.step(dve.bn_stats(rstat[:, t, ret_stats, :], o1[:, t, DV * ret_stats:DV * (ret_stats + 1)]))
            dve.wait_ge(rhead_sb, 2 * RH)
            for t in range(TT):
                ch.step(dve.bn_stats(rstat[:, t, RH - 1, :], o1[:, t, DV * (RH - 1):]))
            ch.hold()
            for t in range(TT):
                for h in range(RH):
                    ch.step(dve.bn_aggr(rmv[:, t, h, :], rstat[:, t, h, :]))
            ch.hold()
            dve.tensor_scalar(rsd, rmv[:, :, :, 1], LN_EPS, None, ALU.add).then_inc(rvar_ready, 1)
            dve.wait_ge(rstd_ready, 1)
            ch.link(dve.reciprocal(rrs, rsd))
            dve.wait_ge(ret_sb, 2 * RET_CHUNKS)
            for t in range(TT):
                for h in range(RH):
                    o = o1[:, t, DV * h:DV * (h + 1)]
                    ch.step(dve.tensor_scalar(o, o, rmv[:, t, h, 0:1], rrs[:, t, h:h + 1], ALU.subtract, ALU.mult))
            ch.hold()
            for t in range(TT):
                ins = dve.tensor_tensor(o1[:, t, :], o1[:, t, :], g1[:, t, :], ALU.mult)
            ins.then_inc(ret_y, 1)
            for n in range(RV // P // 2):
                dve.wait_ge(ryT_ps, n + 1)
                for k in (2 * n, 2 * n + 1):
                    dve.tensor_scalar(yT1[:, k, :], PS[:, 4 + n % 4, 256 * (k % 2):256 * (k % 2) + 256], gn_g[:, k:k + 1], None,
                                      ALU.mult).then_inc(ryT_ready, 1)
            dve.wait_ge(y_ps, 4)
            layer_norm(2, lambda t, h: PS[:, 2 * t + h, :])

            adaln(3)
            h_banks(3)
            router(1)
            experts(1)
            layer_norm(3, lambda t, h: y_acc[:, t, HALF * h:HALF * (h + 1)])


_INS = ['x', 'c', 'positions', 'ada_mix_w', 'ada_mix_b', 'ln_mix_g', 'ln_mix_b',
        'ab_w_in', 'ab_conv_w', 'ab_q_norm_g', 'ab_kv_norm_g', 'ab_w_uq', 'ab_w_ukv', 'ab_w_out',
        'ret_w_in', 'ret_gn_g', 'ret_w_out', 'ada_ffn_w', 'ada_ffn_b', 'ln_ffn_g', 'ln_ffn_b',
        'moe_rg_w', 'moe_rg_b', 'moe_re_w', 'moe_re_b', 'moe_w_gate', 'moe_w_up', 'moe_w_down']


def kernel(**inputs):
    import concourse.bacc as bacc
    from concourse.bass_utils import run_bass_kernel_spmd

    nc = bacc.Bacc("TRN2", target_bir_lowering=False, num_devices=1)
    arrays = {name: np.ascontiguousarray(inputs[name]) for name in _INS}
    arrays["table"], arrays["decay"] = shape_constants()
    aps = {name: nc.dram_tensor(f"in_{name}", v.shape, mybir.dt.from_np(v.dtype), kind="ExternalInput").ap()
           for name, v in arrays.items()}
    out = nc.dram_tensor("out_0", (1, SEQ, D), F32, kind="ExternalOutput").ap()
    build(nc, aps, out)
    got = run_bass_kernel_spmd(nc, [{f"in_{name}": v for name, v in arrays.items()}], core_ids=[0])
    return got.results[0]["out_0"]
```

```python
from contextlib import ExitStack

import numpy as np

import concourse.bass as bass
from concourse import mybir

ALU = mybir.AluOpType
ACT = mybir.ActivationFunctionType
AX = mybir.AxisListType
F32 = mybir.dt.float32
I32 = mybir.dt.int32
U32 = mybir.dt.uint32
F32R = mybir.dt.float32r
BF16 = mybir.dt.bfloat16

P = 128
D = 1024
SEQ = 256
TT = SEQ // P
KD = D // P
DEPTH = 2
SUBLAYERS = 2 * DEPTH
ALPHA = float(2 * DEPTH) ** 0.25
LN_EPS, RMS_EPS = 1e-5, 1e-6
HALF = 512

CONV = 512
CT = CONV // P
QR, KVR, ROPE, NOPE, HV, HEADS = 256, 128, 32, 64, 64, 8
LOWRANK = QR + KVR + ROPE
QK = NOPE + ROPE
MLA_SCALE = float(QK) ** -0.5

RH, DK, DV = 8, 128, 256
RQ = RH * DK
RV = RH * DV
RET_CHUNKS = (2 * RQ + 2 * RV) // HALF
RET_PARTS = 2 * RET_CHUNKS
OUT_PARTS = RV // P // 2

THIRDS = 3 * SUBLAYERS
BLOCKS = KD * THIRDS
LATE = KD * 9
RING = 4
LATE_AT = {0: 3, 2: 3, 4: 4, 5: 2, 6: 4, 8: 2, 9: 3, 10: 3}

GROUPS, PER_GROUP = 4, 8
EXPERTS = GROUPS * PER_GROUP
FE = 256
KF = FE // P
SLOTS = 64
PAIRS = EXPERTS // 2

C_ID, C_ONE, C_UP, C_MASK = 0, 128, 256, 384
C_SLOT = 768
C_EXP = C_SLOT + SLOTS
C_INVM = C_EXP + EXPERTS
C_INVR = C_INVM + ROPE // 2
C_N = C_INVR + DK // 2

TWO_PI = 2 * np.pi
PI_A = float(np.float32(6.28125))
PI_B = float(np.float32(np.float64(TWO_PI) - 6.28125))
PI_C = float(np.float32(TWO_PI - 6.28125 - np.float64(np.float32(TWO_PI - 6.28125))))
ROUND = float(1.5 * 2 ** 23)
SIN_MAX = 3.1415925


def shape_constants():
    t = np.zeros((P, C_N), np.float32)
    t[:, C_ID:C_ID + P] = np.eye(P)
    t[:, C_ONE:C_ONE + P] = 1.0
    t[:, C_UP:C_UP + P] = np.triu(np.ones((P, P)), 1)
    causal = np.where(np.arange(P)[None, :] <= np.arange(P)[:, None], 0.0, -1e30)
    t[:, C_MASK:C_MASK + P] = causal
    t[:, C_MASK + 2 * P:C_MASK + 3 * P] = causal
    t[:, C_SLOT:C_SLOT + SLOTS] = np.arange(SLOTS)
    t[:, C_EXP:C_EXP + EXPERTS] = np.arange(EXPERTS)
    for at, dim in ((C_INVM, ROPE), (C_INVR, DK)):
        inv = np.float32(10000.0) ** (-np.arange(0, dim, 2, dtype=np.float32) / np.float32(dim))
        t[:, at:at + dim // 2] = inv
    lg = np.log1p(-np.exp2(-5.0 - np.arange(RH)))
    lag = np.arange(SEQ)[None, :] - np.arange(P)[:, None]
    decay = np.where(lag[:, None, :] >= 0, np.exp(lg[None, :, None] * np.maximum(lag, 0)[:, None, :]), 0.0)
    decay = decay * DK ** -0.5
    return t, np.ascontiguousarray(decay.astype(np.float32).reshape(P, RH * SEQ))


class Chain:

    def __init__(self, eng, sem):
        self.eng, self.sem, self.n, self.moving = eng, sem, 0, None

    def value(self):
        return self.n if self.moving is None else self.moving + self.n

    def step(self, ins):
        self.n += 1
        ins.then_inc(self.sem, 1)

    def hold(self):
        self.eng.wait_ge(self.sem, self.value())

    def link(self, ins):
        self.step(ins)
        self.hold()

    def enter(self, i, per):
        self.before, self.per = self.n, per
        self.moving, self.n = self.before + per * i, 0

    def again(self):
        assert self.n == self.per, (self.n, self.per)

    def leave(self, times):
        self.moving, self.n = None, self.before + self.per * times


def build(nc, a, out):
    ctx = ExitStack()
    with ctx:
        def sb(name, shape, dt=F32):
            return ctx.enter_context(nc.sbuf_tensor(name, shape, dt))

        def sem(name):
            return ctx.enter_context(nc.semaphore(name))

        W = sb("W", [P, 24576])
        w_end = nc.sbuf_base
        M = sb("M", [P, 16384])
        m_end = nc.sbuf_base

        def rounded(name, arena, at, width):
            end, words = (w_end, 24576) if arena == "W" else (m_end, 16384)
            return nc.alloc_sbuf_tensor_at(name, [P, width], F32R, offset=end - 4 * (words - at))

        x = sb("x", [P, TT, D])
        hT = sb("hT", [P, KD, SEQ])
        gates = sb("gates", [P, SUBLAYERS, D])
        ln_g = sb("ln_g", [P, D])
        ln_b = sb("ln_b", [P, D])
        cst = sb("cst", [P, C_N])
        router_w = sb("router_w", [P, KD, GROUPS + EXPERTS])
        router_b = sb("router_b", [1, GROUPS + EXPERTS])
        gains = sb("gains", [P, 31])
        gn_g, q_g, kv_g = gains[:, 0:16], gains[:, 16:18], gains[:, 18:19]
        conv_w = gains[:, 19:31].rearrange("p (j c) -> p j c", j=3)
        gain_rows = M[0:31, 0:P]
        pos_i = M[0:TT, P:2 * P].bitcast(I32)
        pos_r = M[0:TT, 2 * P:3 * P]
        bias_c = sb("bias_c", [P, SUBLAYERS, 2, KD])
        mod_c = sb("mod_c", [P, SUBLAYERS, 2, KD])
        c_in = sb("c_in", [P, KD])
        c_silu = sb("c_silu", [P, KD])
        pos_f = sb("pos_f", [P, TT])
        trig_m = sb("trig_m", [P, 2, TT, ROPE // 2])
        trig_r = sb("trig_r", [P, 2, TT, DK // 2])
        stats = sb("stats", [P, TT, 2, 6])
        mv = sb("mv", [P, TT, 2])
        std = sb("std", [P, TT])
        rstd = sb("rstd", [P, TT])
        over = sb("over", [1, 1], I32)
        over_f = sb("over_f", [P, 1])
        PS = ctx.enter_context(nc.psum_tensor("PS", [P, 8, HALF], F32))

        ident = cst[:, C_ID:C_ID + P]
        ones = cst[:, C_ONE:C_ONE + P]
        upper = cst[:, C_UP:C_UP + P]
        hflat = hT[:, :, :].rearrange("p k t -> p (k t)")

        def ada_buf(n):
            at = 10240 + D * (n % RING) if n < LATE else 22528 + D * (n % 2)
            return (M if n < LATE else W)[:, at:at + D]

        def ada_acc(m):
            return M[:, 14336 + D * (m % 2):14336 + D * (m % 2 + 1)] if m < 9 else hflat[:, D * (m % 2):D * (m % 2 + 1)]

        y_acc = M[:, 0:2048].rearrange("p (t d) -> p t d", t=TT)

        in_ld = sem("in_ld")
        pos_rows = sem("pos_rows")
        columns_ps = sem("columns_ps")
        ada_ld = [sem(f"ada_ld{j}") for j in range(RING)]
        late_ld = [sem(f"late_ld{j}") for j in range(2)]
        c_silu_ready = sem("c_silu_ready")
        ada_used = sem("ada_used")
        ln_ld = sem("ln_ld")
        third_ps = sem("third_ps")
        third_ready = sem("third_ready")
        xT_ps = sem("xT_ps")
        hT_even = sem("hT_even")
        hT_odd = sem("hT_odd")
        var_ready = sem("var_ready")
        std_ready = sem("std_ready")
        x_ready = sem("x_ready")
        y_ps = sem("y_ps")
        dve_chain = sem("dve_chain")
        act_chain = sem("act_chain")
        angle_ready = sem("angle_ready")
        trig_ready = sem("trig_ready")
        lowrank_ld = sem("lowrank_ld")
        convw_ld = [sem(f"conv_ld{j}") for j in range(3)]
        upw_ld = sem("upw_ld")
        out_ld = [sem(f"out_ld{j}") for j in range(3)]
        lowrank_ps = sem("lowrank_ps")
        lowrank_sb = sem("lowrank_sb")
        square_ready = sem("square_ready")
        ms_ready = sem("ms_ready")
        rms_ready = sem("rms_ready")
        lowrank_n = sem("lowrank_n")
        lowT_ps = sem("lowT_ps")
        lowT_ready = sem("lowT_ready")
        conv_ps = sem("conv_ps")
        conv_x_sb = sem("conv_x_sb")
        conv_done = sem("conv_done")
        up_ps = sem("up_ps")
        up_q_sb = sem("up_q_sb")
        up_k_sb = sem("up_k_sb")
        qk_ready = sem("qk_ready")
        qkT_ps = sem("qkT_ps")
        qkT_ready = sem("qkT_ready")
        score_ps = sem("score_ps")
        shift_ready = sem("shift_ready")
        prob_ready = sem("prob_ready")
        probT_ps = sem("probT_ps")
        probT_ready = sem("probT_ready")
        head_ps = sem("head_ps")
        head_sb = sem("head_sb")
        oT_ps = sem("oT_ps")
        oT_ready = sem("oT_ready")
        ret_ld = [sem(f"ret_ld{j}") for j in range(3)]
        ret_out_ld = [sem(f"ret_out_ld{j}") for j in range(4)]
        h_hi_ready = sem("h_hi_ready")
        h_lo_ready = sem("h_lo_ready")
        w_hi_ready = sem("w_hi_ready")
        w_lo_ready = sem("w_lo_ready")
        part_used = sem("part_used")
        decay_ld = sem("decay_ld")
        ret_ps = sem("ret_ps")
        ret_sb = sem("ret_sb")
        rope_ready = sem("rope_ready")
        retT_ps = sem("retT_ps")
        retT_ready = sem("retT_ready")
        rscore_ps = sem("rscore_ps")
        decayed = sem("decayed")
        rhead_ps = sem("rhead_ps")
        rhead_sb = sem("rhead_sb")
        rvar_ready = sem("rvar_ready")
        rstd_ready = sem("rstd_ready")
        ret_y = sem("ret_y")
        ryT_ps = sem("ryT_ps")
        ryT_hi = sem("ryT_hi")
        ryT_lo = sem("ryT_lo")
        rw_ld = sem("rw_ld")
        x1_ready = sem("x1_ready")
        rest_ready = sem("rest_ready")
        x2_ready = sem("x2_ready")
        x3_ready = sem("x3_ready")
        logit_ps = sem("logit_ps")
        gdiff_ready = sem("gdiff_ready")
        gexp_ready = sem("gexp_ready")
        ediff_ready = sem("ediff_ready")
        eexp_ready = sem("eexp_ready")
        mask_ready = sem("mask_ready")
        rank_ps = sem("rank_ps")
        route_ready = sem("route_ready")
        gu_ld = [sem("gu_ld0"), sem("gu_ld1")]
        down_ld = [sem("down_ld0"), sem("down_ld1")]
        sel_ready = sem("sel_ready")
        gath_ps = sem("gath_ps")
        gath_sb = sem("gath_sb")
        gu_ps = sem("gu_ps")
        silu_ready = sem("silu_ready")
        act_ready = sem("act_ready")
        turn_ps = sem("turn_ps")
        turn_sb = sem("turn_sb")
        down_ps = sem("down_ps")
        y_hi_ready = sem("y_hi_ready")
        y_lo_ready = sem("y_lo_ready")
        scat_ps = sem("scat_ps")
        acc_done = sem("acc_done")
        dense = [{n: sem(f"dense{l}_{n}") for n in
                  ("ld", "gu", "silu", "act", "turn", "turned", "down", "added")} for l in range(DEPTH)]
        out_st = sem("out_st")

        n_in = [0]

        block = ctx.enter_context(nc.Block())
        rows8 = lambda w: w.rearrange("(p k) n -> p k n", k=KD)

        w_low = W[:, 0:KD * LOWRANK].rearrange("p (k n) -> p k n", k=KD)
        at = KD * LOWRANK
        w_conv = [W[:, at + 4096 * j:at + 4096 * (j + 1)].rearrange("p (k n) -> p k n", k=KD) for j in range(3)]
        at += 3 * 4096
        w_uq = W[:, at:at + 1536].rearrange("p (k n) -> p k n", k=QR // P)
        w_ukv = W[:, at + 1536:at + 2560]
        w_out0 = [M[:, 7168:10240].rearrange("p (k n) -> p k n", k=3), W[:, 20480:23552].rearrange("p (k n) -> p k n", k=3),
                  M[:, 832:2880].rearrange("p (k n) -> p k n", k=2)]
        qT0 = W[0:QK, 0:2048].rearrange("p (h t) -> p h t", h=HEADS)
        kT0 = W[0:QK, 2048:4096].rearrange("p (h t) -> p h t", h=HEADS)
        k_sb = W[:, 4096:5632].rearrange("p (t h c) -> p t h c", t=TT, h=HEADS)
        prob = W[:, 5632:6400].rearrange("p (b c) -> p b c", b=2)
        q_sb = W[:, 6400:7936].rearrange("p (t h c) -> p t h c", t=TT, h=HEADS)
        v_sb = W[:, 7936:8960].rearrange("p (t h c) -> p t h c", t=TT, h=HEADS)
        score = W[:, 8960:9728].rearrange("p (b c) -> p b c", b=2)
        low = M[:, 0:832].rearrange("p (t c) -> p t c", t=TT)
        conv_x = M[:, 832:1856].rearrange("p (c t) -> p c t", c=CT)
        conv_u = M[:, 1856:1856 + CT * (SEQ + 2)].rearrange("p (c t) -> p c t", c=CT)
        yT0 = M[:, 2888:4936].rearrange("p (k t) -> p k t", k=KD)
        lowT = M[:, 4936:5704].rearrange("p (k t) -> p k t", k=3)
        probT = M[:, 5704:6472].rearrange("p (b c) -> p b c", b=2)
        soft = M[:, 6472:6600]
        low_sq = M[:, 6600:6856]
        o_sb = hflat[:, 0:1024].rearrange("p (t c) -> p t c", t=TT)
        rope_t = [hflat[:, 1024 + 256 * j:1280 + 256 * j] for j in range(4)]

        w_raw = [W[:, 12288 + 2048 * j:14336 + 2048 * j] for j in range(3)]
        w_raw_out = [M[:, 2048 * j:2048 * (j + 1)] for j in range(4)]
        w_hi = [rounded(f"w_hi{j}", "W", 4096 * j, 2048) for j in range(2)]
        w_lo = [rounded(f"w_lo{j}", "W", 4096 * j + 2048, 2048) for j in range(2)]
        h_hi = rounded("h_hi", "W", 18432, 2048)
        h_lo = rounded("h_lo", "W", 20480, 2048)
        decay = W[:, 8192:10240].rearrange("p (h t) -> p h t", h=RH)
        rope_r = [W[:, 10240 + 512 * j:10752 + 512 * j].rearrange("p (h c) -> p h c", h=RH) for j in range(4)]
        v1 = M[:, 0:4096].rearrange("p (t c) -> p t c", t=TT)
        g1 = M[:, 4096:8192].rearrange("p (t c) -> p t c", t=TT)
        qkT1 = [M[:, 8192 + 2048 * j:10240 + 2048 * j].rearrange("p (h t) -> p h t", h=RH) for j in range(2)]
        raw1 = M[:, 12288:14336].rearrange("p (t h c) -> p t h c", t=TT, h=RH)
        turned1 = M[:, 14336:16384].rearrange("p (t h c) -> p t h c", t=TT, h=RH)
        o1 = M[:, 12288:16384].rearrange("p (t c) -> p t c", t=TT)
        yT_hi = rounded("yT_hi", "M", 8192, 4096)
        yT_lo = rounded("yT_lo", "W", 8192, 4096)
        sT1 = W[:, 10240:11008].rearrange("p (b c) -> p b c", b=2)
        rstat = W[:, 11008:11104].rearrange("p (t h c) -> p t h c", t=TT, h=RH)
        rmv = W[:, 11104:11136].rearrange("p (t h c) -> p t h c", t=TT, h=RH)
        rsd = W[:, 11136:11152].rearrange("p (t h) -> p t h", t=TT)
        rrs = W[:, 11152:11168].rearrange("p (t h) -> p t h", t=TT)

        w_gu = [W[:, 12288 - 12288 * b:20480 - 12288 * b].rearrange("p (u e k f) -> p u e k f", u=2, e=2, k=KD) for b in range(2)]
        w_down = [W[:, 20480 - 12288 * b:24576 - 12288 * b].rearrange("p (e k n) -> p e k n", e=2, k=KF) for b in range(2)]
        xselT = M[:, 2048:3072].rearrange("p (k s) -> p k s", k=KD)
        y_hi = rounded("y_hi", "M", 3072, D)
        y_lo = rounded("y_lo", "M", 4096, D)
        selT_hi = [rounded(f"selT_hi{b}", "M", 5120 + SEQ * b, SEQ) for b in range(2)]
        selT_lo = [rounded(f"selT_lo{b}", "M", 5632 + SEQ * b, SEQ) for b in range(2)]
        sel_w = [M[:, 6144 + 256 * b:6400 + 256 * b].rearrange("p (t e s) -> p t e s", t=TT, e=2) for b in range(2)]
        sel = [M[:, 6656 + 128 * b:6784 + 128 * b].bitcast(BF16).rearrange("p (t e s) -> p t e s", t=TT, e=2)
               for b in range(2)]
        turn = [M[:, 6912 + 256 * b:7168 + 256 * b] for b in range(2)]
        silu_sb = M[:, 7424:7680]
        act_sb = M[:, 7680:7936]
        r = M[:, 7936:8448]
        x_parts = [M[:, 8448 + 1024 * j:9472 + 1024 * j].bitcast(BF16).rearrange("p (t k q) -> p t k q", t=TT, k=KD)
                   for j in range(3)]
        x_rest = y_acc.rearrange("p t (k q) -> p t k q", k=KD)
        rank = r[:, 0:64].rearrange("p (t e) -> p t e", t=TT)
        cw = r[:, 64:128].rearrange("p (t e) -> p t e", t=TT)
        cw_over = r[:, 128:192].rearrange("p (t e) -> p t e", t=TT)
        mask = r[:, 192:256].rearrange("p (t e) -> p t e", t=TT)
        eq2 = r[:, 256:320].rearrange("p (t e) -> p t e", t=TT)
        g_pad = r[:, 320:336].rearrange("p (t e) -> p t e", t=TT)
        mx = r[:, 336:352].rearrange("p (t e) -> p t e", t=TT)
        mi = r[:, 352:368].bitcast(U32).rearrange("p (t e) -> p t e", t=TT)
        d4 = r[:, 368:376].rearrange("p (t e) -> p t e", t=TT)
        oh4 = r[:, 376:384].rearrange("p (t e) -> p t e", t=TT)
        e_sel = r[:, 384:400].rearrange("p (t e) -> p t e", t=TT)
        e_prod = r[:, 400:464].rearrange("p (t j g) -> p t j g", t=TT, j=PER_GROUP)
        g_sum = r[:, 464:466]
        g_p = r[:, 466:468].rearrange("p (t e) -> p t e", t=TT)
        g_i = r[:, 468:470].rearrange("p (t e) -> p t e", t=TT)
        g_8 = r[:, 470:472].rearrange("p (t e) -> p t e", t=TT)
        e_d = r[:, 472:474].rearrange("p (t e) -> p t e", t=TT)
        e_x = r[:, 474:476].rearrange("p (t e) -> p t e", t=TT)
        w_1 = r[:, 476:478].rearrange("p (t e) -> p t e", t=TT)
        w_2 = r[:, 478:480].rearrange("p (t e) -> p t e", t=TT)
        e_id = r[:, 480:484].rearrange("p (t e) -> p t e", t=TT)
        den = r[:, 484:486].rearrange("p (t e) -> p t e", t=TT)
        GATH, GU, DOWN, SCAT, TURN = (0, 1), 2, (3, 4), (5, 6), 7

        ada_w = [a["ada_mix_w"][0], a["ada_ffn_w"][0], a["ada_mix_w"][1], a["ada_ffn_w"][1]]
        ada_b = [a["ada_mix_b"][0], a["ada_ffn_b"][0], a["ada_mix_b"][1], a["ada_ffn_b"][1]]
        lng_d = [a["ln_mix_g"][0], a["ln_ffn_g"][0], a["ln_mix_g"][1], a["ln_ffn_g"][1]]
        lnb_d = [a["ln_mix_b"][0], a["ln_ffn_b"][0], a["ln_mix_b"][1], a["ln_ffn_b"][1]]
        wg_d = a["moe_w_gate"].rearrange("l e (p k) f -> (l e) p (k f)", k=KD)
        wu_d = a["moe_w_up"].rearrange("l e (p k) f -> (l e) p (k f)", k=KD)
        wd_d = a["moe_w_down"].rearrange("l e (p k) n -> (l e) p (k n)", k=KF)
        IN_LOADS = 16

        @block.sync
        def _(sp):
            def load_ada(n):
                ring, early = (RING, 0) if n < LATE else (2, LATE)
                if n - early >= ring:
                    sp.wait_ge(ada_used, n - ring + 1)
                s, u, k = n // KD // 3, n // KD % 3, n % KD
                ld = ada_ld[n % RING] if n < LATE else late_ld[n % 2]
                sp.dma_start(ada_buf(n), rows8(ada_w[s])[:, k, D * u:D * (u + 1)]).then_inc(ld, 16)

            def load_ln(s):
                if s:
                    sp.wait_ge(x_ready, 2 * s)
                sp.dma_start(ln_g[:, :], lng_d[s].partition_broadcast(P)).then_inc(ln_ld, 16)
                sp.dma_start(ln_b[:, :], lnb_d[s].partition_broadcast(P)).then_inc(ln_ld, 16)

            def load_gate_up(l, i, b, u):
                pair = bass.ds(EXPERTS * l + 2 * i, 2)
                sp.dma_start(w_gu[b][:, u], (wg_d, wu_d)[u][pair].rearrange("e p n -> p e n")).then_inc(gu_ld[b], 16)

            def load_down(l, i, b):
                pair = bass.ds(EXPERTS * l + 2 * i, 2)
                sp.dma_start(w_down[b], wd_d[pair].rearrange("e p n -> p e n")).then_inc(down_ld[b], 16)

            def load_experts(l, i, b):
                q = PAIRS * l + i
                sp.wait_ge(gu_ps, q - 1)
                load_gate_up(l, i, b, 0)
                load_gate_up(l, i, b, 1)
                sp.wait_ge(down_ps, 2 * (q - 1))
                load_down(l, i, b)

            def load_router(l):
                if l:
                    sp.wait_ge(logit_ps, l)
                sp.dma_start(router_w[:, :, 0:GROUPS], rows8(a["moe_rg_w"][l])).then_inc(rw_ld, 16)
                sp.dma_start(router_w[:, :, GROUPS:], rows8(a["moe_re_w"][l])).then_inc(rw_ld, 16)
                sp.dma_start(router_b[:, 0:GROUPS], a["moe_rg_b"][l].unsqueeze(0)).then_inc(rw_ld, 16)
                sp.dma_start(router_b[:, GROUPS:], a["moe_re_b"][l].unsqueeze(0)).then_inc(rw_ld, 16)

            def dense_loads(l):
                d = dense[l]
                sp.wait_ge(route_ready, l + 1)
                sp.wait_ge(down_ps, 2 * PAIRS * (l + 1))
                flag = sp.value_load(over[0:1, 0:1])
                with sp.If(flag > 0):
                    def load(e):
                        one = bass.ds(e + EXPERTS * l, 1)
                        sp.dma_start(w_gu[1][:, 0, 0:1], wg_d[one].rearrange("e p n -> p e n")).then_inc(d["ld"], 16)
                        sp.dma_start(w_gu[1][:, 1, 0:1], wu_d[one].rearrange("e p n -> p e n")).then_inc(d["ld"], 16)
                        sp.dma_start(w_down[1][:, 0:1], wd_d[one].rearrange("e p n -> p e n")).then_inc(d["ld"], 16)

                    load(0)
                    with sp.Fori(1, EXPERTS) as e:
                        sp.wait_ge(d["added"], 4 * e)
                        load(e)
                    sp.wait_ge(d["added"], 4 * EXPERTS)

            for dst, src in (
                (c_in[:, :], a["c"][0].rearrange("(p k) -> p k", k=KD)),
                (cst[:, :], a["table"]),
                (x[:, :, :], a["x"][0].rearrange("(t p) d -> p t d", p=P)),
                (pos_i, a["positions"][0].rearrange("(t p) -> t p", p=P)),
                (gain_rows[0:16, :], a["ret_gn_g"][0].rearrange("(k p) -> k p", p=P)),
                (gain_rows[16:18, :], a["ab_q_norm_g"][0].rearrange("(k p) -> k p", p=P)),
                (gain_rows[18:19, :], a["ab_kv_norm_g"][0].rearrange("(k p) -> k p", p=P)),
                (gain_rows[19:31, :], a["ab_conv_w"][0].rearrange("j (c p) -> (j c) p", p=P)),
            ):
                sp.dma_start(dst, src).then_inc(in_ld, 16)
                n_in[0] += 1
            for s in range(SUBLAYERS):
                sp.dma_start(bias_c[:, s, :, :],
                             ada_b[s][0:2 * D].rearrange("(u p k) -> p u k", u=2, k=KD)).then_inc(in_ld, 16)
                sp.dma_start(gates[0:1, s, :], ada_b[s][2 * D:3 * D].unsqueeze(0)).then_inc(in_ld, 16)
                n_in[0] += 2
            assert n_in[0] == IN_LOADS
            for n in range(3 * KD):
                load_ada(n)
            w_in = rows8(a["ab_w_in"][0])
            sp.dma_start(w_low, w_in[:, :, 3 * CONV:]).then_inc(lowrank_ld, 16)
            for j, c in enumerate((0, 2, 1)):
                sp.dma_start(w_conv[j], w_in[:, :, CONV * c:CONV * (c + 1)]).then_inc(convw_ld[j], 16)
            sp.dma_start(w_uq, a["ab_w_uq"][0].rearrange("(k p) n -> p k n", p=P)).then_inc(upw_ld, 16)
            sp.dma_start(w_ukv, a["ab_w_ukv"][0]).then_inc(upw_ld, 16)
            w_o = a["ab_w_out"][0].rearrange("(k p) n -> p k n", p=P)
            for n in range(3 * KD, 3 * KD + 8):
                load_ada(n)
            sp.dma_start(w_out0[0], w_o[:, 0:3, :]).then_inc(out_ld[0], 16)
            sp.dma_start(w_out0[1], w_o[:, 3:6, :]).then_inc(out_ld[1], 16)
            load_router(0)
            load_ln(0)
            for n in range(3 * KD + 8, 6 * KD):
                if n == 3 * KD + 12:
                    sp.wait_ge(conv_done, 1)
                    sp.dma_start(w_out0[2], w_o[:, 6:8, :]).then_inc(out_ld[2], 16)
                load_ada(n)
            sp.wait_ge(up_ps, 8)
            load_gate_up(0, 0, 0, 0)
            load_gate_up(0, 0, 0, 1)
            for n in range(6 * KD, 9 * KD):
                load_ada(n)
            sp.wait_ge(head_sb, HEADS)
            for u in range(2):
                load_gate_up(0, 1, 1, u)
            load_down(0, 1, 1)
            sp.wait_ge(y_ps, 2)
            load_down(0, 0, 0)
            load_ln(1)
            with sp.Fori(1, PAIRS // 2) as j:
                for b in range(2):
                    load_experts(0, 2 * j + b, b)
            w_in = rows8(a["ret_w_in"][0])

            def load_part(n):
                if n >= 3:
                    sp.wait_ge(w_lo_ready, n - 2)
                c, k = n // 2, 4 * (n % 2)
                sp.dma_start(w_raw[n % 3].rearrange("p (k n) -> p k n", k=4),
                             w_in[:, k:k + 4, HALF * c:HALF * (c + 1)]).then_inc(ret_ld[n % 3], 16)

            sp.wait_ge(down_ps, 2 * (PAIRS - 1))
            for n in range(3):
                load_part(n)
            dense_loads(0)
            load_router(1)
            load_ln(2)
            sp.wait_ge(down_ps, 2 * PAIRS)
            sp.dma_start(W[:, 8192:10240], a["decay"]).then_inc(decay_ld, 16)
            late = LATE
            for c in range(RET_CHUNKS):
                for n in (2 * c + 3, 2 * c + 4):
                    if n < RET_PARTS:
                        load_part(n)
                for _ in range(LATE_AT.get(c, 0)):
                    if late == LATE:
                        sp.wait_ge(h_lo_ready, 1)
                    load_ada(late)
                    late += 1
            assert late == BLOCKS
            w_o = a["ret_w_out"][0].rearrange("(k p) n -> p k n", p=P)

            def load_out_part(j):
                if j < 2:
                    sp.wait_ge(rhead_ps, RH)
                elif j < 4:
                    sp.wait_ge(ret_y, 1)
                else:
                    sp.wait_ge(w_lo_ready, RET_PARTS + j - 3)
                sp.dma_start(w_raw_out[j % 4].rearrange("p (k n) -> p k n", k=2), w_o[:, 2 * j:2 * j + 2, :])\
                  .then_inc(ret_out_ld[j % 4], 16)

            load_out_part(0)
            load_out_part(1)
            sp.wait_ge(ret_ps, 2 * RET_CHUNKS)
            sp.wait_ge(ada_used, BLOCKS)
            load_gate_up(1, 0, 0, 0)
            for j in range(2, 5):
                load_out_part(j)
            load_gate_up(1, 0, 0, 1)
            for j in range(5, OUT_PARTS):
                load_out_part(j)
            load_down(1, 0, 0)
            sp.wait_ge(y_ps, 4)
            for u in range(2):
                load_gate_up(1, 1, 1, u)
            load_down(1, 1, 1)
            load_ln(3)
            with sp.Fori(1, PAIRS // 2) as j:
                for b in range(2):
                    load_experts(1, 2 * j + b, b)
            dense_loads(1)
            for t in range(TT):
                sp.wait_ge(x_ready, 2 * (SUBLAYERS - 1) + t + 1)
                sp.dma_start(out[0, P * t:P * (t + 1), :], x[:, t, :]).then_inc(out_st, 16)
            sp.wait_ge(out_st, 16 * TT)

        @block.scalar
        def _(act):
            ch = Chain(act, act_chain)

            def h_banks(s):
                for bank in (1, 3):
                    act.wait_ge(xT_ps, 4 * s + bank + 1)
                    act.wait_ge(third_ready, 3 * s + 2)
                    for k in (2 * bank, 2 * bank + 1):
                        ins = act.activation(hT[:, k, :], PS[:, bank, 256 * (k % 2):256 * (k % 2) + 256], ACT.Identity,
                                             bias=mod_c[:, s, 0, k:k + 1], scale=mod_c[:, s, 1, k:k + 1])
                    ins.then_inc(hT_odd, 1)

            def norm_std(s):
                for t in range(TT):
                    act.wait_ge(var_ready, 2 * s + t + 1)
                    act.activation(std[:, t:t + 1], mv[:, t, 1:2], ACT.Sqrt).then_inc(std_ready, 1)

            def router(l):
                xk = x[:, :, :].rearrange("q t (p k) -> q t k p", k=KD)
                for t in range(TT):
                    act.activation(x_parts[0][:, t], xk[:, t], ACT.Copy).then_inc(x1_ready, 1)
                for t in range(TT):
                    act.wait_ge(rest_ready, 2 * l + t + 1)
                    act.activation(x_parts[1][:, t], x_rest[:, t], ACT.Copy).then_inc(x2_ready, 1)
                act.wait_ge(gdiff_ready, l + 1)
                act.activation(d4, d4, ACT.Exp).then_inc(gexp_ready, 1)
                act.wait_ge(ediff_ready, l + 1)
                act.activation(e_x, e_d, ACT.Exp).then_inc(eexp_ready, 1)

            def gathered(l, q):
                for g in range(2):
                    act.wait_ge(gath_ps, 2 * q + g + 1)
                    for k in range(4 * g, 4 * g + 4):
                        ins = act.activation(xselT[:, k, :], PS[:, GATH[g], P * (k % 4):P * (k % 4) + P], ACT.Identity,
                                             bias=mod_c[:, 2 * l + 1, 0, k:k + 1], scale=mod_c[:, 2 * l + 1, 1, k:k + 1])
                    ins.then_inc(gath_sb, 1)

            def pair(l, i, last=False):
                q = PAIRS * l + i
                act.wait_ge(gu_ps, q + 1)
                act.activation(silu_sb, PS[:, GU, 0:FE], ACT.Silu).then_inc(silu_ready, 1)
                if not last:
                    gathered(l, q + 1)
                for h in range(2):
                    act.wait_ge(down_ps, 2 * q + h + 1)
                    act.activation(y_hi[:, HALF * h:HALF * (h + 1)], PS[:, DOWN[h], :], ACT.Copy).then_inc(y_hi_ready, 1)

            def experts(l):
                gathered(l, PAIRS * l)
                with act.Fori(0, PAIRS // 2 - 1) as j:
                    for b in range(2):
                        pair(l, 2 * j + b)
                pair(l, PAIRS - 2)
                pair(l, PAIRS - 1, last=True)
                d = dense[l]
                act.wait_ge(route_ready, l + 1)
                flag = act.value_load(over[0:1, 0:1])
                with act.If(flag > 0):
                    with act.Fori(0, EXPERTS) as e:
                        for t in range(TT):
                            act.wait_ge(d["gu"], 2 * e + t + 1)
                            act.activation(silu_sb, PS[:, GU, 0:FE], ACT.Silu).then_inc(d["silu"], 1)

            act.wait_ge(in_ld, 16 * IN_LOADS)
            act.activation(c_silu[:, :], c_in[:, :], ACT.Silu).then_inc(c_silu_ready, 1)
            act.wait_ge(angle_ready, 4)
            act.activation(trig_m[:, :, :, :], trig_m[:, :, :, :], ACT.Sin)
            act.activation(trig_r[:, :, :, :], trig_r[:, :, :, :], ACT.Sin).then_inc(trig_ready, 1)

            h_banks(0)
            for t in range(TT):
                act.wait_ge(lowrank_sb, t + 1)
                act.activation(low_sq, low[:, t, 0:QR], ACT.Square, accum_out=soft[:, 2 * t:2 * t + 1]).then_inc(square_ready, 1)
                ch.step(act.activation(M[:, 6856:6984], low[:, t, QR:QR + KVR], ACT.Square,
                                       accum_out=soft[:, 2 * t + 1:2 * t + 2]))
                ch.hold()
            act.wait_ge(square_ready, TT)
            act.wait_ge(ms_ready, 2)
            act.activation(soft[:, 8:12], soft[:, 4:8], ACT.Sqrt).then_inc(rms_ready, 1)
            act.wait_ge(conv_ps, 2)
            for h in range(2):
                act.activation(conv_x[:, 2 * h:2 * h + 2, :].rearrange("p c t -> p (c t)"), PS[:, 2 + h, :],
                               ACT.Copy).then_inc(conv_x_sb, 1)
            for t in range(TT):
                for h in range(2):
                    act.wait_ge(up_ps, 2 * t + h + 1)
                    act.activation(q_sb[:, t, 4 * h:4 * h + 4, :],
                                   PS[:, 2 * t + h, 0:4 * QK].rearrange("p (h c) -> p h c", h=4), ACT.Copy).then_inc(up_q_sb, 1)
            for t in range(TT):
                for h in range(2):
                    act.wait_ge(up_ps, 4 + 2 * t + h + 1)
                    src = PS[:, 4 + 2 * t + h, :].rearrange("p (h c) -> p h c", h=4)
                    act.activation(k_sb[:, t, 4 * h:4 * h + 4, 0:NOPE], src[:, :, 0:NOPE], ACT.Copy).then_inc(up_k_sb, 1)
                    act.activation(v_sb[:, t, 4 * h:4 * h + 4, :], src[:, :, NOPE:], ACT.Copy).then_inc(up_k_sb, 1)
            for h in range(HEADS):
                b = h % 2
                act.wait_ge(shift_ready, h + 1)
                if h >= 2:
                    act.wait_ge(probT_ps, h - 1)
                act.activation(prob[:, b, 0:P], score[:, b, 0:P], ACT.Exp, bias=soft[:, 16 + 2 * h:17 + 2 * h],
                               scale=MLA_SCALE, accum_out=soft[:, 32 + 2 * h:33 + 2 * h]).then_inc(prob_ready, 1)
                act.activation(prob[:, b, P:3 * P], score[:, b, P:3 * P], ACT.Exp, bias=soft[:, 17 + 2 * h:18 + 2 * h],
                               scale=MLA_SCALE, accum_out=soft[:, 33 + 2 * h:34 + 2 * h]).then_inc(prob_ready, 1)
            norm_std(0)

            h_banks(1)
            router(0)
            experts(0)
            norm_std(1)

            h_banks(2)
            act.wait_ge(hT_even, 6)
            ch.hold()
            act.wait_ge(hT_odd, 6)
            act.activation(h_hi[:, :], hflat, ACT.Copy).then_inc(h_hi_ready, 1)

            def split_hi(n):
                j = n - RET_PARTS
                if j < 0:
                    act.wait_ge(ret_ld[n % 3], 16 * (n // 3 + 1))
                else:
                    act.wait_ge(ret_out_ld[j % 4], 16 * (j // 4 + 1))
                m = n - 2
                if m >= RET_PARTS:
                    act.wait_ge(part_used, RET_CHUNKS + m - RET_PARTS + 1)
                elif m >= 0:
                    act.wait_ge(ret_ps if m % 2 else part_used, m + 1 if m % 2 else m // 2 + 1)
                act.activation(w_hi[n % 2][:, :], w_raw[n % 3] if j < 0 else w_raw_out[j % 4], ACT.Copy).then_inc(w_hi_ready, 1)

            def head_out(h):
                act.wait_ge(rhead_ps, h + 1)
                for t in range(TT):
                    act.activation(o1[:, t, DV * h:DV * (h + 1)], PS[:, 6 + h % 2, DV * t:DV * (t + 1)],
                                   ACT.Copy).then_inc(rhead_sb, 1)

            split_hi(0)
            split_hi(1)
            for c in range(RET_CHUNKS):
                for n in (2 * c + 2, 2 * c + 3):
                    if n < RET_PARTS:
                        split_hi(n)
                for t in range(TT):
                    n = 2 * c + t
                    act.wait_ge(ret_ps, n + 1)
                    bank = PS[:, n % 4, :]
                    if c < 4:
                        if c == 2:
                            act.wait_ge(rope_ready, 2)
                        dst = raw1[:, t, 4 * (c % 2):4 * (c % 2) + 4, :].rearrange("p h c -> p (h c)")
                        act.activation(dst, bank, ACT.Copy).then_inc(ret_sb, 1)
                    elif c < 8:
                        act.activation(v1[:, t, HALF * (c - 4):HALF * (c - 3)], bank, ACT.Copy).then_inc(ret_sb, 1)
                    else:
                        act.activation(g1[:, t, HALF * (c - 8):HALF * (c - 7)], bank, ACT.Silu).then_inc(ret_sb, 1)
                if c >= 8:
                    head_out(2 * (c - 8))
                    head_out(2 * (c - 8) + 1)
            split_hi(RET_PARTS)
            split_hi(RET_PARTS + 1)
            act.wait_ge(rvar_ready, 1)
            act.activation(rsd, rsd, ACT.Sqrt).then_inc(rstd_ready, 1)
            for n in range(OUT_PARTS):
                act.wait_ge(ryT_ps, n + 1)
                for k in (2 * n, 2 * n + 1):
                    act.activation(yT_hi[:, SEQ * k:SEQ * (k + 1)], PS[:, 4 + n % 4, 256 * (k % 2):256 * (k % 2) + 256], ACT.Copy,
                                   scale=gn_g[:, k:k + 1]).then_inc(ryT_hi, 1)
            for j in range(2, OUT_PARTS):
                split_hi(RET_PARTS + j)
            norm_std(2)

            h_banks(3)
            router(1)
            experts(1)
            norm_std(3)

        @block.tensor
        def _(pe):
            def third(m, bank):
                acc, s = ada_acc(m), m // 3
                pe.wait_ge(ada_used, KD * (m + 1))
                if m % 3 < 2:
                    part = acc.rearrange("q (p k) -> q k p", k=KD)
                    for k in range(KD):
                        ins = pe.matmul(PS[:, bank, k:k + 1], part[:, k, :], ones[:, 0:1], start=True, stop=True)
                else:
                    for h in range(2):
                        cut = slice(HALF * h, HALF * (h + 1))
                        pe.matmul(PS[:, bank + h, :], ones, acc[:, cut], start=True, stop=False)
                        ins = pe.matmul(PS[:, bank + h, :], ones[0:1, :], gates[0:1, s, cut], start=False, stop=True)
                ins.then_inc(third_ps, 1)

            def turn_x(s):
                if s:
                    pe.wait_ge(x_ready, 2 * s)
                xk = x[:, :, :].rearrange("q t (p k) -> q t k p", k=KD)
                for k in range(KD):
                    for t in range(TT):
                        at = 256 * (k % 2) + P * t
                        ins = pe.transpose(PS[:, k // 2, at:at + P], xk[:, t, k, :], ident)
                    if k % 2:
                        ins.then_inc(xT_ps, 1)

            def h_ready(s):
                pe.wait_ge(hT_even, 2 * (s + 1))
                pe.wait_ge(hT_odd, 2 * (s + 1))

            def router(l):
                h_ready(2 * l + 1)
                pe.wait_ge(third_ready, (9, 12)[l])
                pe.wait_ge(rw_ld, 64 * (l + 1))
                for t in range(TT):
                    o = PS[:, 4, 64 * t:64 * t + GROUPS + EXPERTS]
                    for k in range(KD):
                        pe.matmul(o, hT[:, k, P * t:P * (t + 1)], router_w[:, k, :], start=(k == 0), stop=False)
                    ins = pe.matmul(o, ones[0:1, :], router_b[0:1, :], start=False, stop=True)
                ins.then_inc(logit_ps, 1)
                pe.wait_ge(mask_ready, l + 1)
                pe.matmul(PS[:, 5, 0:32], upper, mask[:, 0, :], start=True, stop=True)
                pe.matmul(PS[:, 5, 32:64], ones, mask[:, 0, :], start=True, stop=False)
                pe.matmul(PS[:, 5, 32:64], upper, mask[:, 1, :], start=False, stop=True)
                pe.matmul(PS[:, 5, 64:96], ones, mask[:, 0, :], start=True, stop=False)
                pe.matmul(PS[:, 5, 64:96], ones, mask[:, 1, :], start=False, stop=True).then_inc(rank_ps, 1)

            def gather(q, b):
                pe.wait_ge(sel_ready, q + 1)
                for g in range(2):
                    for k in range(4 * g, 4 * g + 4):
                        o = PS[:, GATH[g], P * (k % 4):P * (k % 4) + P]
                        for t in range(TT):
                            for j in range(3):
                                ins = pe.matmul(o, x_parts[j][:, t, k, :], sel[b][:, t].rearrange("p e s -> p (e s)"),
                                                start=(t + j == 0), stop=(t + j == TT + 1))
                    ins.then_inc(gath_ps, 1)

            def scatter(q, b):
                pe.wait_ge(y_lo_ready, 2 * (q + 1))
                for t in range(TT):
                    for h in range(2):
                        c = 2 * t + h
                        if not (isinstance(q, int) and 4 * q + c < 2):
                            pe.wait_ge(acc_done, 4 * q + c - 1)
                        tok, cut = slice(P * t, P * (t + 1)), slice(HALF * h, HALF * (h + 1))
                        pe.matmul(PS[:, SCAT[c % 2], :], selT_hi[b][:, tok], y_hi[:, cut], start=True, stop=False)
                        pe.matmul(PS[:, SCAT[c % 2], :], selT_hi[b][:, tok], y_lo[:, cut], start=False, stop=False)
                        pe.matmul(PS[:, SCAT[c % 2], :], selT_lo[b][:, tok], y_hi[:, cut], start=False, stop=True)\
                          .then_inc(scat_ps, 1)

            def pair(l, i, b, first=False, last=False):
                q = PAIRS * l + i
                pe.wait_ge(gath_sb, 2 * (q + 1))
                pe.wait_ge(gu_ld[b], 32 * (PAIRS // 2 * l + 1) + 16 * (i - b))
                if not (isinstance(q, int) and q == 0):
                    pe.wait_ge(act_ready, q)
                for k in range(KD):
                    for e in range(2):
                        o = PS[64 * e:64 * e + 64, GU, :].rearrange("p (u f) -> p u f", u=2)
                        ins = pe.matmul(o, xselT[:, k, 64 * e:64 * e + 64], w_gu[b][:, :, e, k, :],
                                        start=(k == 0), stop=(k == KD - 1))
                ins.then_inc(gu_ps, 1)
                if not last:
                    gather(q + 1, 1 - b)
                pe.wait_ge(act_ready, q + 1)
                if not (isinstance(q, int) and q == 0):
                    pe.wait_ge(turn_sb, q)
                for k in range(KF):
                    pe.transpose(PS[:, TURN, P * k:P * (k + 1)], act_sb[:, P * k:P * (k + 1)], ident)
                for t in range(TT):
                    ins = pe.transpose(PS[:, TURN, 2 * P + P * t:2 * P + P * (t + 1)],
                                       sel_w[b][:, t].rearrange("p e s -> p (e s)"), ident)
                ins.then_inc(turn_ps, 1)
                if not first:
                    scatter(q - 1, 1 - b)
                pe.wait_ge(turn_sb, q + 1)
                pe.wait_ge(down_ld[b], 16 * (PAIRS // 2 * l + 1) + 8 * (i - b))
                if not (isinstance(q, int) and q == 0):
                    pe.wait_ge(y_lo_ready, 2 * q)
                for h in range(2):
                    for k in range(KF):
                        for e in range(2):
                            ins = pe.matmul(PS[64 * e:64 * e + 64, DOWN[h], :], turn[b][:, P * k + 64 * e:P * k + 64 * e + 64],
                                            w_down[b][:, e, k, HALF * h:HALF * (h + 1)], start=(k == 0), stop=(k == KF - 1))
                    ins.then_inc(down_ps, 1)

            def experts(l):
                gather(PAIRS * l, 0)
                pair(l, 0, 0, first=True)
                pair(l, 1, 1)
                with pe.Fori(1, PAIRS // 2 - 1) as j:
                    for b in range(2):
                        pair(l, 2 * j + b, b)
                pair(l, PAIRS - 2, 0)
                pair(l, PAIRS - 1, 1, last=True)
                scatter(PAIRS * (l + 1) - 1, 1)
                d = dense[l]
                pe.wait_ge(acc_done, 4 * PAIRS * (l + 1))
                flag = pe.value_load(over[0:1, 0:1])
                with pe.If(flag > 0):
                    with pe.Fori(0, EXPERTS) as e:
                        pe.wait_ge(d["ld"], 48 * e + 48)
                        for t in range(TT):
                            for k in range(KD):
                                ins = pe.matmul(PS[:, GU, :].rearrange("p (u f) -> p u f", u=2), hT[:, k, P * t:P * (t + 1)],
                                                w_gu[1][:, :, 0, k, :], start=(k == 0), stop=(k == KD - 1))
                            ins.then_inc(d["gu"], 1)
                            pe.wait_ge(d["act"], 2 * e + t + 1)
                            for k in range(KF):
                                ins = pe.transpose(PS[:, TURN, P * k:P * (k + 1)], act_sb[:, P * k:P * (k + 1)], ident)
                            ins.then_inc(d["turn"], 1)
                            pe.wait_ge(d["turned"], 2 * e + t + 1)
                            for h in range(2):
                                for k in range(KF):
                                    ins = pe.matmul(PS[:, DOWN[h], :], turn[0][:, P * k:P * (k + 1)],
                                                    w_down[1][:, 0, k, HALF * h:HALF * (h + 1)], start=(k == 0), stop=(k == KF - 1))
                            ins.then_inc(d["down"], 1)
                            pe.wait_ge(d["added"], 4 * e + 2 * t + 2)

            pe.wait_ge(in_ld, 16 * IN_LOADS)
            pe.transpose(PS[:, 7, 0:31], gain_rows, ident[0:31, 0:31])
            pe.wait_ge(pos_rows, 1)
            pe.transpose(PS[:, 7, 32:34], pos_r, ident[0:TT, 0:TT]).then_inc(columns_ps, 1)
            turn_x(0)
            third(0, 4)
            third(1, 5)
            h_ready(0)
            pe.wait_ge(lowrank_ld, 16)
            for t in range(TT):
                for k in range(KD):
                    ins = pe.matmul(PS[:, t, 0:LOWRANK], hT[:, k, P * t:P * (t + 1)], w_low[:, k, :],
                                    start=(k == 0), stop=(k == KD - 1))
                ins.then_inc(lowrank_ps, 1)
            third(2, 6)
            for j in range(3):
                pe.wait_ge(convw_ld[j], 16)
                if j == 2:
                    pe.wait_ge(third_ready, 3)
                for c in range(CT):
                    o = PS[:, 2 + 2 * j + c // 2, 256 * (c % 2):256 * (c % 2) + 256]
                    for k in range(KD):
                        ins = pe.matmul(o, w_conv[j][:, k, P * c:P * (c + 1)], hT[:, k, :], start=(k == 0), stop=(k == KD - 1))
                    if c % 2:
                        ins.then_inc(conv_ps, 1)
            pe.wait_ge(lowrank_n, TT)
            for k in range(3):
                for t in range(TT):
                    at = 256 * (k % 2) + P * t
                    ins = pe.transpose(PS[:, k // 2, at:at + P], low[:, t, P * k:P * (k + 1)], ident)
            ins.then_inc(lowT_ps, 1)
            pe.wait_ge(lowT_ready, 1)
            pe.wait_ge(upw_ld, 32)
            pe.wait_ge(conv_x_sb, 2)
            for t in range(TT):
                for h in range(2):
                    for k in range(2):
                        ins = pe.matmul(PS[:, 2 * t + h, 0:4 * QK], lowT[:, k, P * t:P * (t + 1)], w_uq[:, k, 4 * QK * h:4 * QK * (h + 1)],
                                        start=(k == 0), stop=(k == 1))
                    ins.then_inc(up_ps, 1)
            pe.wait_ge(conv_done, 1)
            for t in range(TT):
                for h in range(2):
                    pe.matmul(PS[:, 4 + 2 * t + h, :], lowT[:, 2, P * t:P * (t + 1)], w_ukv[:, HALF * h:HALF * (h + 1)],
                              start=True, stop=True).then_inc(up_ps, 1)
            pe.wait_ge(up_q_sb, 4)
            pe.wait_ge(up_k_sb, 8)
            for u, src in enumerate((q_sb, k_sb)):
                pe.wait_ge(qk_ready, u + 1)
                for h in range(HEADS):
                    for t in range(TT):
                        at = 256 * (h % 2) + P * t
                        ins = pe.transpose(PS[0:QK, 4 * u + h // 2, at:at + P], src[:, t, h, :], ident)
                    if h % 2:
                        ins.then_inc(qkT_ps, 1)
            pe.wait_ge(qkT_ready, 8)

            def scores(h):
                b = h % 2
                if h >= 2:
                    pe.wait_ge(shift_ready, h - 1)
                pe.matmul(PS[:, b, 0:P], qT0[:, h, 0:P], kT0[:, h, 0:P], start=True, stop=True)
                pe.matmul(PS[:, b, P:3 * P], qT0[:, h, P:SEQ], kT0[:, h, :], start=True, stop=True).then_inc(score_ps, 1)

            scores(0)
            for h in range(HEADS):
                b = h % 2
                if h + 1 < HEADS:
                    scores(h + 1)
                pe.wait_ge(prob_ready, 2 * (h + 1))
                if h >= 2:
                    pe.wait_ge(probT_ready, h - 1)
                if h in (1, 5):
                    third(3 + h // 4, 6 + h // 4)
                for j in range(3):
                    ins = pe.transpose(PS[:, 2 + b, P * j:P * (j + 1)], prob[:, b, P * j:P * (j + 1)], ident)
                ins.then_inc(probT_ps, 1)
                pe.wait_ge(probT_ready, h + 1)
                if h >= 2:
                    pe.wait_ge(head_sb, h - 1)
                pe.matmul(PS[:, 4 + b, 0:HV], probT[:, b, 0:P], v_sb[:, 0, h, :], start=True, stop=True)
                pe.matmul(PS[:, 4 + b, HV:2 * HV], probT[:, b, P:2 * P], v_sb[:, 0, h, :], start=True, stop=False)
                pe.matmul(PS[:, 4 + b, HV:2 * HV], probT[:, b, 2 * P:3 * P], v_sb[:, 1, h, :], start=False, stop=True)\
                  .then_inc(head_ps, 1)
            pe.wait_ge(head_sb, HEADS)
            pe.wait_ge(third_ready, 5)
            for k in range(4):
                for t in range(TT):
                    at = 256 * (k % 2) + P * t
                    ins = pe.transpose(PS[:, 6 + k // 2, at:at + P], o_sb[:, t, P * k:P * (k + 1)], ident)
            ins.then_inc(oT_ps, 1)
            third(5, 4)
            pe.wait_ge(oT_ready, 1)
            for j in range(3):
                pe.wait_ge(out_ld[j], 16)
            for t in range(TT):
                for h in range(2):
                    for k in range(KD):
                        ins = pe.matmul(PS[:, 2 * t + h, :], yT0[:, k, P * t:P * (t + 1)],
                                        w_out0[k // 3][:, k % 3, HALF * h:HALF * (h + 1)], start=(k == 0), stop=(k == KD - 1))
                ins.then_inc(y_ps, 1)
                if t == 0:
                    third(6, 6)

            third(7, 7)
            pe.wait_ge(third_ready, 6)
            third(8, 4)
            turn_x(1)
            router(0)
            experts(0)

            pe.wait_ge(x_ready, 4)
            turn_x(2)
            h_ready(2)
            pe.wait_ge(h_lo_ready, 1)

            def turn_heads(u):
                pe.wait_ge(rope_ready, 2 * (u + 1))
                if u:
                    pe.wait_ge(retT_ready, 4)
                for h in range(RH):
                    for t in range(TT):
                        at = 256 * (h % 2) + P * t
                        ins = pe.transpose(PS[:, 4 + h // 2, at:at + P], turned1[:, t, h, :], ident)
                    if h % 2:
                        ins.then_inc(retT_ps, 1)

            def ret_scores(h):
                b = h % 2
                if h >= 2:
                    pe.wait_ge(decayed, h - 1)
                pe.matmul(PS[:, 4 + b, 0:SEQ], qkT1[1][:, h, 0:P], qkT1[0][:, h, :], start=True, stop=True)
                pe.matmul(PS[:, 4 + b, SEQ:SEQ + P], qkT1[1][:, h, P:SEQ], qkT1[0][:, h, P:SEQ], start=True, stop=True)\
                  .then_inc(rscore_ps, 1)

            def ret_head(h):
                b = h % 2
                pe.wait_ge(decayed, h + 1)
                if h >= 2:
                    pe.wait_ge(rhead_sb, 2 * (h - 1))
                vh = v1[:, :, DV * h:DV * (h + 1)]
                pe.matmul(PS[:, 6 + b, 0:DV], sT1[:, b, 0:P], vh[:, 0, :], start=True, stop=True)
                pe.matmul(PS[:, 6 + b, DV:2 * DV], sT1[:, b, P:2 * P], vh[:, 0, :], start=True, stop=False)
                pe.matmul(PS[:, 6 + b, DV:2 * DV], sT1[:, b, 2 * P:3 * P], vh[:, 1, :], start=False, stop=True)\
                  .then_inc(rhead_ps, 1)

            for c in range(RET_CHUNKS):
                for part in range(2):
                    m = 2 * c + part
                    pe.wait_ge(w_lo_ready, m + 1)
                    hi = w_hi[m % 2][:, :].rearrange("p (k n) -> p k n", k=4)
                    lo = w_lo[m % 2][:, :].rearrange("p (k n) -> p k n", k=4)
                    for t in range(TT):
                        n = 2 * c + t
                        if n >= 4 and part == 0:
                            pe.wait_ge(ret_sb, n - 3)
                        for k in range(4):
                            kk = 4 * part + k
                            tok = slice(SEQ * kk + P * t, SEQ * kk + P * (t + 1))
                            pe.matmul(PS[:, n % 4, :], h_hi[:, tok], hi[:, k, :], start=(kk == 0), stop=False)
                            pe.matmul(PS[:, n % 4, :], h_hi[:, tok], lo[:, k, :], start=False, stop=False)
                            ins = pe.matmul(PS[:, n % 4, :], h_lo[:, tok], hi[:, k, :], start=False, stop=(kk == KD - 1))
                        if part == 1:
                            ins.then_inc(ret_ps, 1)
                    if part == 0:
                        ins.then_inc(part_used, 1)
                if c == 3:
                    turn_heads(0)
                if c == 5:
                    turn_heads(1)
                if c == 7:
                    pe.wait_ge(retT_ready, 8)
                    third(9, 4)
                    third(10, 5)
                    pe.wait_ge(third_ready, 11)
                    pe.wait_ge(ret_sb, 16)
                if c >= 8:
                    ret_head(2 * (c - 8))
                    ret_head(2 * (c - 8) + 1)
                if 7 <= c < 11:
                    ret_scores(2 * (c - 7))
                    ret_scores(2 * (c - 7) + 1)
            pe.wait_ge(decayed, RH)
            pe.wait_ge(rhead_sb, 2 * RH)
            third(11, 4)
            pe.wait_ge(third_ready, 12)
            for n in range(OUT_PARTS):
                if n == 0:
                    pe.wait_ge(ret_y, 1)
                if n >= 4:
                    pe.wait_ge(ryT_lo, 2 * (n - 3))
                for k in (2 * n, 2 * n + 1):
                    for t in range(TT):
                        at = 256 * (k % 2) + P * t
                        ins = pe.transpose(PS[:, 4 + n % 4, at:at + P], o1[:, t, P * k:P * (k + 1)], ident)
                ins.then_inc(ryT_ps, 1)
            pe.wait_ge(ret_sb, 2 * RET_CHUNKS)
            for j in range(OUT_PARTS):
                m = RET_PARTS + j
                pe.wait_ge(w_lo_ready, m + 1)
                pe.wait_ge(ryT_lo, 2 * (j + 1))
                hi = w_hi[m % 2][:, :].rearrange("p (k n) -> p k n", k=2)
                lo = w_lo[m % 2][:, :].rearrange("p (k n) -> p k n", k=2)
                for t in range(TT):
                    for h in range(2):
                        cut = slice(HALF * h, HALF * (h + 1))
                        for k in range(2):
                            kk = 2 * j + k
                            tok = slice(SEQ * kk + P * t, SEQ * kk + P * (t + 1))
                            pe.matmul(PS[:, 2 * t + h, :], yT_hi[:, tok], hi[:, k, cut], start=(kk == 0), stop=False)
                            pe.matmul(PS[:, 2 * t + h, :], yT_hi[:, tok], lo[:, k, cut], start=False, stop=False)
                            ins = pe.matmul(PS[:, 2 * t + h, :], yT_lo[:, tok], hi[:, k, cut], start=False, stop=(kk == RV // P - 1))
                    if j == OUT_PARTS - 1:
                        ins.then_inc(y_ps, 1)
                if j < OUT_PARTS - 1:
                    ins.then_inc(part_used, 1)

            turn_x(3)
            router(1)
            experts(1)

        @block.vector
        def _(dve):
            ch = Chain(dve, dve_chain)

            def ada_sum(n):
                m, k = n // KD, n % KD
                acc = ada_acc(m)
                if n < LATE:
                    dve.wait_ge(ada_ld[n % RING], 16 * (n // RING + 1))
                else:
                    dve.wait_ge(late_ld[n % 2], 16 * ((n - LATE) // 2 + 1))
                if k == 0:
                    if m >= 2:
                        dve.wait_ge(third_ps, m - 1)
                    dve.tensor_scalar(acc, ada_buf(n), c_silu[:, 0:1], None, ALU.mult).then_inc(ada_used, 1)
                else:
                    dve.wait_ge(ada_used, n)
                    dve.scalar_tensor_tensor(acc, ada_buf(n), c_silu[:, k:k + 1], acc, ALU.mult, ALU.add)\
                       .then_inc(ada_used, 1)

            def third(m, bank):
                s, u = m // 3, m % 3
                dve.wait_ge(third_ps, m + 1)
                if u == 0:
                    dve.tensor_tensor(mod_c[:, s, 0, :], PS[:, bank, 0:KD], bias_c[:, s, 0, :], ALU.add).then_inc(third_ready, 1)
                elif u == 1:
                    dve.scalar_tensor_tensor(mod_c[:, s, 1, :], PS[:, bank, 0:KD], 1.0, bias_c[:, s, 1, :], ALU.add, ALU.add)\
                       .then_inc(third_ready, 1)
                else:
                    for h in range(2):
                        ins = dve.tensor_scalar(gates[:, s, HALF * h:HALF * (h + 1)], PS[:, bank + h, :], 1.0, None, ALU.add)
                    ins.then_inc(third_ready, 1)

            def h_banks(s):
                dve.wait_ge(third_ready, 3 * s + 2)
                for bank in (0, 2):
                    dve.wait_ge(xT_ps, 4 * s + bank + 1)
                    for k in (2 * bank, 2 * bank + 1):
                        ins = dve.tensor_scalar(hT[:, k, :], PS[:, bank, 256 * (k % 2):256 * (k % 2) + 256],
                                                mod_c[:, s, 1, k:k + 1], mod_c[:, s, 0, k:k + 1], ALU.mult, ALU.add)
                    ins.then_inc(hT_even, 1)

            def layer_norm(s, y):
                z = y_acc
                dve.wait_ge(third_ready, 3 * s + 3)
                for t in range(TT):
                    for h in range(2):
                        cut = slice(HALF * h, HALF * (h + 1))
                        ch.step(dve.tensor_tensor(z[:, t, cut], y(t, h), gates[:, s, cut], ALU.mult))
                    ch.hold()
                    ch.link(dve.scalar_tensor_tensor(z[:, t, :], x[:, t, :], ALPHA, z[:, t, :], ALU.mult, ALU.add))
                    for h in range(2):
                        ch.step(dve.bn_stats(stats[:, t, h, :], z[:, t, HALF * h:HALF * (h + 1)]))
                    ch.hold()
                    ch.link(dve.bn_aggr(mv[:, t, :], stats[:, t, :, :].rearrange("p h c -> p (h c)")))
                    dve.tensor_scalar(mv[:, t, 1:2], mv[:, t, 1:2], LN_EPS, None, ALU.add).then_inc(var_ready, 1)
                dve.wait_ge(ln_ld, 32 * (s + 1))
                for t in range(TT):
                    dve.wait_ge(std_ready, 2 * s + t + 1)
                    ch.link(dve.reciprocal(rstd[:, t:t + 1], std[:, t:t + 1]))
                    ch.link(dve.tensor_scalar(z[:, t, :], z[:, t, :], mv[:, t, 0:1], rstd[:, t:t + 1], ALU.subtract, ALU.mult))
                    ch.link(dve.tensor_tensor(z[:, t, :], z[:, t, :], ln_g[:, :], ALU.mult))
                    dve.tensor_tensor(x[:, t, :], z[:, t, :], ln_b[:, :], ALU.add).then_inc(x_ready, 1)

            def rope(src, dst, lo, half, cos, sin, tmp, view):
                a1, a2 = src[..., lo:lo + half], src[..., lo + half:lo + 2 * half]
                t = [view(x) for x in tmp]
                ch.hold()
                ch.step(dve.tensor_tensor(t[0], a1, cos, ALU.mult))
                ch.step(dve.tensor_tensor(t[1], a2, sin, ALU.mult))
                ch.step(dve.tensor_tensor(t[2], a2, cos, ALU.mult))
                ch.step(dve.tensor_tensor(t[3], a1, sin, ALU.mult))
                ch.hold()
                ch.step(dve.tensor_tensor(dst[..., lo:lo + half], t[0], t[1], ALU.subtract))
                return dve.tensor_tensor(dst[..., lo + half:lo + 2 * half], t[2], t[3], ALU.add)

            def router(l):
                xk = x[:, :, :].rearrange("q t (p k) -> q t k p", k=KD)
                for t in range(TT):
                    dve.wait_ge(x1_ready, 2 * l + t + 1)
                    dve.tensor_tensor(x_rest[:, t], xk[:, t], x_parts[0][:, t], ALU.subtract).then_inc(rest_ready, 1)
                for t in range(TT):
                    dve.wait_ge(x2_ready, 2 * l + t + 1)
                    ins = dve.tensor_tensor(x_parts[2][:, t], x_rest[:, t], x_parts[1][:, t], ALU.subtract)
                    ins.then_inc(x3_ready, 1)
                dve.wait_ge(logit_ps, l + 1)
                lg = PS[:, 4, 0:128].rearrange("p (t c) -> p t c", t=TT)
                ch.link(dve.memset(g_pad, -3e38))
                ch.link(dve.tensor_copy(g_pad[:, :, 0:GROUPS], lg[:, :, 0:GROUPS]))
                for t in range(TT):
                    ch.step(dve.max(mx[:, t, :], g_pad[:, t, :]))
                ch.hold()
                for t in range(TT):
                    ch.step(dve.max_index(mi[:, t, :], mx[:, t, :], g_pad[:, t, :]))
                dve.tensor_tensor(d4, g_pad[:, :, 0:GROUPS], mx[:, :, 0:1].broadcast_to((P, TT, GROUPS)), ALU.subtract)\
                   .then_inc(gdiff_ready, 1)
                ch.hold()
                ch.link(dve.tensor_copy(g_i, mi[:, :, 0:1]))
                slots4 = cst[:, C_EXP:C_EXP + GROUPS].unsqueeze(1).broadcast_to((P, TT, GROUPS))
                ch.link(dve.tensor_tensor(oh4, slots4, g_i.broadcast_to((P, TT, GROUPS)), ALU.is_equal))
                for t in range(TT):
                    ch.step(dve.tensor_tensor(e_prod[:, t], lg[:, t, GROUPS:GROUPS + EXPERTS].rearrange("p (g j) -> p j g", g=GROUPS),
                                              oh4[:, t].unsqueeze(1).broadcast_to((P, PER_GROUP, GROUPS)), ALU.mult))
                ch.hold()
                ch.link(dve.tensor_reduce(e_sel, e_prod, AX.X, ALU.add))
                for t in range(TT):
                    ch.step(dve.max(mx[:, t, :], e_sel[:, t, :]))
                ch.hold()
                for t in range(TT):
                    ch.step(dve.max_index(mi[:, t, :], mx[:, t, :], e_sel[:, t, :]))
                dve.tensor_tensor(e_d, mx[:, :, 1:2], mx[:, :, 0:1], ALU.subtract).then_inc(ediff_ready, 1)
                ch.step(dve.tensor_scalar(g_8, g_i, float(PER_GROUP), None, ALU.mult))
                ch.hold()
                ch.link(dve.tensor_copy(e_id, mi[:, :, 0:2]))
                ch.link(dve.tensor_tensor(e_id, e_id, g_8.broadcast_to((P, TT, 2)), ALU.add))
                numbers = cst[:, C_EXP:C_EXP + EXPERTS].unsqueeze(1).broadcast_to((P, TT, EXPERTS))
                ch.step(dve.tensor_tensor(cw, numbers, e_id[:, :, 0:1].broadcast_to((P, TT, EXPERTS)), ALU.is_equal))
                ch.link(dve.tensor_tensor(eq2, numbers, e_id[:, :, 1:2].broadcast_to((P, TT, EXPERTS)), ALU.is_equal))
                dve.tensor_tensor(mask, cw, eq2, ALU.add).then_inc(mask_ready, 1)
                dve.wait_ge(gexp_ready, l + 1)
                ch.link(dve.tensor_reduce(g_sum, d4, AX.X, ALU.add))
                ch.link(dve.reciprocal(g_p, g_sum.rearrange("p (t e) -> p t e", t=TT)))
                dve.wait_ge(eexp_ready, l + 1)
                ch.link(dve.tensor_scalar(den, e_x, 1.0, None, ALU.add))
                ch.link(dve.reciprocal(den, den))
                ch.link(dve.tensor_tensor(w_1, g_p, den, ALU.mult))
                ch.link(dve.tensor_tensor(w_2, w_1, e_x, ALU.mult))
                ch.step(dve.tensor_tensor(cw, cw, w_1.broadcast_to((P, TT, EXPERTS)), ALU.mult))
                ch.link(dve.tensor_tensor(eq2, eq2, w_2.broadcast_to((P, TT, EXPERTS)), ALU.mult))
                ch.link(dve.tensor_tensor(cw, cw, eq2, ALU.add))
                dve.wait_ge(rank_ps, l + 1)
                flat = lambda v: v.rearrange("p t e -> p (t e)")
                ch.step(dve.tensor_reduce(over_f[:, :], PS[:, 5, 64:96], AX.X, ALU.max))
                ch.link(dve.scalar_tensor_tensor(flat(rank), PS[:, 5, 0:64], 1.0, flat(mask), ALU.add, ALU.mult))
                ch.link(dve.tensor_scalar(flat(rank), flat(rank), -1.0, None, ALU.add))
                ch.link(dve.scalar_tensor_tensor(flat(cw_over), flat(rank), float(SLOTS), flat(cw), ALU.is_ge, ALU.mult))
                dve.tensor_scalar(over[:, :], over_f[0:1, :], float(SLOTS), None, ALU.is_gt).then_inc(route_ready, 1)
                dve.wait_ge(route_ready, l + 1)

            slot_no = cst[:, C_SLOT:C_SLOT + SLOTS].unsqueeze(1).broadcast_to((P, 2, SLOTS))

            def select(l, i, b):
                for t in range(TT):
                    rk = rank[:, t, bass.ds(2 * i, 2)].unsqueeze(2).broadcast_to((P, 2, SLOTS))
                    ch.step(dve.tensor_tensor(sel[b][:, t], slot_no, rk, ALU.is_equal))
                if isinstance(i, int) and i < 2:
                    dve.wait_ge(x3_ready, 2 * (l + 1))
                ch.hold()
                for t in range(TT):
                    wt = cw[:, t, bass.ds(2 * i, 2)].unsqueeze(2).broadcast_to((P, 2, SLOTS))
                    ins = dve.tensor_tensor(sel_w[b][:, t], sel[b][:, t], wt, ALU.mult)
                ins.then_inc(sel_ready, 1)

            def accumulate(l, q, first):
                for c in range(4):
                    t, h = c // 2, c % 2
                    dve.wait_ge(scat_ps, 4 * q + c + 1)
                    cut = y_acc[:, t, HALF * h:HALF * (h + 1)]
                    if first:
                        dve.tensor_copy(cut, PS[:, SCAT[c % 2], :]).then_inc(acc_done, 1)
                    else:
                        dve.tensor_tensor(cut, cut, PS[:, SCAT[c % 2], :], ALU.add).then_inc(acc_done, 1)

            def pair(l, i, b, first=False, second=False, tail=False):
                q = PAIRS * l + i
                dve.wait_ge(silu_ready, q + 1)
                dve.tensor_tensor(act_sb.rearrange("p (k f) -> p f k", k=KF), silu_sb.rearrange("p (f k) -> p f k", k=KF),
                                  PS[:, GU, FE:2 * FE].rearrange("p (f k) -> p f k", k=KF), ALU.mult).then_inc(act_ready, 1)
                dve.wait_ge(turn_ps, q + 1)
                dve.tensor_copy(turn[b], PS[:, TURN, 0:2 * P])
                ch.link(dve.tensor_copy(selT_hi[b][:, :], PS[:, TURN, 2 * P:4 * P]))
                dve.tensor_tensor(selT_lo[b][:, :], PS[:, TURN, 2 * P:4 * P], selT_hi[b][:, :].bitcast(F32), ALU.subtract)\
                   .then_inc(turn_sb, 1)
                if not first:
                    accumulate(l, q - 1, second)
                if not tail:
                    select(l, i + 2, b)
                for h in range(2):
                    dve.wait_ge(y_hi_ready, 2 * q + h + 1)
                    cut = slice(HALF * h, HALF * (h + 1))
                    dve.tensor_tensor(y_lo[:, cut], PS[:, DOWN[h], :], y_hi[:, cut].bitcast(F32), ALU.subtract)\
                       .then_inc(y_lo_ready, 1)

            def experts(l):
                select(l, 0, 0)
                select(l, 1, 1)
                pair(l, 0, 0, first=True)
                pair(l, 1, 1, second=True)
                with dve.Fori(1, PAIRS // 2 - 1) as j:
                    ch.enter(j - 1, 6)
                    for b in range(2):
                        pair(l, 2 * j + b, b)
                    ch.again()
                ch.leave(PAIRS // 2 - 2)
                pair(l, PAIRS - 2, 0, tail=True)
                pair(l, PAIRS - 1, 1, tail=True)
                accumulate(l, PAIRS * (l + 1) - 1, False)
                dve.wait_ge(acc_done, 4 * PAIRS * (l + 1))
                d = dense[l]
                flag = dve.value_load(over[0:1, 0:1])
                with dve.If(flag > 0):
                    with dve.Fori(0, EXPERTS) as e:
                        for t in range(TT):
                            n = 2 * e + t
                            dve.wait_ge(d["silu"], n + 1)
                            dve.scalar_tensor_tensor(act_sb.rearrange("p (k f) -> p f k", k=KF),
                                                     silu_sb.rearrange("p (f k) -> p f k", k=KF), cw_over[:, t, bass.ds(e, 1)],
                                                     PS[:, GU, FE:2 * FE].rearrange("p (f k) -> p f k", k=KF),
                                                     ALU.mult, ALU.mult).then_inc(d["act"], 1)
                            dve.wait_ge(d["turn"], n + 1)
                            dve.tensor_copy(turn[0][:, 0:2 * P], PS[:, TURN, 0:2 * P]).then_inc(d["turned"], 1)
                            dve.wait_ge(d["down"], n + 1)
                            for h in range(2):
                                cut = y_acc[:, t, HALF * h:HALF * (h + 1)]
                                dve.tensor_tensor(cut, cut, PS[:, DOWN[h], :], ALU.add).then_inc(d["added"], 1)
                    dve.wait_ge(d["added"], 4 * EXPERTS)

            dve.wait_ge(in_ld, 16 * IN_LOADS)
            dve.tensor_copy(pos_r, pos_i).then_inc(pos_rows, 1)
            dve.wait_ge(columns_ps, 1)
            ch.step(dve.tensor_copy(gains[:, :], PS[:, 7, 0:31]))
            ch.link(dve.tensor_copy(pos_f[:, :], PS[:, 7, 32:34]))
            tables = 0
            for trig, at, half, tmp in ((trig_m, C_INVM, ROPE // 2, M[:, 0:32]), (trig_r, C_INVR, DK // 2, M[:, 0:128])):
                n = tmp.shape[1]
                flat = [trig[:, u].rearrange("p t c -> p (t c)") for u in range(2)]
                ang, turns = M[:, 128:128 + n], M[:, 256:256 + n]
                for t in range(TT):
                    ch.step(dve.tensor_scalar(ang[:, half * t:half * (t + 1)], cst[:, at:at + half], pos_f[:, t:t + 1], None, ALU.mult))
                ch.hold()
                for u, quarter in ((0, 0.25), (1, 0.0)):
                    ch.link(dve.tensor_scalar(turns, ang, float(1 / TWO_PI), quarter, ALU.mult, ALU.add))
                    ch.link(dve.tensor_scalar(turns, turns, ROUND, None, ALU.add))
                    ch.link(dve.tensor_scalar(turns, turns, -ROUND, None, ALU.add))
                    ch.link(dve.scalar_tensor_tensor(tmp, turns, -PI_A, ang, ALU.mult, ALU.add))
                    ch.link(dve.scalar_tensor_tensor(tmp, turns, -PI_B, tmp, ALU.mult, ALU.add))
                    ch.link(dve.scalar_tensor_tensor(tmp, turns, -PI_C, tmp, ALU.mult, ALU.add))
                    ch.link(dve.tensor_scalar(tmp, tmp, float(quarter * TWO_PI), SIN_MAX, ALU.add, ALU.min))
                    dve.tensor_scalar(flat[u], tmp, -SIN_MAX, None, ALU.max).then_inc(angle_ready, 1)
                    tables += 1
                    dve.wait_ge(angle_ready, tables)
            dve.wait_ge(c_silu_ready, 1)
            for n in range(2 * KD):
                ada_sum(n)

            third(0, 4)
            third(1, 5)
            h_banks(0)
            for n in range(2 * KD, 3 * KD):
                ada_sum(n)
            for t in range(TT):
                dve.wait_ge(lowrank_ps, t + 1)
                dve.tensor_copy(low[:, t, :], PS[:, t, 0:LOWRANK]).then_inc(lowrank_sb, 1)
            ch.step(dve.memset(conv_u[:, :, 0:2], 0.0))
            dve.wait_ge(square_ready, TT)
            dve.wait_ge(act_chain, TT)
            sq = soft[:, 0:4].rearrange("p (t c) -> p t c", t=TT)
            ms = soft[:, 4:8].rearrange("p (t c) -> p t c", t=TT)
            dve.tensor_scalar(ms[:, :, 0:1], sq[:, :, 0:1], 1.0 / QR, RMS_EPS, ALU.mult, ALU.add).then_inc(ms_ready, 1)
            dve.tensor_scalar(ms[:, :, 1:2], sq[:, :, 1:2], 1.0 / KVR, RMS_EPS, ALU.mult, ALU.add).then_inc(ms_ready, 1)
            dve.wait_ge(rms_ready, 1)
            ch.link(dve.reciprocal(soft[:, 12:16], soft[:, 8:12]))
            for t in range(TT):
                ch.step(dve.tensor_scalar(low[:, t, 0:QR], low[:, t, 0:QR], soft[:, 12 + 2 * t:13 + 2 * t], None, ALU.mult))
                dve.tensor_scalar(low[:, t, QR:QR + KVR], low[:, t, QR:QR + KVR], soft[:, 13 + 2 * t:14 + 2 * t], None,
                                  ALU.mult).then_inc(lowrank_n, 1)
            third(2, 6)
            for n in range(3 * KD, 3 * KD + 8):
                ada_sum(n)
            dve.wait_ge(conv_x_sb, 2)
            for c in range(CT):
                dve.wait_ge(conv_ps, 3 + c // 2)
                ch.step(dve.tensor_tensor(conv_u[:, c, 2:], conv_x[:, c, :], PS[:, 4 + c // 2, 256 * (c % 2):256 * (c % 2) + 256], ALU.mult))
            ch.hold()
            for c in range(CT):
                ch.step(dve.tensor_scalar(yT0[:, c, :], conv_u[:, c, 0:SEQ], conv_w[:, 0, c:c + 1], None, ALU.mult))
            for j in (1, 2):
                ch.hold()
                for c in range(CT):
                    ch.step(dve.scalar_tensor_tensor(yT0[:, c, :], conv_u[:, c, j:SEQ + j], conv_w[:, j, c:c + 1], yT0[:, c, :],
                                                     ALU.mult, ALU.add))
            ch.hold()
            for c in range(CT):
                dve.wait_ge(conv_ps, 5 + c // 2)
                ins = dve.tensor_tensor(yT0[:, c, :], yT0[:, c, :], PS[:, 6 + c // 2, 256 * (c % 2):256 * (c % 2) + 256], ALU.mult)
            ins.then_inc(conv_done, 1)
            dve.wait_ge(lowT_ps, 1)
            for k in range(3):
                ins = dve.tensor_scalar(lowT[:, k, :], PS[:, k // 2, 256 * (k % 2):256 * (k % 2) + 256],
                                        q_g[:, k:k + 1] if k < 2 else kv_g[:, 0:1], None, ALU.mult)
            ins.then_inc(lowT_ready, 1)
            for n in range(3 * KD + 8, 3 * KD + 12):
                ada_sum(n)
            dve.wait_ge(trig_ready, 1)
            dve.wait_ge(up_q_sb, 4)
            for t in range(TT):
                bc = lambda v: v.unsqueeze(1).broadcast_to((P, HEADS, ROPE // 2))
                view = lambda v: v[:, 128 * t:128 * t + 128].rearrange("p (h c) -> p h c", h=HEADS)
                ins = rope(q_sb[:, t], q_sb[:, t], NOPE, ROPE // 2, bc(trig_m[:, 0, t]), bc(trig_m[:, 1, t]), rope_t, view)
                if t < TT - 1:
                    ch.step(ins)
            ins.then_inc(qk_ready, 1)
            dve.wait_ge(qk_ready, 1)
            ins = rope(low[:, :, QR + KVR:], low[:, :, QR + KVR:], 0, ROPE // 2, trig_m[:, 0], trig_m[:, 1], rope_t,
                       lambda v: v[:, 0:32].rearrange("p (t c) -> p t c", t=TT))
            ch.link(ins)
            dve.wait_ge(up_k_sb, 8)
            for t in range(TT):
                ins = dve.tensor_copy(k_sb[:, t, :, NOPE:], low[:, t, QR + KVR:].unsqueeze(1).broadcast_to((P, HEADS, ROPE)))
            ins.then_inc(qk_ready, 1)
            for n in range(8):
                dve.wait_ge(qkT_ps, n + 1)
                dst = (qT0, kT0)[n // 4][:, 2 * (n % 4):2 * (n % 4) + 2, :].rearrange("p h t -> p (h t)")
                dve.tensor_copy(dst, PS[0:QK, n, :]).then_inc(qkT_ready, 1)

            def softmax_shift(h):
                b = h % 2
                dve.wait_ge(score_ps, h + 1)
                if h >= 2:
                    dve.wait_ge(prob_ready, 2 * (h - 1))
                ch.link(dve.tensor_tensor(score[:, b, :], PS[:, b, 0:3 * P], cst[:, C_MASK:C_MASK + 3 * P], ALU.add))
                at = 64 + 2 * h
                ch.step(dve.tensor_reduce(soft[:, at:at + 1], score[:, b, 0:P], AX.X, ALU.max))
                ch.link(dve.tensor_reduce(soft[:, at + 1:at + 2], score[:, b, P:3 * P], AX.X, ALU.max))
                dve.tensor_scalar(soft[:, 16 + 2 * h:18 + 2 * h], soft[:, at:at + 2], -MLA_SCALE, None, ALU.mult).then_inc(shift_ready, 1)

            softmax_shift(0)
            for h in range(HEADS):
                b = h % 2
                if h + 1 < HEADS:
                    softmax_shift(h + 1)
                dve.wait_ge(probT_ps, h + 1)
                dve.tensor_copy(probT[:, b, :], PS[:, 2 + b, 0:3 * P]).then_inc(probT_ready, 1)
                ch.link(dve.reciprocal(soft[:, 96 + 2 * h:98 + 2 * h], soft[:, 32 + 2 * h:34 + 2 * h]))
                dve.wait_ge(head_ps, h + 1)
                for t in range(TT):
                    ins = dve.tensor_scalar(o_sb[:, t, HV * h:HV * (h + 1)], PS[:, 4 + b, HV * t:HV * (t + 1)],
                                            soft[:, 96 + 2 * h + t:97 + 2 * h + t], None, ALU.mult)
                ins.then_inc(head_sb, 1)
                for n in ([3 * KD + 12 + h] if h < 4 else [3 * KD + 8 + 2 * h, 3 * KD + 9 + 2 * h]):
                    ada_sum(n)
                if h in (1, 5):
                    third(3 + h // 4, 6 + h // 4)
            dve.wait_ge(oT_ps, 1)
            for k in range(4):
                ins = dve.tensor_copy(yT0[:, 4 + k, :], PS[:, 6 + k // 2, 256 * (k % 2):256 * (k % 2) + 256])
            ins.then_inc(oT_ready, 1)
            for n in range(6 * KD, 7 * KD):
                ada_sum(n)
            third(5, 4)
            for n in range(7 * KD, 8 * KD):
                ada_sum(n)
            third(6, 6)
            for n in range(8 * KD, 9 * KD):
                ada_sum(n)
            dve.wait_ge(y_ps, 2)
            layer_norm(0, lambda t, h: PS[:, 2 * t + h, :])

            third(7, 7)
            third(8, 4)
            h_banks(1)
            router(0)
            experts(0)
            layer_norm(1, lambda t, h: y_acc[:, t, HALF * h:HALF * (h + 1)])

            h_banks(2)
            dve.wait_ge(h_hi_ready, 1)
            dve.tensor_tensor(h_lo[:, :], hflat, h_hi[:, :].bitcast(F32), ALU.subtract).then_inc(h_lo_ready, 1)
            dve.wait_ge(h_lo_ready, 1)

            def split_lo(n):
                j = n - RET_PARTS
                dve.wait_ge(w_hi_ready, n + 1)
                dve.tensor_tensor(w_lo[n % 2][:, :], w_raw[n % 3] if j < 0 else w_raw_out[j % 4], w_hi[n % 2][:, :].bitcast(F32),
                                  ALU.subtract).then_inc(w_lo_ready, 1)

            def ret_rope(u):
                for t in range(TT):
                    dve.wait_ge(ret_sb, 4 * u + 2 + t + 1)
                    if u:
                        dve.wait_ge(retT_ps, 4)
                    cos, sin = (trig_r[:, v, t].unsqueeze(1).broadcast_to((P, RH, DK // 2)) for v in range(2))
                    if u or t:
                        dve.wait_ge(rope_ready, 2 * u + t)
                    ins = rope(raw1[:, t], turned1[:, t], 0, DK // 2, cos, sin, rope_r, lambda v: v)
                    ins.then_inc(rope_ready, 1)

            def ret_turned(u):
                for n in range(4):
                    dve.wait_ge(retT_ps, 4 * u + n + 1)
                    dve.tensor_copy(qkT1[u][:, 2 * n:2 * n + 2, :].rearrange("p h t -> p (h t)"), PS[:, 4 + n, :])\
                       .then_inc(retT_ready, 1)

            def decayed_scores(h):
                b = h % 2
                dve.wait_ge(rscore_ps, h + 1)
                if h >= 2:
                    dve.wait_ge(rhead_ps, h - 1)
                dve.tensor_tensor(sT1[:, b, 0:SEQ], PS[:, 4 + b, 0:SEQ], decay[:, h, :], ALU.mult)
                dve.tensor_tensor(sT1[:, b, SEQ:SEQ + P], PS[:, 4 + b, SEQ:SEQ + P], decay[:, h, 0:P], ALU.mult).then_inc(decayed, 1)

            def head_stats(h):
                dve.wait_ge(rhead_sb, 2 * (h + 1))
                for t in range(TT):
                    ch.step(dve.bn_stats(rstat[:, t, h, :], o1[:, t, DV * h:DV * (h + 1)]))

            split_lo(0)
            split_lo(1)
            late = LATE
            for c in range(RET_CHUNKS):
                for n in (2 * c + 2, 2 * c + 3):
                    if n < RET_PARTS:
                        split_lo(n)
                if c == 1:
                    ret_rope(0)
                if c == 3:
                    ret_turned(0)
                    ret_rope(1)
                if c == 5:
                    ret_turned(1)
                    dve.wait_ge(decay_ld, 16)
                for _ in range(LATE_AT.get(c, 0)):
                    ada_sum(late)
                    late += 1
                if c == 7:
                    third(9, 4)
                    third(10, 5)
                if 7 <= c < 11:
                    decayed_scores(2 * (c - 7))
                    decayed_scores(2 * (c - 7) + 1)
                if c >= 9:
                    head_stats(2 * (c - 9))
                    head_stats(2 * (c - 9) + 1)
            head_stats(RH - 2)
            third(11, 4)
            dve.wait_ge(rhead_sb, 2 * RH)
            for t in range(TT):
                ch.step(dve.bn_stats(rstat[:, t, RH - 1, :], o1[:, t, DV * (RH - 1):]))
            ch.hold()
            for t in range(TT):
                for h in range(RH):
                    ch.step(dve.bn_aggr(rmv[:, t, h, :], rstat[:, t, h, :]))
            ch.hold()
            dve.tensor_scalar(rsd, rmv[:, :, :, 1], LN_EPS, None, ALU.add).then_inc(rvar_ready, 1)
            dve.wait_ge(rstd_ready, 1)
            ch.link(dve.reciprocal(rrs, rsd))
            dve.wait_ge(ret_sb, 2 * RET_CHUNKS)
            for t in range(TT):
                for h in range(RH):
                    o = o1[:, t, DV * h:DV * (h + 1)]
                    ch.step(dve.tensor_scalar(o, o, rmv[:, t, h, 0:1], rrs[:, t, h:h + 1], ALU.subtract, ALU.mult))
            ch.hold()
            for t in range(TT):
                ins = dve.tensor_tensor(o1[:, t, :], o1[:, t, :], g1[:, t, :], ALU.mult)
            ins.then_inc(ret_y, 1)
            split_lo(RET_PARTS)
            split_lo(RET_PARTS + 1)
            for n in range(OUT_PARTS):
                for k in (2 * n, 2 * n + 1):
                    dve.wait_ge(ryT_hi, 2 * n + 2)
                    dve.scalar_tensor_tensor(yT_lo[:, SEQ * k:SEQ * (k + 1)], PS[:, 4 + n % 4, 256 * (k % 2):256 * (k % 2) + 256],
                                             gn_g[:, k:k + 1], yT_hi[:, SEQ * k:SEQ * (k + 1)].bitcast(F32), ALU.mult, ALU.subtract)\
                       .then_inc(ryT_lo, 1)
            for j in range(2, OUT_PARTS):
                split_lo(RET_PARTS + j)
            dve.wait_ge(y_ps, 4)
            layer_norm(2, lambda t, h: PS[:, 2 * t + h, :])

            h_banks(3)
            router(1)
            experts(1)
            layer_norm(3, lambda t, h: y_acc[:, t, HALF * h:HALF * (h + 1)])


_INS = ['x', 'c', 'positions', 'ada_mix_w', 'ada_mix_b', 'ln_mix_g', 'ln_mix_b',
        'ab_w_in', 'ab_conv_w', 'ab_q_norm_g', 'ab_kv_norm_g', 'ab_w_uq', 'ab_w_ukv', 'ab_w_out',
        'ret_w_in', 'ret_gn_g', 'ret_w_out', 'ada_ffn_w', 'ada_ffn_b', 'ln_ffn_g', 'ln_ffn_b',
        'moe_rg_w', 'moe_rg_b', 'moe_re_w', 'moe_re_b', 'moe_w_gate', 'moe_w_up', 'moe_w_down']


def kernel(**inputs):
    import concourse.bacc as bacc
    from concourse.bass_utils import run_bass_kernel_spmd

    nc = bacc.Bacc("TRN2", target_bir_lowering=False, num_devices=1)
    arrays = {name: np.ascontiguousarray(inputs[name]) for name in _INS}
    arrays["table"], arrays["decay"] = shape_constants()
    aps = {name: nc.dram_tensor(f"in_{name}", v.shape, mybir.dt.from_np(v.dtype), kind="ExternalInput").ap()
           for name, v in arrays.items()}
    out = nc.dram_tensor("out_0", (1, SEQ, D), F32, kind="ExternalOutput").ap()
    build(nc, aps, out)
    got = run_bass_kernel_spmd(nc, [{f"in_{name}": v for name, v in arrays.items()}], core_ids=[0])
    return got.results[0]["out_0"]
```

```python
from contextlib import ExitStack

import numpy as np

import concourse.bass as bass
from concourse import mybir

ALU = mybir.AluOpType
ACT = mybir.ActivationFunctionType
AX = mybir.AxisListType
F32 = mybir.dt.float32
I32 = mybir.dt.int32
U32 = mybir.dt.uint32
F32R = mybir.dt.float32r
BF16 = mybir.dt.bfloat16

P = 128
D = 1024
SEQ = 256
TT = SEQ // P
KD = D // P
DEPTH = 2
SUBLAYERS = 2 * DEPTH
ALPHA = float(2 * DEPTH) ** 0.25
LN_EPS, RMS_EPS = 1e-5, 1e-6
HALF = 512

CONV = 512
CT = CONV // P
QR, KVR, ROPE, NOPE, HV, HEADS = 256, 128, 32, 64, 64, 8
LOWRANK = QR + KVR + ROPE
QK = NOPE + ROPE
MLA_SCALE = float(QK) ** -0.5

RH, DK, DV = 8, 128, 256
RQ = RH * DK
RV = RH * DV
RET_CHUNKS = (2 * RQ + 2 * RV) // HALF
RET_PARTS = 2 * RET_CHUNKS
OUT_PARTS = RV // P // 2
RAW_PARTS = RET_PARTS + 3

THIRDS = 3 * SUBLAYERS
BLOCKS = KD * THIRDS
LATE_M = 8
LATE = KD * LATE_M
RING = 4
WITH_HEAD = 3
LATE_AT = (3, 3, 2, 3, 3, 3, 3, 3, 3, 3, 2, 1)

GROUPS, PER_GROUP = 4, 8
EXPERTS = GROUPS * PER_GROUP
FE = 256
KF = FE // P
SLOTS = 64
PAIRS = EXPERTS // 2

SHARED = [n for n in range(3 * KD + WITH_HEAD - 1, 3 * KD + WITH_HEAD * HEADS, WITH_HEAD) if n % KD]

C_ID, C_ONE, C_UP, C_MASK = 0, 128, 256, 384
C_SLOT = 768
C_EXP = C_SLOT + SLOTS
C_INVM = C_EXP + EXPERTS
C_INVR = C_INVM + ROPE // 2
C_N = C_INVR + DK // 2

TWO_PI = 2 * np.pi
PI_A = float(np.float32(6.28125))
PI_B = float(np.float32(np.float64(TWO_PI) - 6.28125))
PI_C = float(np.float32(TWO_PI - 6.28125 - np.float64(np.float32(TWO_PI - 6.28125))))
ROUND = float(1.5 * 2 ** 23)
SIN_MAX = 3.1415925


def shape_constants():
    t = np.zeros((P, C_N), np.float32)
    t[:, C_ID:C_ID + P] = np.eye(P)
    t[:, C_ONE:C_ONE + P] = 1.0
    t[:, C_UP:C_UP + P] = np.triu(np.ones((P, P)), 1)
    causal = np.where(np.arange(P)[None, :] <= np.arange(P)[:, None], 0.0, -1e30)
    t[:, C_MASK:C_MASK + P] = causal
    t[:, C_MASK + 2 * P:C_MASK + 3 * P] = causal
    t[:, C_SLOT:C_SLOT + SLOTS] = np.arange(SLOTS)
    t[:, C_EXP:C_EXP + EXPERTS] = np.arange(EXPERTS)
    for at, dim in ((C_INVM, ROPE), (C_INVR, DK)):
        inv = np.float32(10000.0) ** (-np.arange(0, dim, 2, dtype=np.float32) / np.float32(dim))
        t[:, at:at + dim // 2] = inv
    lg = np.log1p(-np.exp2(-5.0 - np.arange(RH)))
    lag = np.arange(SEQ)[None, :] - np.arange(P)[:, None]
    decay = np.where(lag[:, None, :] >= 0, np.exp(lg[None, :, None] * np.maximum(lag, 0)[:, None, :]), 0.0)
    decay = decay * DK ** -0.5
    return t, np.ascontiguousarray(decay.astype(np.float32).reshape(P, RH * SEQ))


class Chain:

    def __init__(self, eng, sem):
        self.eng, self.sem, self.n, self.moving = eng, sem, 0, None

    def value(self):
        return self.n if self.moving is None else self.moving + self.n

    def step(self, ins):
        self.n += 1
        ins.then_inc(self.sem, 1)

    def hold(self):
        self.eng.wait_ge(self.sem, self.value())

    def link(self, ins):
        self.step(ins)
        self.hold()

    def enter(self, i, per):
        self.before, self.per = self.n, per
        self.moving, self.n = self.before + per * i, 0

    def again(self):
        assert self.n == self.per, (self.n, self.per)

    def leave(self, times):
        self.moving, self.n = None, self.before + self.per * times


def build(nc, a, out):
    ctx = ExitStack()
    with ctx:
        def sb(name, shape, dt=F32):
            return ctx.enter_context(nc.sbuf_tensor(name, shape, dt))

        def sem(name):
            return ctx.enter_context(nc.semaphore(name))

        W = sb("W", [P, 24576])
        w_end = nc.sbuf_base
        M = sb("M", [P, 16384])
        m_end = nc.sbuf_base

        def rounded(name, arena, at, width):
            end, words = (w_end, 24576) if arena == "W" else (m_end, 16384)
            return nc.alloc_sbuf_tensor_at(name, [P, width], F32R, offset=end - 4 * (words - at))

        x = sb("x", [P, TT, D])
        hT = sb("hT", [P, KD, SEQ])
        gates = sb("gates", [P, SUBLAYERS, D])
        ln_g = sb("ln_g", [P, D])
        ln_b = sb("ln_b", [P, D])
        cst = sb("cst", [P, C_N])
        router_w = sb("router_w", [P, KD, GROUPS + EXPERTS])
        router_b = sb("router_b", [GROUPS + EXPERTS, 1])
        gains = sb("gains", [P, 31])
        gn_g, q_g, kv_g = gains[:, 0:16], gains[:, 16:18], gains[:, 18:19]
        conv_w = gains[:, 19:31].rearrange("p (j c) -> p j c", j=3)
        gain_rows = M[0:31, 0:P]
        pos_i = M[0:TT, P:2 * P].bitcast(I32)
        pos_r = M[0:TT, 2 * P:3 * P]
        bias_c = sb("bias_c", [P, SUBLAYERS, 2, KD])
        mod_c = sb("mod_c", [P, SUBLAYERS, 2, KD])
        ln_c = sb("ln_c", [P, SUBLAYERS, 2, KD])
        c_in = sb("c_in", [P, KD])
        c_silu = sb("c_silu", [P, KD])
        pos_f = sb("pos_f", [P, TT])
        trig_m = sb("trig_m", [P, 2, TT, ROPE // 2])
        trig_r = sb("trig_r", [P, 2, TT, DK // 2])
        shift_add = sb("shift_add", [P, KD])
        stats = sb("stats", [P, TT, 2, 6])
        mv = sb("mv", [P, TT, 2])
        rvar = sb("rvar", [P, TT])
        rstd = sb("rstd", [P, TT])
        over = sb("over", [1, 1], I32)
        over_f = sb("over_f", [P, 1])
        PS = ctx.enter_context(nc.psum_tensor("PS", [P, 8, HALF], F32))

        ident = cst[:, C_ID:C_ID + P]
        ones = cst[:, C_ONE:C_ONE + P]
        upper = cst[:, C_UP:C_UP + P]
        hflat = hT[:, :, :].rearrange("p k t -> p (k t)")

        def ada_buf(n):
            at = 10240 + D * (n % RING) if n < LATE else 22528 + D * (n % 2)
            return (M if n < LATE else W)[:, at:at + D]

        def ada_acc(m):
            return M[:, 14336 + D * (m % 2):14336 + D * (m % 2 + 1)] if m < LATE_M else hflat[:, D * (m % 2):D * (m % 2 + 1)]

        y_acc = M[:, 0:2048].rearrange("p (t d) -> p t d", t=TT)

        c_ld = sem("c_ld")
        in_ld = sem("in_ld")
        small_ld = sem("small_ld")
        pos_rows = sem("pos_rows")
        columns_ps = sem("columns_ps")
        columns_sb = sem("columns_sb")
        ada_ld = [sem(f"ada_ld{j}") for j in range(RING)]
        late_ld = [sem(f"late_ld{j}") for j in range(2)]
        c_silu_ready = sem("c_silu_ready")
        ada_used = sem("ada_used")
        ada_scaled = sem("ada_scaled")
        ln_ld = sem("ln_ld")
        third_ps = sem("third_ps")
        third_ready = sem("third_ready")
        xT_ps = sem("xT_ps")
        hT_even = sem("hT_even")
        hT_odd = sem("hT_odd")
        var_ready = sem("var_ready")
        rstd_made = sem("rstd_made")
        x_full = sem("x_full")
        pool_chain = sem("pool_chain")
        x_ready = sem("x_ready")
        y_ps = sem("y_ps")
        dve_chain = sem("dve_chain")
        act_chain = sem("act_chain")
        angle_ready = sem("angle_ready")
        trig_ready = sem("trig_ready")
        lowrank_ld = sem("lowrank_ld")
        convw_ld = [sem(f"conv_ld{j}") for j in range(3)]
        upw_ld = sem("upw_ld")
        out_ld = sem("out_ld")
        lowrank_ps = sem("lowrank_ps")
        lowrank_sb = sem("lowrank_sb")
        square_ready = sem("square_ready")
        ms_ready = sem("ms_ready")
        rms_ready = sem("rms_ready")
        lowrank_n = sem("lowrank_n")
        lowT_ps = sem("lowT_ps")
        lowT_ready = sem("lowT_ready")
        conv_ps = sem("conv_ps")
        conv_x_sb = sem("conv_x_sb")
        conv_used = sem("conv_used")
        up_ps = sem("up_ps")
        up_q_sb = sem("up_q_sb")
        up_k_sb = sem("up_k_sb")
        qk_ready = sem("qk_ready")
        qkT_ps = sem("qkT_ps")
        qT_ready = sem("qT_ready")
        kT_ready = sem("kT_ready")
        score_ps = sem("score_ps")
        shift_ready = sem("shift_ready")
        prob_ready = sem("prob_ready")
        probT_ps = sem("probT_ps")
        probT_ready = sem("probT_ready")
        head_ps = sem("head_ps")
        head_sb = sem("head_sb")
        psum_inv = sem("psum_inv")
        oT_ps = sem("oT_ps")
        oT_ready = sem("oT_ready")
        ret_ld = [sem(f"ret_ld{j}") for j in range(3)]
        ret_out_ld = [sem(f"ret_out_ld{j}") for j in range(4)]
        h_hi_ready = sem("h_hi_ready")
        h_lo_ready = sem("h_lo_ready")
        w_hi_ready = sem("w_hi_ready")
        w_lo_ready = sem("w_lo_ready")
        part_used = sem("part_used")
        decay_ld = sem("decay_ld")
        ret_ps = sem("ret_ps")
        ret_sb = sem("ret_sb")
        rope_ready = sem("rope_ready")
        retT_ps = sem("retT_ps")
        retT_ready = sem("retT_ready")
        rscore_ps = sem("rscore_ps")
        decayed = sem("decayed")
        rhead_ps = sem("rhead_ps")
        rhead_sb = sem("rhead_sb")
        rvar_ready = sem("rvar_ready")
        rstd_ready = sem("rstd_ready")
        ret_y = sem("ret_y")
        ryT_ps = sem("ryT_ps")
        ryT_hi = sem("ryT_hi")
        ryT_lo = sem("ryT_lo")
        rw_ld = sem("rw_ld")
        x1_ready = sem("x1_ready")
        rest_ready = sem("rest_ready")
        x2_ready = sem("x2_ready")
        x3_ready = sem("x3_ready")
        logitT_ps = sem("logitT_ps")
        logitT_sb = sem("logitT_sb")
        logit_ps = sem("logit_ps")
        gdiff_ready = sem("gdiff_ready")
        gexp_ready = sem("gexp_ready")
        ediff_ready = sem("ediff_ready")
        eexp_ready = sem("eexp_ready")
        mask_ready = sem("mask_ready")
        rank_ps = sem("rank_ps")
        route_ready = sem("route_ready")
        gu_ld = [sem("gu_ld0"), sem("gu_ld1")]
        down_ld = [sem("down_ld0"), sem("down_ld1")]
        sel_ready = sem("sel_ready")
        gath_ps = sem("gath_ps")
        gath_sb = sem("gath_sb")
        gu_ps = sem("gu_ps")
        silu_ready = sem("silu_ready")
        act_ready = sem("act_ready")
        turn_ps = sem("turn_ps")
        turn_sb = sem("turn_sb")
        down_ps = sem("down_ps")
        y_hi_ready = sem("y_hi_ready")
        y_lo_ready = sem("y_lo_ready")
        scat_ps = sem("scat_ps")
        acc_done = sem("acc_done")
        ahead_ready = sem("ahead_ready")
        dense = [{n: sem(f"dense{l}_{n}") for n in
                  ("ld", "gu", "silu", "act", "turn", "turned", "down", "gated", "added", "stats")} for l in range(DEPTH)]
        out_st = sem("out_st")

        block = ctx.enter_context(nc.Block())
        rows8 = lambda w: w.rearrange("(p k) n -> p k n", k=KD)

        w_ukv = W[:, 0:1024]
        w_uq = W[:, 1024:2560].rearrange("p (k n) -> p k n", k=QR // P)
        w_low = W[:, 2560:2560 + KD * LOWRANK].rearrange("p (k n) -> p k n", k=KD)
        q_sb = W[:, 5888:7424].rearrange("p (t h c) -> p t h c", t=TT, h=HEADS)
        k_sb = W[:, 7424:8960].rearrange("p (t h c) -> p t h c", t=TT, h=HEADS)
        v_sb = W[:, 8960:9984].rearrange("p (t h c) -> p t h c", t=TT, h=HEADS)
        kT0 = W[0:QK, 9984:12032].rearrange("p (h t) -> p h t", h=HEADS)
        o_sb = W[:, 0:1024].rearrange("p (t c) -> p t c", t=TT)
        rope_t = [W[:, 1024 + 256 * j:1280 + 256 * j] for j in range(4)]
        qT0 = W[0:QK, 2048:4096].rearrange("p (h t) -> p h t", h=HEADS)
        prob = W[:, 4096:4864].rearrange("p (b c) -> p b c", b=2)
        score = W[:, 4864:5632].rearrange("p (b c) -> p b c", b=2)
        w_conv = [W[:, at:at + 4096].rearrange("p (k n) -> p k n", k=KD) for at in (20480, 12288, 16384)]
        w_out0 = [M[:, 7168:10240].rearrange("p (k n) -> p k n", k=3), W[:, 20480:24576].rearrange("p (k n) -> p k n", k=4),
                  M[:, 832:1856].rearrange("p (k n) -> p k n", k=1)]
        w_out0 = [w_out0[j][:, k, :] for j, k in ((0, 0), (0, 1), (0, 2), (1, 0), (1, 1), (1, 2), (1, 3), (2, 0))]
        low = M[:, 0:832].rearrange("p (t c) -> p t c", t=TT)
        conv_x = M[:, 832:1856].rearrange("p (c t) -> p c t", c=CT)
        conv_u = M[:, 1856:1856 + CT * (SEQ + 2)].rearrange("p (c t) -> p c t", c=CT)
        yT0 = M[:, 2888:4936].rearrange("p (k t) -> p k t", k=KD)
        lowT = M[:, 4936:5704].rearrange("p (k t) -> p k t", k=3)
        probT = M[:, 5704:6472].rearrange("p (b c) -> p b c", b=2)
        soft = M[:, 6472:6600]
        low_sq = M[:, 6600:6856]

        mixed = {0: hflat[:, 0:D], 2: M[:, 12288:12288 + D]}
        w_raw = [W[:, 12288 + 2048 * j:14336 + 2048 * j] for j in range(3)]
        w_raw_out = [M[:, 2048 * j:2048 * (j + 1)] for j in range(4)]
        def part_raw(n):
            if n < RAW_PARTS:
                return w_raw[n % 3], ret_ld[n % 3], 16 * (n // 3 + 1)
            j = n - RAW_PARTS
            return w_raw_out[j % 4], ret_out_ld[j % 4], 16 * (j // 4 + 1)

        w_hi = [rounded(f"w_hi{j}", "W", 4096 * j, 2048) for j in range(2)]
        w_lo = [rounded(f"w_lo{j}", "W", 4096 * j + 2048, 2048) for j in range(2)]
        h_hi = rounded("h_hi", "W", 18432, 2048)
        h_lo = rounded("h_lo", "W", 20480, 2048)
        decay = W[:, 8192:10240].rearrange("p (h t) -> p h t", h=RH)
        rope_r = [W[:, 10240 + 512 * j:10752 + 512 * j].rearrange("p (h c) -> p h c", h=RH) for j in range(4)]
        v1 = M[:, 0:4096].rearrange("p (t c) -> p t c", t=TT)
        g1 = M[:, 4096:8192].rearrange("p (t c) -> p t c", t=TT)
        qkT1 = [M[:, 8192 + 2048 * j:10240 + 2048 * j].rearrange("p (h t) -> p h t", h=RH) for j in range(2)]
        raw1 = M[:, 12288:14336].rearrange("p (t h c) -> p t h c", t=TT, h=RH)
        turned1 = M[:, 14336:16384].rearrange("p (t h c) -> p t h c", t=TT, h=RH)
        o1 = M[:, 12288:16384].rearrange("p (t c) -> p t c", t=TT)
        yT_hi = rounded("yT_hi", "M", 8192, 4096)
        yT_lo = rounded("yT_lo", "W", 8192, 4096)
        sT1 = W[:, 10240:11008].rearrange("p (b c) -> p b c", b=2)
        rstat = W[:, 11008:11104].rearrange("p (t h c) -> p t h c", t=TT, h=RH)
        rmv = W[:, 11104:11136].rearrange("p (t h c) -> p t h c", t=TT, h=RH)
        rsd = W[:, 11136:11152].rearrange("p (t h) -> p t h", t=TT)
        rrs = W[:, 11152:11168].rearrange("p (t h) -> p t h", t=TT)

        w_gu = [W[:, 12288 - 12288 * b:20480 - 12288 * b].rearrange("p (u e k f) -> p u e k f", u=2, e=2, k=KD) for b in range(2)]
        w_down = [W[:, 20480 - 12288 * b:24576 - 12288 * b].rearrange("p (e k n) -> p e k n", e=2, k=KF) for b in range(2)]
        logitT = M[0:GROUPS + EXPERTS, 2048:2048 + SEQ]
        xselT = M[:, 2048:3072].rearrange("p (k s) -> p k s", k=KD)
        y_hi = rounded("y_hi", "M", 3072, D)
        y_lo = rounded("y_lo", "M", 4096, D)
        selT_hi = [rounded(f"selT_hi{b}", "M", 5120 + SEQ * b, SEQ) for b in range(2)]
        selT_lo = [rounded(f"selT_lo{b}", "M", 5632 + SEQ * b, SEQ) for b in range(2)]
        sel_w = [M[:, 6144 + 256 * b:6400 + 256 * b].rearrange("p (t e s) -> p t e s", t=TT, e=2) for b in range(2)]
        sel = [M[:, 6656 + 128 * b:6784 + 128 * b].bitcast(BF16).rearrange("p (t e s) -> p t e s", t=TT, e=2)
               for b in range(2)]
        turn = [M[:, 6912 + 256 * b:7168 + 256 * b] for b in range(2)]
        silu_sb = M[:, 7424:7680]
        act_sb = M[:, 7680:7936]
        r = M[:, 7936:8448]
        x_parts = [M[:, 8448 + 1024 * j:9472 + 1024 * j].bitcast(BF16).rearrange("p (t k q) -> p t k q", t=TT, k=KD)
                   for j in range(3)]
        gated = [M[:, 8448 + HALF * c:8448 + HALF * (c + 1)] for c in range(4)]
        x_rest = y_acc.rearrange("p t (k q) -> p t k q", k=KD)
        rank = r[:, 0:64].rearrange("p (t e) -> p t e", t=TT)
        cw = r[:, 64:128].rearrange("p (t e) -> p t e", t=TT)
        cw_over = r[:, 128:192].rearrange("p (t e) -> p t e", t=TT)
        mask = r[:, 192:256].rearrange("p (t e) -> p t e", t=TT)
        eq2 = r[:, 256:320].rearrange("p (t e) -> p t e", t=TT)
        g_pad = r[:, 320:336].rearrange("p (t e) -> p t e", t=TT)
        mx = r[:, 336:352].rearrange("p (t e) -> p t e", t=TT)
        mi = r[:, 352:368].bitcast(U32).rearrange("p (t e) -> p t e", t=TT)
        d4 = r[:, 368:376].rearrange("p (t e) -> p t e", t=TT)
        oh4 = r[:, 376:384].rearrange("p (t e) -> p t e", t=TT)
        e_sel = r[:, 384:400].rearrange("p (t e) -> p t e", t=TT)
        e_prod = r[:, 400:464].rearrange("p (t j g) -> p t j g", t=TT, j=PER_GROUP)
        g_sum = r[:, 464:466]
        g_p = r[:, 466:468].rearrange("p (t e) -> p t e", t=TT)
        g_i = r[:, 468:470].rearrange("p (t e) -> p t e", t=TT)
        g_8 = r[:, 470:472].rearrange("p (t e) -> p t e", t=TT)
        e_d = r[:, 472:474].rearrange("p (t e) -> p t e", t=TT)
        e_x = r[:, 474:476].rearrange("p (t e) -> p t e", t=TT)
        w_1 = r[:, 476:478].rearrange("p (t e) -> p t e", t=TT)
        w_2 = r[:, 478:480].rearrange("p (t e) -> p t e", t=TT)
        e_id = r[:, 480:484].rearrange("p (t e) -> p t e", t=TT)
        den = r[:, 484:486].rearrange("p (t e) -> p t e", t=TT)
        GATH, GU, DOWN, SCAT, TURN = (0, 1), 2, (3, 4), (5, 6), 7

        ada_w = [a["ada_mix_w"][0], a["ada_ffn_w"][0], a["ada_mix_w"][1], a["ada_ffn_w"][1]]
        ada_b = [a["ada_mix_b"][0], a["ada_ffn_b"][0], a["ada_mix_b"][1], a["ada_ffn_b"][1]]
        lng_d = [a["ln_mix_g"][0], a["ln_ffn_g"][0], a["ln_mix_g"][1], a["ln_ffn_g"][1]]
        lnb_d = [a["ln_mix_b"][0], a["ln_ffn_b"][0], a["ln_mix_b"][1], a["ln_ffn_b"][1]]
        wg_d = a["moe_w_gate"].rearrange("l e (p k) f -> (l e) p (k f)", k=KD)
        wu_d = a["moe_w_up"].rearrange("l e (p k) f -> (l e) p (k f)", k=KD)
        wd_d = a["moe_w_down"].rearrange("l e (p k) n -> (l e) p (k n)", k=KF)
        SMALL_LOADS = 5 + 4 * SUBLAYERS

        @block.sync
        def _(sp):
            def load_ada(n):
                ring, early = (RING, 0) if n < LATE else (2, LATE)
                if n - early >= ring:
                    sp.wait_ge(ada_used, n - ring + 1)
                s, u, k = n // KD // 3, n // KD % 3, n % KD
                ld = ada_ld[n % RING] if n < LATE else late_ld[n % 2]
                sp.dma_start(ada_buf(n), rows8(ada_w[s])[:, k, D * u:D * (u + 1)]).then_inc(ld, 16)

            def load_ln(s):
                if s:
                    sp.wait_ge(x_full, 2 * s)
                sp.dma_start(ln_g[:, :], lng_d[s].partition_broadcast(P)).then_inc(ln_ld, 16)
                sp.dma_start(ln_b[:, :], lnb_d[s].partition_broadcast(P)).then_inc(ln_ld, 16)

            def load_gate_up(l, i, b, u):
                pair = bass.ds(EXPERTS * l + 2 * i, 2)
                sp.dma_start(w_gu[b][:, u], (wg_d, wu_d)[u][pair].rearrange("e p n -> p e n")).then_inc(gu_ld[b], 16)

            def load_down(l, i, b):
                pair = bass.ds(EXPERTS * l + 2 * i, 2)
                sp.dma_start(w_down[b], wd_d[pair].rearrange("e p n -> p e n")).then_inc(down_ld[b], 16)

            def load_experts(l, i, b):
                q = PAIRS * l + i
                sp.wait_ge(gu_ps, q - 1)
                load_gate_up(l, i, b, 0)
                load_gate_up(l, i, b, 1)
                sp.wait_ge(down_ps, 2 * (q - 1))
                load_down(l, i, b)

            def load_router(l):
                if l:
                    sp.wait_ge(logit_ps, l)
                sp.dma_start(router_w[:, :, 0:GROUPS], rows8(a["moe_rg_w"][l])).then_inc(rw_ld, 16)
                sp.dma_start(router_w[:, :, GROUPS:], rows8(a["moe_re_w"][l])).then_inc(rw_ld, 16)
                sp.dma_start(router_b[0:GROUPS, :], a["moe_rg_b"][l].unsqueeze(1)).then_inc(rw_ld, 16)
                sp.dma_start(router_b[GROUPS:, :], a["moe_re_b"][l].unsqueeze(1)).then_inc(rw_ld, 16)

            def dense_loads(l):
                d = dense[l]
                sp.wait_ge(route_ready, l + 1)
                sp.wait_ge(down_ps, 2 * PAIRS * (l + 1))
                flag = sp.value_load(over[0:1, 0:1])
                with sp.If(flag > 0):
                    def load(e):
                        one = bass.ds(e + EXPERTS * l, 1)
                        sp.dma_start(w_gu[1][:, 0, 0:1], wg_d[one].rearrange("e p n -> p e n")).then_inc(d["ld"], 16)
                        sp.dma_start(w_gu[1][:, 1, 0:1], wu_d[one].rearrange("e p n -> p e n")).then_inc(d["ld"], 16)
                        sp.dma_start(w_down[1][:, 0:1], wd_d[one].rearrange("e p n -> p e n")).then_inc(d["ld"], 16)

                    load(0)
                    with sp.Fori(1, EXPERTS) as e:
                        sp.wait_ge(d["added"], 4 * e)
                        load(e)
                    sp.wait_ge(d["added"], 4 * EXPERTS)

            sp.dma_start(c_in[:, :], a["c"][0].rearrange("(p k) -> p k", k=KD)).then_inc(c_ld, 16)
            for n in range(RING):
                load_ada(n)
            sp.dma_start(cst[:, :], a["table"]).then_inc(in_ld, 16)
            sp.dma_start(x[:, :, :], a["x"][0].rearrange("(t p) d -> p t d", p=P)).then_inc(in_ld, 16)
            for dst, src in (
                (pos_i, a["positions"][0].rearrange("(t p) -> t p", p=P)),
                (gain_rows[0:16, :], a["ret_gn_g"][0].rearrange("(k p) -> k p", p=P)),
                (gain_rows[16:18, :], a["ab_q_norm_g"][0].rearrange("(k p) -> k p", p=P)),
                (gain_rows[18:19, :], a["ab_kv_norm_g"][0].rearrange("(k p) -> k p", p=P)),
                (gain_rows[19:31, :], a["ab_conv_w"][0].rearrange("j (c p) -> (j c) p", p=P)),
            ):
                sp.dma_start(dst, src).then_inc(small_ld, 16)
            for s in range(SUBLAYERS):
                sp.dma_start(bias_c[:, s, :, :],
                             ada_b[s][0:2 * D].rearrange("(u p k) -> p u k", u=2, k=KD)).then_inc(small_ld, 16)
                sp.dma_start(gates[0:1, s, :], ada_b[s][2 * D:3 * D].unsqueeze(0)).then_inc(small_ld, 16)
                for u, src in enumerate((lng_d[s], lnb_d[s])):
                    sp.dma_start(ln_c[:, s, u, :], src.rearrange("(p k) -> p k", k=KD)).then_inc(small_ld, 16)
            for n in range(RING, 2 * KD):
                load_ada(n)
            w_in = rows8(a["ab_w_in"][0])

            def load_conv(j):
                at = CONV * (0, 2, 1)[j]
                sp.dma_start(w_conv[j], w_in[:, :, at:at + CONV]).then_inc(convw_ld[j], 16)

            sp.dma_start(w_low, w_in[:, :, 3 * CONV:]).then_inc(lowrank_ld, 16)
            load_conv(0)
            sp.dma_start(w_uq, a["ab_w_uq"][0].rearrange("(k p) n -> p k n", p=P)).then_inc(upw_ld, 16)
            sp.dma_start(w_ukv, a["ab_w_ukv"][0]).then_inc(upw_ld, 16)
            load_conv(1)
            load_conv(2)
            w_o = a["ab_w_out"][0].rearrange("(k p) n -> p k n", p=P)
            for n in range(2 * KD, 3 * KD):
                load_ada(n)
            sp.dma_start(M[:, 7168:10240].rearrange("p (k n) -> p k n", k=3), w_o[:, 0:3, :]).then_inc(out_ld, 16)
            load_router(0)
            load_ln(0)
            for n in range(3 * KD, 6 * KD):
                if n == 3 * KD + RING:
                    sp.wait_ge(conv_ps, CT)
                    sp.dma_start(W[:, 20480:24576].rearrange("p (k n) -> p k n", k=4), w_o[:, 3:7, :]).then_inc(out_ld, 16)
                if n == 5 * KD:
                    sp.wait_ge(conv_used, CT)
                    sp.dma_start(M[:, 832:1856], w_o[:, 7, :]).then_inc(out_ld, 16)
                load_ada(n)
            for n in range(6 * KD, LATE):
                load_ada(n)
            sp.wait_ge(conv_ps, 2 * CT)
            load_gate_up(0, 0, 0, 0)
            sp.wait_ge(conv_ps, 3 * CT)
            load_gate_up(0, 0, 0, 1)
            sp.wait_ge(oT_ps, 1)
            for u in range(2):
                load_gate_up(0, 1, 1, u)
            load_down(0, 1, 1)
            sp.wait_ge(y_ps, 4)
            load_down(0, 0, 0)
            with sp.Fori(1, PAIRS // 2) as j:
                for b in range(2):
                    load_experts(0, 2 * j + b, b)
            w_in = rows8(a["ret_w_in"][0])
            w_o1 = a["ret_w_out"][0].rearrange("(k p) n -> p k n", p=P)

            def load_part(n):
                dst, ld, _ = part_raw(n)
                j = n - RAW_PARTS
                if j >= 4:
                    sp.wait_ge(w_lo_ready, n - 3)
                elif j >= 2:
                    sp.wait_ge(ret_y, RH // 2)
                elif j >= 0:
                    sp.wait_ge(rhead_ps, RH)
                elif n >= 3:
                    sp.wait_ge(w_lo_ready, n - 2)
                c, k = n // 2, 4 * (n % 2)
                src = w_in[:, k:k + 4, HALF * c:HALF * (c + 1)] if n < RET_PARTS else \
                    w_o1[:, 2 * (n - RET_PARTS):2 * (n - RET_PARTS) + 2, :]
                sp.dma_start(dst.rearrange("p (k n) -> p k n", k=src.shape[1]), src).then_inc(ld, 16)

            sp.wait_ge(down_ps, 2 * (PAIRS - 1))
            for n in range(3):
                load_part(n)
            load_ln(1)
            dense_loads(0)
            load_router(1)
            sp.wait_ge(down_ps, 2 * PAIRS)
            sp.dma_start(W[:, 8192:10240], a["decay"]).then_inc(decay_ld, 16)
            late = LATE
            for c in range(RET_CHUNKS):
                for j in range(LATE_AT[c]):
                    if j < 2:
                        load_part(2 * c + 3 + j)
                    if late == LATE:
                        sp.wait_ge(h_lo_ready, 2)
                    load_ada(late)
                    late += 1
                if LATE_AT[c] < 2:
                    load_part(2 * c + 4)
            assert late == BLOCKS
            load_ln(2)
            load_part(RAW_PARTS)
            load_part(RAW_PARTS + 1)
            sp.wait_ge(w_lo_ready, RET_PARTS + 2)
            load_gate_up(1, 0, 0, 0)
            load_part(RAW_PARTS + 2)
            load_part(RAW_PARTS + 3)
            sp.wait_ge(w_lo_ready, RAW_PARTS)
            sp.wait_ge(ret_ps, 2 * RET_CHUNKS)
            load_gate_up(1, 0, 0, 1)
            load_part(RAW_PARTS + 4)
            sp.wait_ge(ada_used, BLOCKS)
            load_down(1, 0, 0)
            sp.wait_ge(y_ps, 8)
            for u in range(2):
                load_gate_up(1, 1, 1, u)
            load_down(1, 1, 1)
            with sp.Fori(1, PAIRS // 2) as j:
                for b in range(2):
                    load_experts(1, 2 * j + b, b)
            load_ln(3)
            dense_loads(1)
            for t in range(TT):
                sp.wait_ge(x_ready, 2 * (SUBLAYERS - 1) + t + 1)
                sp.dma_start(out[0, P * t:P * (t + 1), :], x[:, t, :]).then_inc(out_st, 16)
            sp.wait_ge(out_st, 16 * TT)

        @block.scalar
        def _(act):
            ch = Chain(act, act_chain)

            def h_rounded(i):
                act.wait_ge(hT_even, 5 + i)
                act.wait_ge(hT_odd, 5 + i)
                act.activation(h_hi[:, D * i:D * (i + 1)], hflat[:, D * i:D * (i + 1)], ACT.Copy).then_inc(h_hi_ready, 1)

            def h_banks(s, then=None):
                for bank in (1, 3):
                    act.wait_ge(xT_ps, 4 * s + bank + 1)
                    act.wait_ge(third_ready, 3 * s + 2)
                    for k in (2 * bank, 2 * bank + 1):
                        ins = act.activation(hT[:, k, :], PS[:, bank, 256 * (k % 2):256 * (k % 2) + 256], ACT.Identity,
                                             bias=mod_c[:, s, 0, k:k + 1], scale=mod_c[:, s, 1, k:k + 1])
                    ins.then_inc(hT_odd, 1)
                    if then:
                        then(bank // 2)

            def norm_rstd(s):
                for t in range(TT):
                    act.wait_ge(var_ready, 2 * s + t + 1)
                    act.activation(rstd[:, t:t + 1], rvar[:, t:t + 1], ACT.Sqrt).then_inc(rstd_made, 1)

            def router(l):
                xk = x[:, :, :].rearrange("q t (p k) -> q t k p", k=KD)
                for t in range(TT):
                    act.activation(x_parts[0][:, t], xk[:, t], ACT.Copy).then_inc(x1_ready, 1)
                for t in range(TT):
                    act.wait_ge(rest_ready, 2 * l + t + 1)
                    act.activation(x_parts[1][:, t], x_rest[:, t], ACT.Copy).then_inc(x2_ready, 1)
                act.wait_ge(gdiff_ready, l + 1)
                act.activation(d4, d4, ACT.Exp).then_inc(gexp_ready, 1)
                act.wait_ge(ediff_ready, l + 1)
                act.activation(e_x, e_d, ACT.Exp).then_inc(eexp_ready, 1)

            def gathered(l, q):
                for g in range(2):
                    act.wait_ge(gath_ps, 2 * q + g + 1)
                    for k in range(4 * g, 4 * g + 4):
                        ins = act.activation(xselT[:, k, :], PS[:, GATH[g], P * (k % 4):P * (k % 4) + P], ACT.Identity,
                                             bias=mod_c[:, 2 * l + 1, 0, k:k + 1], scale=mod_c[:, 2 * l + 1, 1, k:k + 1])
                    ins.then_inc(gath_sb, 1)

            def pair(l, i, last=False):
                q = PAIRS * l + i
                act.wait_ge(gu_ps, q + 1)
                act.activation(silu_sb, PS[:, GU, 0:FE], ACT.Silu).then_inc(silu_ready, 1)
                if not last:
                    gathered(l, q + 1)
                for h in range(2):
                    act.wait_ge(down_ps, 2 * q + h + 1)
                    act.activation(y_hi[:, HALF * h:HALF * (h + 1)], PS[:, DOWN[h], :], ACT.Copy).then_inc(y_hi_ready, 1)

            def experts(l):
                gathered(l, PAIRS * l)
                with act.Fori(0, PAIRS // 2 - 1) as j:
                    for b in range(2):
                        pair(l, 2 * j + b)
                pair(l, PAIRS - 2)
                pair(l, PAIRS - 1, last=True)
                d = dense[l]
                act.wait_ge(route_ready, l + 1)
                flag = act.value_load(over[0:1, 0:1])
                with act.If(flag > 0):
                    with act.Fori(0, EXPERTS) as e:
                        for t in range(TT):
                            act.wait_ge(d["gu"], 2 * e + t + 1)
                            act.activation(silu_sb, PS[:, GU, 0:FE], ACT.Silu).then_inc(d["silu"], 1)

            act.wait_ge(c_ld, 16)
            act.activation(c_silu[:, :], c_in[:, :], ACT.Silu).then_inc(c_silu_ready, 1)

            h_banks(0)
            act.wait_ge(angle_ready, 4)
            act.activation(trig_m[:, :, :, :], trig_m[:, :, :, :], ACT.Sin)
            act.activation(trig_r[:, :, :, :], trig_r[:, :, :, :], ACT.Sin).then_inc(trig_ready, 1)
            for t in range(TT):
                act.wait_ge(lowrank_sb, t + 1)
                act.activation(low_sq, low[:, t, 0:QR], ACT.Square, accum_out=soft[:, 2 * t:2 * t + 1]).then_inc(square_ready, 1)
                ch.step(act.activation(M[:, 6856:6984], low[:, t, QR:QR + KVR], ACT.Square,
                                       accum_out=soft[:, 2 * t + 1:2 * t + 2]))
                ch.hold()
            act.wait_ge(square_ready, TT)
            act.wait_ge(ms_ready, 2)
            act.activation(soft[:, 8:12], soft[:, 4:8], ACT.Sqrt).then_inc(rms_ready, 1)
            for h in range(2):
                act.wait_ge(conv_ps, 2 * h + 2)
                act.activation(conv_x[:, 2 * h:2 * h + 2, :].rearrange("p c t -> p (c t)"), PS[:, 4 + h, :],
                               ACT.Copy).then_inc(conv_x_sb, 1)
            for t in range(TT):
                for h in range(2):
                    act.wait_ge(up_ps, 2 * t + h + 1)
                    act.activation(q_sb[:, t, 4 * h:4 * h + 4, :],
                                   PS[:, 2 * t + h, 0:4 * QK].rearrange("p (h c) -> p h c", h=4), ACT.Copy).then_inc(up_q_sb, 1)
            for t in range(TT):
                for h in range(2):
                    act.wait_ge(up_ps, 4 + 2 * t + h + 1)
                    src = PS[:, 4 + 2 * t + h, :].rearrange("p (h c) -> p h c", h=4)
                    act.activation(k_sb[:, t, 4 * h:4 * h + 4, 0:NOPE], src[:, :, 0:NOPE], ACT.Copy).then_inc(up_k_sb, 1)
                    act.activation(v_sb[:, t, 4 * h:4 * h + 4, :], src[:, :, NOPE:], ACT.Copy).then_inc(up_k_sb, 1)
            for n in range(4):
                act.wait_ge(qkT_ps, 4 + n + 1)
                act.activation(kT0[:, 2 * n:2 * n + 2, :].rearrange("p h t -> p (h t)"), PS[0:QK, 4 + n, :], ACT.Copy)\
                   .then_inc(kT_ready, 1)
            def probabilities(h):
                b = h % 2
                act.wait_ge(shift_ready, h + 1)
                if h >= 2:
                    act.wait_ge(probT_ps, h - 1)
                act.activation(prob[:, b, 0:P], score[:, b, 0:P], ACT.Exp, bias=soft[:, 16 + 2 * h:17 + 2 * h],
                               scale=MLA_SCALE, accum_out=soft[:, 32 + 2 * h:33 + 2 * h]).then_inc(prob_ready, 1)
                act.activation(prob[:, b, P:3 * P], score[:, b, P:3 * P], ACT.Exp, bias=soft[:, 17 + 2 * h:18 + 2 * h],
                               scale=MLA_SCALE, accum_out=soft[:, 33 + 2 * h:34 + 2 * h]).then_inc(prob_ready, 1)

            probabilities(0)
            for h in range(HEADS):
                b = h % 2
                act.wait_ge(probT_ps, h + 1)
                act.activation(probT[:, b, :], PS[:, 2 + b, 0:3 * P], ACT.Copy).then_inc(probT_ready, 1)
                if h + 1 < HEADS:
                    probabilities(h + 1)
                act.wait_ge(head_ps, h + 1)
                act.wait_ge(psum_inv, h + 1)
                for t in range(TT):
                    act.activation(o_sb[:, t, HV * h:HV * (h + 1)], PS[:, 2 + b, 384 + HV * t:384 + HV * (t + 1)], ACT.Copy,
                                   scale=soft[:, 96 + 2 * h + t:97 + 2 * h + t]).then_inc(head_sb, 1)
                n = 3 * KD + WITH_HEAD * (h + 1) - 1
                if n in SHARED:
                    act.wait_ge(ada_ld[n % RING], 16 * (n // RING + 1))
                    act.activation(ada_buf(n), ada_buf(n), ACT.Copy, scale=c_silu[:, n % KD:n % KD + 1]).then_inc(ada_scaled, 1)
            norm_rstd(0)

            def split_hi(n):
                raw, ld, loaded = part_raw(n)
                act.wait_ge(ld, loaded)
                m = n - 2
                if m >= RET_PARTS:
                    act.wait_ge(part_used, RET_CHUNKS + m - RET_PARTS + 1)
                elif m >= 0:
                    act.wait_ge(ret_ps if m % 2 else part_used, m + 1 if m % 2 else m // 2 + 1)
                act.activation(w_hi[n % 2][:, :], raw, ACT.Copy).then_inc(w_hi_ready, 1)

            h_banks(1)
            router(0)
            experts(0)
            split_hi(0)
            split_hi(1)
            norm_rstd(1)

            h_banks(2, then=h_rounded)

            def head_out(h):
                act.wait_ge(rhead_ps, h + 1)
                for t in range(TT):
                    act.activation(o1[:, t, DV * h:DV * (h + 1)], PS[:, 6 + h % 2, DV * t:DV * (t + 1)],
                                   ACT.Copy).then_inc(rhead_sb, 1)

            def pair_rstd(p):
                act.wait_ge(rvar_ready, p + 1)
                v = rsd[:, :, 2 * p:2 * p + 2]
                act.activation(v, v, ACT.Sqrt).then_inc(rstd_ready, 1)

            for c in range(RET_CHUNKS):
                split_hi(2 * c + 2)
                split_hi(2 * c + 3)
                for t in range(TT):
                    n = 2 * c + t
                    act.wait_ge(ret_ps, n + 1)
                    bank = PS[:, n % 4, :]
                    if c < 4:
                        if c == 2:
                            act.wait_ge(rope_ready, 2)
                        dst = raw1[:, t, 4 * (c % 2):4 * (c % 2) + 4, :].rearrange("p h c -> p (h c)")
                        act.activation(dst, bank, ACT.Copy).then_inc(ret_sb, 1)
                    elif c < 8:
                        act.activation(v1[:, t, HALF * (c - 4):HALF * (c - 3)], bank, ACT.Copy).then_inc(ret_sb, 1)
                    else:
                        act.activation(g1[:, t, HALF * (c - 8):HALF * (c - 7)], bank, ACT.Silu).then_inc(ret_sb, 1)
                if c >= 8:
                    head_out(2 * (c - 8))
                    head_out(2 * (c - 8) + 1)
                if c >= 9:
                    pair_rstd(c - 9)

            def turned_y(n):
                act.wait_ge(ryT_ps, n + 1)
                for k in (2 * n, 2 * n + 1):
                    act.activation(yT_hi[:, SEQ * k:SEQ * (k + 1)], PS[:, 4 + n % 4, 256 * (k % 2):256 * (k % 2) + 256], ACT.Copy,
                                   scale=gn_g[:, k:k + 1]).then_inc(ryT_hi, 1)

            turned_y(0)
            turned_y(1)
            pair_rstd(RH // 2 - 1)
            turned_y(2)
            for n in range(3, RH + 1):
                split_hi(RET_PARTS + n - 1)
                if n < RH:
                    turned_y(n)
            norm_rstd(2)

            h_banks(3)
            router(1)
            experts(1)
            norm_rstd(3)

        @block.tensor
        def _(pe):
            def third(m, bank):
                acc, s = ada_acc(m), m // 3
                pe.wait_ge(ada_used, KD * (m + 1))
                if m % 3 < 2:
                    part = acc.rearrange("q (p k) -> q k p", k=KD)
                    for k in range(KD):
                        ins = pe.matmul(PS[:, bank, k:k + 1], part[:, k, :], ones[:, 0:1], start=True, stop=True)
                else:
                    for h in range(2):
                        cut = slice(HALF * h, HALF * (h + 1))
                        pe.matmul(PS[:, bank + h, :], ones, acc[:, cut], start=True, stop=False)
                        ins = pe.matmul(PS[:, bank + h, :], ones[0:1, :], gates[0:1, s, cut], start=False, stop=True)
                ins.then_inc(third_ps, 1)

            def turn_x(s):
                xk = x[:, :, :].rearrange("q t (p k) -> q t k p", k=KD)
                for t in range(TT):
                    if s:
                        pe.wait_ge(x_ready, 2 * (s - 1) + t + 1)
                    for k in range(KD):
                        at = 256 * (k % 2) + P * t
                        ins = pe.transpose(PS[:, k // 2, at:at + P], xk[:, t, k, :], ident)
                        if t == TT - 1 and k % 2:
                            ins.then_inc(xT_ps, 1)

            def h_ready(s):
                pe.wait_ge(hT_even, 2 * (s + 1))
                pe.wait_ge(hT_odd, 2 * (s + 1))

            def router(l):
                h_ready(2 * l + 1)
                pe.wait_ge(third_ready, (8, 12)[l])
                pe.wait_ge(rw_ld, 64 * (l + 1))
                n = GROUPS + EXPERTS
                for k in range(KD):
                    ins = pe.matmul(PS[0:n, 4, 0:SEQ], router_w[:, k, :], hT[:, k, :], start=(k == 0), stop=(k == KD - 1))
                ins.then_inc(logitT_ps, 1)
                pe.wait_ge(logitT_sb, l + 1)
                for t in range(TT):
                    ins = pe.transpose(PS[:, 4, 64 * t:64 * t + n], logitT[:, P * t:P * (t + 1)], ident[0:n, 0:n])
                ins.then_inc(logit_ps, 1)
                pe.wait_ge(mask_ready, l + 1)
                pe.matmul(PS[:, 5, 0:32], upper, mask[:, 0, :], start=True, stop=True)
                pe.matmul(PS[:, 5, 32:64], ones, mask[:, 0, :], start=True, stop=False)
                pe.matmul(PS[:, 5, 32:64], upper, mask[:, 1, :], start=False, stop=True)
                pe.matmul(PS[:, 5, 64:96], ones, mask[:, 0, :], start=True, stop=False)
                pe.matmul(PS[:, 5, 64:96], ones, mask[:, 1, :], start=False, stop=True).then_inc(rank_ps, 1)

            def gather(q, b):
                pe.wait_ge(sel_ready, q + 1)
                for g in range(2):
                    for k in range(4 * g, 4 * g + 4):
                        o = PS[:, GATH[g], P * (k % 4):P * (k % 4) + P]
                        for t in range(TT):
                            for j in range(3):
                                ins = pe.matmul(o, x_parts[j][:, t, k, :], sel[b][:, t].rearrange("p e s -> p (e s)"),
                                                start=(t + j == 0), stop=(t + j == TT + 1))
                    ins.then_inc(gath_ps, 1)

            def scatter(q, b, h):
                pe.wait_ge(y_lo_ready, 2 * q + h + 1)
                for t in range(TT):
                    c = 2 * h + t
                    if not (isinstance(q, int) and 4 * q + c < 2):
                        pe.wait_ge(acc_done, 4 * q + c - 1)
                    tok, cut = slice(P * t, P * (t + 1)), slice(HALF * h, HALF * (h + 1))
                    pe.matmul(PS[:, SCAT[t], :], selT_hi[b][:, tok], y_hi[:, cut], start=True, stop=False)
                    pe.matmul(PS[:, SCAT[t], :], selT_hi[b][:, tok], y_lo[:, cut], start=False, stop=False)
                    pe.matmul(PS[:, SCAT[t], :], selT_lo[b][:, tok], y_hi[:, cut], start=False, stop=True)\
                      .then_inc(scat_ps, 1)

            def pair(l, i, b, first=False, last=False):
                q = PAIRS * l + i
                pe.wait_ge(gath_sb, 2 * (q + 1))
                pe.wait_ge(gu_ld[b], 32 * (PAIRS // 2 * l + 1) + 16 * (i - b))
                if not (isinstance(q, int) and q == 0):
                    pe.wait_ge(act_ready, q)
                for k in range(KD):
                    for e in range(2):
                        o = PS[64 * e:64 * e + 64, GU, :].rearrange("p (u f) -> p u f", u=2)
                        ins = pe.matmul(o, xselT[:, k, 64 * e:64 * e + 64], w_gu[b][:, :, e, k, :],
                                        start=(k == 0), stop=(k == KD - 1))
                ins.then_inc(gu_ps, 1)
                if not last:
                    gather(q + 1, 1 - b)
                pe.wait_ge(act_ready, q + 1)
                if not (isinstance(q, int) and q == 0):
                    pe.wait_ge(turn_sb, q)
                for k in range(KF):
                    pe.transpose(PS[:, TURN, P * k:P * (k + 1)], act_sb[:, P * k:P * (k + 1)], ident)
                for t in range(TT):
                    ins = pe.transpose(PS[:, TURN, 2 * P + P * t:2 * P + P * (t + 1)],
                                       sel_w[b][:, t].rearrange("p e s -> p (e s)"), ident)
                ins.then_inc(turn_ps, 1)
                for h in range(2):
                    if not first:
                        scatter(q - 1, 1 - b, h)
                    elif not (isinstance(q, int) and q == 0):
                        pe.wait_ge(y_lo_ready, 2 * (q - 1) + h + 1)
                    if h == 0:
                        pe.wait_ge(turn_sb, q + 1)
                        pe.wait_ge(down_ld[b], 16 * (PAIRS // 2 * l + 1) + 8 * (i - b))
                    for k in range(KF):
                        for e in range(2):
                            ins = pe.matmul(PS[64 * e:64 * e + 64, DOWN[h], :], turn[b][:, P * k + 64 * e:P * k + 64 * e + 64],
                                            w_down[b][:, e, k, HALF * h:HALF * (h + 1)], start=(k == 0), stop=(k == KF - 1))
                    ins.then_inc(down_ps, 1)

            def experts(l):
                gather(PAIRS * l, 0)
                pair(l, 0, 0, first=True)
                pair(l, 1, 1)
                with pe.Fori(1, PAIRS // 2 - 1) as j:
                    for b in range(2):
                        pair(l, 2 * j + b, b)
                pair(l, PAIRS - 2, 0)
                pair(l, PAIRS - 1, 1, last=True)
                for h in range(2):
                    scatter(PAIRS * (l + 1) - 1, 1, h)
                d = dense[l]
                pe.wait_ge(acc_done, 4 * PAIRS * (l + 1))
                flag = pe.value_load(over[0:1, 0:1])
                with pe.If(flag > 0):
                    with pe.Fori(0, EXPERTS) as e:
                        pe.wait_ge(d["ld"], 48 * e + 48)
                        for t in range(TT):
                            for k in range(KD):
                                ins = pe.matmul(PS[:, GU, :].rearrange("p (u f) -> p u f", u=2), hT[:, k, P * t:P * (t + 1)],
                                                w_gu[1][:, :, 0, k, :], start=(k == 0), stop=(k == KD - 1))
                            ins.then_inc(d["gu"], 1)
                            pe.wait_ge(d["act"], 2 * e + t + 1)
                            for k in range(KF):
                                ins = pe.transpose(PS[:, TURN, P * k:P * (k + 1)], act_sb[:, P * k:P * (k + 1)], ident)
                            ins.then_inc(d["turn"], 1)
                            pe.wait_ge(d["turned"], 2 * e + t + 1)
                            for h in range(2):
                                for k in range(KF):
                                    ins = pe.matmul(PS[:, DOWN[h], :], turn[0][:, P * k:P * (k + 1)],
                                                    w_down[1][:, 0, k, HALF * h:HALF * (h + 1)], start=(k == 0), stop=(k == KF - 1))
                            ins.then_inc(d["down"], 1)
                            pe.wait_ge(d["added"], 4 * e + 2 * t + 2)

            pe.wait_ge(in_ld, 32)
            turn_x(0)
            third(0, 4)
            third(1, 5)
            pe.wait_ge(small_ld, 16 * SMALL_LOADS)
            pe.transpose(PS[:, 7, 0:31], gain_rows, ident[0:31, 0:31])
            pe.wait_ge(pos_rows, 1)
            pe.transpose(PS[:, 7, 32:34], pos_r, ident[0:TT, 0:TT]).then_inc(columns_ps, 1)
            h_ready(0)
            pe.wait_ge(lowrank_ld, 16)
            for t in range(TT):
                for k in range(KD):
                    ins = pe.matmul(PS[:, t, 0:LOWRANK], hT[:, k, P * t:P * (t + 1)], w_low[:, k, :],
                                    start=(k == 0), stop=(k == KD - 1))
                ins.then_inc(lowrank_ps, 1)

            def conv(j, c, steps):
                bank, half = (4 + c // 2, c % 2) if j == 0 else (4 + c % 2, c // 2)
                for k in steps:
                    ins = pe.matmul(PS[:, bank, 256 * half:256 * half + 256], w_conv[j][:, k, P * c:P * (c + 1)], hT[:, k, :],
                                    start=(k == 0), stop=(k == KD - 1))
                if k == KD - 1:
                    ins.then_inc(conv_ps, 1)

            pe.wait_ge(third_ready, 2)
            pe.wait_ge(convw_ld[0], 16)
            conv(0, 0, range(KD))
            conv(0, 1, range(KD))
            pe.wait_ge(lowrank_n, TT)
            for k in range(3):
                for t in range(TT):
                    at = 256 * (k % 2) + P * t
                    ins = pe.transpose(PS[:, k // 2, at:at + P], low[:, t, P * k:P * (k + 1)], ident)
            ins.then_inc(lowT_ps, 1)
            conv(0, 2, range(KD))
            conv(0, 3, range(KD))
            pe.wait_ge(lowT_ready, 1)
            pe.wait_ge(upw_ld, 32)
            for t in range(TT):
                for h in range(2):
                    for k in range(2):
                        ins = pe.matmul(PS[:, 2 * t + h, 0:4 * QK], lowT[:, k, P * t:P * (t + 1)], w_uq[:, k, 4 * QK * h:4 * QK * (h + 1)],
                                        start=(k == 0), stop=(k == 1))
                    ins.then_inc(up_ps, 1)
            pe.wait_ge(conv_x_sb, 2)
            pe.wait_ge(columns_sb, 1)
            for t in range(TT):
                for h in range(2):
                    pe.matmul(PS[:, 4 + 2 * t + h, :], lowT[:, 2, P * t:P * (t + 1)], w_ukv[:, HALF * h:HALF * (h + 1)],
                              start=True, stop=True).then_inc(up_ps, 1)
            pe.wait_ge(up_q_sb, 4)
            pe.wait_ge(up_k_sb, 8)
            for u, src in enumerate((q_sb, k_sb)):
                pe.wait_ge(qk_ready, u + 1)
                for h in range(HEADS):
                    for t in range(TT):
                        at = 256 * (h % 2) + P * t
                        ins = pe.transpose(PS[0:QK, 4 * u + h // 2, at:at + P], src[:, t, h, :], ident)
                    if h % 2:
                        ins.then_inc(qkT_ps, 1)
            pe.wait_ge(qT_ready, 4)

            def scores(h):
                b = h % 2
                pe.wait_ge(kT_ready, h // 2 + 1)
                if h >= 2:
                    pe.wait_ge(shift_ready, h - 1)
                pe.matmul(PS[:, b, 0:P], qT0[:, h, 0:P], kT0[:, h, 0:P], start=True, stop=True)
                pe.matmul(PS[:, b, P:3 * P], qT0[:, h, P:SEQ], kT0[:, h, :], start=True, stop=True).then_inc(score_ps, 1)

            for j in (1, 2):
                pe.wait_ge(convw_ld[j], 16)
            scores(0)
            for h in range(HEADS):
                b = h % 2
                if h + 1 < HEADS:
                    scores(h + 1)
                if h < 2:
                    pe.wait_ge(kT_ready, 4)
                else:
                    pe.wait_ge(conv_used, h - 1)
                conv(1 + h // CT, h % CT, range(0, KD // 2))
                pe.wait_ge(prob_ready, 2 * (h + 1))
                if h >= 2:
                    pe.wait_ge(head_sb, 2 * (h - 1))
                for j in range(3):
                    ins = pe.transpose(PS[:, 2 + b, P * j:P * (j + 1)], prob[:, b, P * j:P * (j + 1)], ident)
                ins.then_inc(probT_ps, 1)
                conv(1 + h // CT, h % CT, range(KD // 2, KD))
                pe.wait_ge(probT_ready, h + 1)
                pe.matmul(PS[:, 2 + b, 384:384 + HV], probT[:, b, 0:P], v_sb[:, 0, h, :], start=True, stop=True)
                pe.matmul(PS[:, 2 + b, 384 + HV:HALF], probT[:, b, P:2 * P], v_sb[:, 0, h, :], start=True, stop=False)
                pe.matmul(PS[:, 2 + b, 384 + HV:HALF], probT[:, b, 2 * P:3 * P], v_sb[:, 1, h, :], start=False, stop=True)\
                  .then_inc(head_ps, 1)
                if h == 2:
                    third(2, 6)
                if h == 5:
                    pe.wait_ge(third_ready, 3)
                    third(3, 6)
            pe.wait_ge(head_sb, 2 * HEADS)
            pe.wait_ge(third_ready, 4)
            for k in range(4):
                for t in range(TT):
                    at = 256 * (k % 2) + P * t
                    ins = pe.transpose(PS[:, 6 + k // 2, at:at + P], o_sb[:, t, P * k:P * (k + 1)], ident)
            ins.then_inc(oT_ps, 1)
            pe.wait_ge(conv_used, 2 * CT)
            third(4, 4)
            pe.wait_ge(out_ld, 48)
            for t in range(TT):
                for h in range(2):
                    for k in range(KD):
                        if k == 4 and t + h == 0:
                            pe.wait_ge(oT_ready, 1)
                        ins = pe.matmul(PS[:, 2 * t + h, :], yT0[:, k, P * t:P * (t + 1)],
                                        w_out0[k][:, HALF * h:HALF * (h + 1)], start=(k == 0), stop=(k == KD - 1))
                    ins.then_inc(y_ps, 1)
                if t == 0:
                    pe.wait_ge(third_ready, 5)
                    third(5, 4)

            third(6, 6)
            third(7, 7)
            turn_x(1)
            router(0)
            experts(0)

            turn_x(2)

            def turn_heads(u):
                pe.wait_ge(rope_ready, 2 * (u + 1))
                if u:
                    pe.wait_ge(third_ready, 9)
                for h in range(RH):
                    for t in range(TT):
                        at = 256 * (h % 2) + P * t
                        ins = pe.transpose(PS[:, 4 + h // 2, at:at + P], turned1[:, t, h, :], ident)
                    if h % 2:
                        ins.then_inc(retT_ps, 1)

            def ret_scores(h):
                b = h % 2
                if h >= 2:
                    pe.wait_ge(decayed, h - 1)
                pe.matmul(PS[:, 4 + b, 0:SEQ], qkT1[1][:, h, 0:P], qkT1[0][:, h, :], start=True, stop=True)
                pe.matmul(PS[:, 4 + b, SEQ:SEQ + P], qkT1[1][:, h, P:SEQ], qkT1[0][:, h, P:SEQ], start=True, stop=True)\
                  .then_inc(rscore_ps, 1)

            def ret_head(h):
                b = h % 2
                pe.wait_ge(decayed, h + 1)
                if h >= 2:
                    pe.wait_ge(rhead_sb, 2 * (h - 1))
                vh = v1[:, :, DV * h:DV * (h + 1)]
                pe.matmul(PS[:, 6 + b, 0:DV], sT1[:, b, 0:P], vh[:, 0, :], start=True, stop=True)
                pe.matmul(PS[:, 6 + b, DV:2 * DV], sT1[:, b, P:2 * P], vh[:, 0, :], start=True, stop=False)
                pe.matmul(PS[:, 6 + b, DV:2 * DV], sT1[:, b, 2 * P:3 * P], vh[:, 1, :], start=False, stop=True)\
                  .then_inc(rhead_ps, 1)

            for c in range(RET_CHUNKS):
                for part in range(2):
                    m = 2 * c + part
                    pe.wait_ge(w_lo_ready, m + 1)
                    pe.wait_ge(h_lo_ready, part + 1)
                    hi = w_hi[m % 2][:, :].rearrange("p (k n) -> p k n", k=4)
                    lo = w_lo[m % 2][:, :].rearrange("p (k n) -> p k n", k=4)
                    for t in range(TT):
                        n = 2 * c + t
                        if n >= 4 and part == 0:
                            pe.wait_ge(ret_sb, n - 3)
                        for k in range(4):
                            kk = 4 * part + k
                            tok = slice(SEQ * kk + P * t, SEQ * kk + P * (t + 1))
                            pe.matmul(PS[:, n % 4, :], h_hi[:, tok], hi[:, k, :], start=(kk == 0), stop=False)
                            pe.matmul(PS[:, n % 4, :], h_hi[:, tok], lo[:, k, :], start=False, stop=False)
                            ins = pe.matmul(PS[:, n % 4, :], h_lo[:, tok], hi[:, k, :], start=False, stop=(kk == KD - 1))
                        if part == 1:
                            ins.then_inc(ret_ps, 1)
                    if part == 0:
                        ins.then_inc(part_used, 1)
                if c == 3:
                    turn_heads(0)
                if c == 4:
                    pe.wait_ge(retT_ready, 4)
                    third(8, 4)
                if c == 5:
                    turn_heads(1)
                if c == 7:
                    pe.wait_ge(retT_ready, 8)
                    third(9, 6)
                if c == 8:
                    pe.wait_ge(third_ready, 10)
                    pe.wait_ge(ret_sb, 16)
                if c >= 8:
                    ret_head(2 * (c - 8))
                    ret_head(2 * (c - 8) + 1)
                if 7 <= c < 11:
                    ret_scores(2 * (c - 7))
                    ret_scores(2 * (c - 7) + 1)
            pe.wait_ge(decayed, RH)
            pe.wait_ge(rhead_sb, 2 * RH)

            def turn_y(n):
                pe.wait_ge(ret_y, n // 2 + 1)
                if n >= 4:
                    pe.wait_ge(ryT_lo, 2 * (n - 3))
                for k in (2 * n, 2 * n + 1):
                    for t in range(TT):
                        at = 256 * (k % 2) + P * t
                        ins = pe.transpose(PS[:, 4 + n % 4, at:at + P], o1[:, t, P * k:P * (k + 1)], ident)
                ins.then_inc(ryT_ps, 1)

            for n in range(3):
                turn_y(n)
            pe.wait_ge(ret_sb, 2 * RET_CHUNKS)
            for j in range(OUT_PARTS):
                m = RET_PARTS + j
                pe.wait_ge(w_lo_ready, m + 1)
                pe.wait_ge(ryT_lo, 2 * (j + 1))
                hi = w_hi[m % 2][:, :].rearrange("p (k n) -> p k n", k=2)
                lo = w_lo[m % 2][:, :].rearrange("p (k n) -> p k n", k=2)
                for t in range(TT):
                    for h in range(2):
                        cut = slice(HALF * h, HALF * (h + 1))
                        for k in range(2):
                            kk = 2 * j + k
                            tok = slice(SEQ * kk + P * t, SEQ * kk + P * (t + 1))
                            pe.matmul(PS[:, 2 * t + h, :], yT_hi[:, tok], hi[:, k, cut], start=(kk == 0), stop=False)
                            pe.matmul(PS[:, 2 * t + h, :], yT_hi[:, tok], lo[:, k, cut], start=False, stop=False)
                            ins = pe.matmul(PS[:, 2 * t + h, :], yT_lo[:, tok], hi[:, k, cut], start=False, stop=(kk == RV // P - 1))
                        if j == OUT_PARTS - 1:
                            ins.then_inc(y_ps, 1)
                if j < OUT_PARTS - 1:
                    ins.then_inc(part_used, 1)
                if j + 3 < RH:
                    turn_y(j + 3)
            pe.wait_ge(ryT_lo, RV // P)
            third(10, 4)
            third(11, 6)

            turn_x(3)
            router(1)
            experts(1)

        def split_lo(eng, n):
            eng.wait_ge(w_hi_ready, n + 1)
            eng.tensor_tensor(w_lo[n % 2][:, :], part_raw(n)[0], w_hi[n % 2][:, :].bitcast(F32), ALU.subtract)\
               .then_inc(w_lo_ready, 1)

        def rope(eng, ch, src, dst, lo, half, cos, sin, tmp, view):
            a1, a2 = src[..., lo:lo + half], src[..., lo + half:lo + 2 * half]
            t = [view(x) for x in tmp]
            ch.hold()
            ch.step(eng.tensor_tensor(t[0], a1, cos, ALU.mult))
            ch.step(eng.tensor_tensor(t[1], a2, sin, ALU.mult))
            ch.step(eng.tensor_tensor(t[2], a2, cos, ALU.mult))
            ch.step(eng.tensor_tensor(t[3], a1, sin, ALU.mult))
            ch.hold()
            ch.step(eng.tensor_tensor(dst[..., lo:lo + half], t[0], t[1], ALU.subtract))
            return eng.tensor_tensor(dst[..., lo + half:lo + 2 * half], t[2], t[3], ALU.add)


        @block.vector
        def _(dve):
            ch = Chain(dve, dve_chain)

            def ada_sum(n):
                m, k = n // KD, n % KD
                acc = ada_acc(m)
                if n < LATE:
                    dve.wait_ge(ada_ld[n % RING], 16 * (n // RING + 1))
                else:
                    dve.wait_ge(late_ld[n % 2], 16 * ((n - LATE) // 2 + 1))
                if k == 0:
                    if n - 1 in SHARED:
                        dve.wait_ge(ada_used, n)
                    if m >= 2:
                        dve.wait_ge(third_ps, m - 1)
                    dve.tensor_scalar(acc, ada_buf(n), c_silu[:, 0:1], None, ALU.mult).then_inc(ada_used, 1)
                else:
                    dve.wait_ge(ada_used, n)
                    dve.scalar_tensor_tensor(acc, ada_buf(n), c_silu[:, k:k + 1], acc, ALU.mult, ALU.add).then_inc(ada_used, 1)

            def third(m, bank):
                s, u = m // 3, m % 3
                dve.wait_ge(third_ps, m + 1)
                if u == 0:
                    dve.tensor_tensor(mod_c[:, s, 0, :], PS[:, bank, 0:KD], bias_c[:, s, 0, :], ALU.add).then_inc(third_ready, 1)
                elif u == 1:
                    shift, scale = mod_c[:, s, 0, :], mod_c[:, s, 1, :]
                    ins = dve.scalar_tensor_tensor(scale, PS[:, bank, 0:KD], 1.0, bias_c[:, s, 1, :], ALU.add, ALU.add)
                    if s:
                        ch.link(ins)
                        dve.wait_ge(third_ready, m)
                        ch.link(dve.tensor_tensor(shift_add[:, :], scale, ln_c[:, s - 1, 1, :], ALU.mult))
                        ch.link(dve.tensor_tensor(shift, shift, shift_add[:, :], ALU.add))
                        ins = dve.tensor_tensor(scale, scale, ln_c[:, s - 1, 0, :], ALU.mult)
                    ins.then_inc(third_ready, 1)
                else:
                    for h in range(2):
                        ins = dve.tensor_scalar(gates[:, s, HALF * h:HALF * (h + 1)], PS[:, bank + h, :], 1.0, None, ALU.add)
                    ins.then_inc(third_ready, 1)

            def h_banks(s):
                dve.wait_ge(third_ready, 3 * s + 2)
                for bank in (0, 2):
                    dve.wait_ge(xT_ps, 4 * s + bank + 1)
                    for k in (2 * bank, 2 * bank + 1):
                        ins = dve.tensor_scalar(hT[:, k, :], PS[:, bank, 256 * (k % 2):256 * (k % 2) + 256],
                                                mod_c[:, s, 1, k:k + 1], mod_c[:, s, 0, k:k + 1], ALU.mult, ALU.add)
                    ins.then_inc(hT_even, 1)

            def half_stats(z, t, h):
                ch.step(dve.bn_stats(stats[:, t, h, :], z[:, t, HALF * h:HALF * (h + 1)]))

            def residual(s, t):
                dve.wait_ge(third_ready, 3 * s + 3)
                for h in range(2):
                    cut = slice(HALF * h, HALF * (h + 1))
                    gated_y = mixed[s][:, cut]
                    dve.wait_ge(y_ps, 2 * s + 2 * t + h + 1)
                    ch.link(dve.tensor_tensor(gated_y, PS[:, 2 * t + h, :], gates[:, s, cut], ALU.mult))
                    if s:
                        dve.wait_ge(x_full, 2 * (s - 1) + t + 1)
                    ch.link(dve.scalar_tensor_tensor(x[:, t, cut], x[:, t, cut], ALPHA, gated_y, ALU.mult, ALU.add))
                    half_stats(x, t, h)

            def variance(s, t):
                ch.hold()
                ch.link(dve.bn_aggr(mv[:, t, :], stats[:, t, :, :].rearrange("p h c -> p (h c)")))
                ch.link(dve.tensor_scalar(rvar[:, t:t + 1], mv[:, t, 1:2], LN_EPS, None, ALU.add))
                dve.reciprocal(rvar[:, t:t + 1], rvar[:, t:t + 1]).then_inc(var_ready, 1)

            def normal(s, t):
                z = y_acc if s % 2 else x
                if s < SUBLAYERS - 1:
                    dve.wait_ge(rstd_made, 2 * s + t + 1)
                    ins = dve.tensor_scalar(x[:, t, :], z[:, t, :], mv[:, t, 0:1], rstd[:, t:t + 1], ALU.subtract, ALU.mult)
                else:
                    if t == 0:
                        dve.wait_ge(ln_ld, 32 * SUBLAYERS)
                    ch.link(dve.scalar_tensor_tensor(z[:, t, :], z[:, t, :], mv[:, t, 0:1], ln_g[:, :], ALU.subtract, ALU.mult))
                    dve.wait_ge(rstd_made, 2 * s + t + 1)
                    ins = dve.scalar_tensor_tensor(x[:, t, :], z[:, t, :], rstd[:, t:t + 1], ln_b[:, :], ALU.mult, ALU.add)
                ins.then_inc(x_ready, 1)

            def router(l):
                xk = x[:, :, :].rearrange("q t (p k) -> q t k p", k=KD)
                for t in range(TT):
                    dve.wait_ge(x1_ready, 2 * l + t + 1)
                    dve.tensor_tensor(x_rest[:, t], xk[:, t], x_parts[0][:, t], ALU.subtract).then_inc(rest_ready, 1)
                for t in range(TT):
                    dve.wait_ge(x2_ready, 2 * l + t + 1)
                    ins = dve.tensor_tensor(x_parts[2][:, t], x_rest[:, t], x_parts[1][:, t], ALU.subtract)
                    ins.then_inc(x3_ready, 1)
                dve.wait_ge(logitT_ps, l + 1)
                dve.wait_ge(rw_ld, 64 * (l + 1))
                dve.tensor_scalar(logitT, PS[0:GROUPS + EXPERTS, 4, 0:SEQ], router_b[:, 0:1], None, ALU.add).then_inc(logitT_sb, 1)
                dve.wait_ge(logit_ps, l + 1)
                lg = PS[:, 4, 0:128].rearrange("p (t c) -> p t c", t=TT)
                ch.link(dve.memset(g_pad, -3e38))
                ch.link(dve.tensor_copy(g_pad[:, :, 0:GROUPS], lg[:, :, 0:GROUPS]))
                for t in range(TT):
                    ch.step(dve.max(mx[:, t, :], g_pad[:, t, :]))
                ch.hold()
                for t in range(TT):
                    ch.step(dve.max_index(mi[:, t, :], mx[:, t, :], g_pad[:, t, :]))
                dve.tensor_tensor(d4, g_pad[:, :, 0:GROUPS], mx[:, :, 0:1].broadcast_to((P, TT, GROUPS)), ALU.subtract)\
                   .then_inc(gdiff_ready, 1)
                ch.hold()
                ch.link(dve.tensor_copy(g_i, mi[:, :, 0:1]))
                slots4 = cst[:, C_EXP:C_EXP + GROUPS].unsqueeze(1).broadcast_to((P, TT, GROUPS))
                ch.link(dve.tensor_tensor(oh4, slots4, g_i.broadcast_to((P, TT, GROUPS)), ALU.is_equal))
                for t in range(TT):
                    ch.step(dve.tensor_tensor(e_prod[:, t], lg[:, t, GROUPS:GROUPS + EXPERTS].rearrange("p (g j) -> p j g", g=GROUPS),
                                              oh4[:, t].unsqueeze(1).broadcast_to((P, PER_GROUP, GROUPS)), ALU.mult))
                ch.hold()
                ch.link(dve.tensor_reduce(e_sel, e_prod, AX.X, ALU.add))
                for t in range(TT):
                    ch.step(dve.max(mx[:, t, :], e_sel[:, t, :]))
                ch.hold()
                for t in range(TT):
                    ch.step(dve.max_index(mi[:, t, :], mx[:, t, :], e_sel[:, t, :]))
                dve.tensor_tensor(e_d, mx[:, :, 1:2], mx[:, :, 0:1], ALU.subtract).then_inc(ediff_ready, 1)
                ch.step(dve.tensor_scalar(g_8, g_i, float(PER_GROUP), None, ALU.mult))
                ch.hold()
                ch.link(dve.tensor_copy(e_id, mi[:, :, 0:2]))
                ch.link(dve.tensor_tensor(e_id, e_id, g_8.broadcast_to((P, TT, 2)), ALU.add))
                numbers = cst[:, C_EXP:C_EXP + EXPERTS].unsqueeze(1).broadcast_to((P, TT, EXPERTS))
                ch.step(dve.tensor_tensor(cw, numbers, e_id[:, :, 0:1].broadcast_to((P, TT, EXPERTS)), ALU.is_equal))
                ch.link(dve.tensor_tensor(eq2, numbers, e_id[:, :, 1:2].broadcast_to((P, TT, EXPERTS)), ALU.is_equal))
                dve.tensor_tensor(mask, cw, eq2, ALU.add).then_inc(mask_ready, 1)
                dve.wait_ge(gexp_ready, l + 1)
                ch.link(dve.tensor_reduce(g_sum, d4, AX.X, ALU.add))
                ch.link(dve.reciprocal(g_p, g_sum.rearrange("p (t e) -> p t e", t=TT)))
                dve.wait_ge(eexp_ready, l + 1)
                ch.link(dve.tensor_scalar(den, e_x, 1.0, None, ALU.add))
                ch.link(dve.reciprocal(den, den))
                ch.link(dve.tensor_tensor(w_1, g_p, den, ALU.mult))
                ch.link(dve.tensor_tensor(w_2, w_1, e_x, ALU.mult))
                ch.step(dve.tensor_tensor(cw, cw, w_1.broadcast_to((P, TT, EXPERTS)), ALU.mult))
                ch.link(dve.tensor_tensor(eq2, eq2, w_2.broadcast_to((P, TT, EXPERTS)), ALU.mult))
                ch.link(dve.tensor_tensor(cw, cw, eq2, ALU.add))
                dve.wait_ge(rank_ps, l + 1)
                flat = lambda v: v.rearrange("p t e -> p (t e)")
                ch.step(dve.tensor_reduce(over_f[:, :], PS[:, 5, 64:96], AX.X, ALU.max))
                ch.link(dve.scalar_tensor_tensor(flat(rank), PS[:, 5, 0:64], 1.0, flat(mask), ALU.add, ALU.mult))
                ch.link(dve.tensor_scalar(flat(rank), flat(rank), -1.0, None, ALU.add))
                ch.link(dve.scalar_tensor_tensor(flat(cw_over), flat(rank), float(SLOTS), flat(cw), ALU.is_ge, ALU.mult))
                dve.tensor_scalar(over[:, :], over_f[0:1, :], float(SLOTS), None, ALU.is_gt).then_inc(route_ready, 1)
                dve.wait_ge(route_ready, l + 1)

            slot_no = cst[:, C_SLOT:C_SLOT + SLOTS].unsqueeze(1).broadcast_to((P, 2, SLOTS))

            def select(l, i, b):
                for t in range(TT):
                    rk = rank[:, t, bass.ds(2 * i, 2)].unsqueeze(2).broadcast_to((P, 2, SLOTS))
                    ch.step(dve.tensor_tensor(sel[b][:, t], slot_no, rk, ALU.is_equal))
                if isinstance(i, int) and i < 2:
                    dve.wait_ge(x3_ready, 2 * (l + 1))
                ch.hold()
                for t in range(TT):
                    wt = cw[:, t, bass.ds(2 * i, 2)].unsqueeze(2).broadcast_to((P, 2, SLOTS))
                    ins = dve.tensor_tensor(sel_w[b][:, t], sel[b][:, t], wt, ALU.mult)
                ins.then_inc(sel_ready, 1)

            def accumulate(l, q, first):
                for c in range(4):
                    h, t = c // 2, c % 2
                    dve.wait_ge(scat_ps, 4 * q + c + 1)
                    cut = y_acc[:, t, HALF * h:HALF * (h + 1)]
                    if first:
                        dve.tensor_copy(cut, PS[:, SCAT[t], :]).then_inc(acc_done, 1)
                    else:
                        dve.tensor_tensor(cut, cut, PS[:, SCAT[t], :], ALU.add).then_inc(acc_done, 1)

            def accumulate_last(l):
                s, q = 2 * l + 1, PAIRS * (l + 1) - 1
                ch.hold()
                for c in range(4):
                    h, t = c // 2, c % 2
                    cut = slice(HALF * h, HALF * (h + 1))
                    dve.wait_ge(scat_ps, 4 * q + c + 1)
                    dve.tensor_tensor(gated[c], PS[:, SCAT[t], :], gates[:, s, cut], ALU.mult).then_inc(acc_done, 1)
                    dve.wait_ge(acc_done, 4 * q + c + 1)
                    dve.wait_ge(ahead_ready, 4 * l + c + 1)
                    ch.link(dve.tensor_tensor(y_acc[:, t, cut], y_acc[:, t, cut], gated[c], ALU.add))
                    half_stats(y_acc, t, h)
                ch.hold()

            def pair(l, i, b, first=False, second=False, tail=False):
                q = PAIRS * l + i
                dve.wait_ge(silu_ready, q + 1)
                dve.tensor_tensor(act_sb.rearrange("p (k f) -> p f k", k=KF), silu_sb.rearrange("p (f k) -> p f k", k=KF),
                                  PS[:, GU, FE:2 * FE].rearrange("p (f k) -> p f k", k=KF), ALU.mult).then_inc(act_ready, 1)
                dve.wait_ge(turn_ps, q + 1)
                dve.tensor_copy(turn[b], PS[:, TURN, 0:2 * P])
                ch.link(dve.tensor_copy(selT_hi[b][:, :], PS[:, TURN, 2 * P:4 * P]))
                dve.tensor_tensor(selT_lo[b][:, :], PS[:, TURN, 2 * P:4 * P], selT_hi[b][:, :].bitcast(F32), ALU.subtract)\
                   .then_inc(turn_sb, 1)
                if not first:
                    accumulate(l, q - 1, second)
                if not tail:
                    select(l, i + 2, b)
                for h in range(2):
                    dve.wait_ge(y_hi_ready, 2 * q + h + 1)
                    cut = slice(HALF * h, HALF * (h + 1))
                    dve.tensor_tensor(y_lo[:, cut], PS[:, DOWN[h], :], y_hi[:, cut].bitcast(F32), ALU.subtract)\
                       .then_inc(y_lo_ready, 1)

            def experts(l):
                select(l, 0, 0)
                select(l, 1, 1)
                pair(l, 0, 0, first=True)
                pair(l, 1, 1, second=True)
                with dve.Fori(1, PAIRS // 2 - 1) as j:
                    ch.enter(j - 1, 6)
                    for b in range(2):
                        pair(l, 2 * j + b, b)
                    ch.again()
                ch.leave(PAIRS // 2 - 2)
                pair(l, PAIRS - 2, 0, tail=True)
                pair(l, PAIRS - 1, 1, tail=True)
                flag = dve.value_load(over[0:1, 0:1])
                accumulate_last(l)
                d, s = dense[l], 2 * l + 1
                with dve.If(flag > 0):
                    with dve.Fori(0, EXPERTS) as e:
                        for t in range(TT):
                            n = 2 * e + t
                            dve.wait_ge(d["silu"], n + 1)
                            dve.scalar_tensor_tensor(act_sb.rearrange("p (k f) -> p f k", k=KF),
                                                     silu_sb.rearrange("p (f k) -> p f k", k=KF), cw_over[:, t, bass.ds(e, 1)],
                                                     PS[:, GU, FE:2 * FE].rearrange("p (f k) -> p f k", k=KF),
                                                     ALU.mult, ALU.mult).then_inc(d["act"], 1)
                            dve.wait_ge(d["turn"], n + 1)
                            dve.tensor_copy(turn[0][:, 0:2 * P], PS[:, TURN, 0:2 * P]).then_inc(d["turned"], 1)
                            dve.wait_ge(d["down"], n + 1)
                            for h in range(2):
                                dve.tensor_tensor(gated[h], PS[:, DOWN[h], :], gates[:, s, HALF * h:HALF * (h + 1)], ALU.mult)\
                                   .then_inc(d["gated"], 1)
                            for h in range(2):
                                z = y_acc[:, t, HALF * h:HALF * (h + 1)]
                                dve.wait_ge(d["gated"], 2 * n + h + 1)
                                dve.tensor_tensor(z, z, gated[h], ALU.add).then_inc(d["added"], 1)
                    dve.wait_ge(d["added"], 4 * EXPERTS)
                    for t in range(TT):
                        for h in range(2):
                            dve.bn_stats(stats[:, t, h, :], y_acc[:, t, HALF * h:HALF * (h + 1)]).then_inc(d["stats"], 1)
                    dve.wait_ge(d["stats"], 4)
                for t in range(TT):
                    variance(s, t)
                for t in range(TT):
                    normal(s, t)

            dve.wait_ge(c_silu_ready, 1)
            for n in range(2 * KD):
                ada_sum(n)

            dve.wait_ge(small_ld, 16 * SMALL_LOADS)
            dve.tensor_copy(pos_r, pos_i).then_inc(pos_rows, 1)
            third(0, 4)
            third(1, 5)
            h_banks(0)
            dve.wait_ge(columns_ps, 1)
            ch.step(dve.tensor_copy(gains[:, :], PS[:, 7, 0:31]))
            dve.tensor_copy(pos_f[:, :], PS[:, 7, 32:34]).then_inc(columns_sb, 1)
            ch.hold()
            dve.wait_ge(columns_sb, 1)
            tables = 0
            for trig, at, half, tmp in ((trig_m, C_INVM, ROPE // 2, M[:, 0:32]), (trig_r, C_INVR, DK // 2, M[:, 0:128])):
                n = tmp.shape[1]
                flat = [trig[:, u].rearrange("p t c -> p (t c)") for u in range(2)]
                ang, turns = M[:, 128:128 + n], M[:, 256:256 + n]
                for t in range(TT):
                    ch.step(dve.tensor_scalar(ang[:, half * t:half * (t + 1)], cst[:, at:at + half], pos_f[:, t:t + 1], None, ALU.mult))
                ch.hold()
                for u, quarter in ((0, 0.25), (1, 0.0)):
                    ch.link(dve.tensor_scalar(turns, ang, float(1 / TWO_PI), quarter, ALU.mult, ALU.add))
                    ch.link(dve.tensor_scalar(turns, turns, ROUND, None, ALU.add))
                    ch.link(dve.tensor_scalar(turns, turns, -ROUND, None, ALU.add))
                    ch.link(dve.scalar_tensor_tensor(tmp, turns, -PI_A, ang, ALU.mult, ALU.add))
                    ch.link(dve.scalar_tensor_tensor(tmp, turns, -PI_B, tmp, ALU.mult, ALU.add))
                    ch.link(dve.scalar_tensor_tensor(tmp, turns, -PI_C, tmp, ALU.mult, ALU.add))
                    ch.link(dve.tensor_scalar(tmp, tmp, float(quarter * TWO_PI), SIN_MAX, ALU.add, ALU.min))
                    dve.tensor_scalar(flat[u], tmp, -SIN_MAX, None, ALU.max).then_inc(angle_ready, 1)
                    tables += 1
                    dve.wait_ge(angle_ready, tables)
            for t in range(TT):
                dve.wait_ge(lowrank_ps, t + 1)
                dve.tensor_copy(low[:, t, :], PS[:, t, 0:LOWRANK]).then_inc(lowrank_sb, 1)
            ch.step(dve.memset(conv_u[:, :, 0:2], 0.0))
            dve.wait_ge(square_ready, TT)
            dve.wait_ge(act_chain, TT)
            sq = soft[:, 0:4].rearrange("p (t c) -> p t c", t=TT)
            ms = soft[:, 4:8].rearrange("p (t c) -> p t c", t=TT)
            dve.tensor_scalar(ms[:, :, 0:1], sq[:, :, 0:1], 1.0 / QR, RMS_EPS, ALU.mult, ALU.add).then_inc(ms_ready, 1)
            dve.tensor_scalar(ms[:, :, 1:2], sq[:, :, 1:2], 1.0 / KVR, RMS_EPS, ALU.mult, ALU.add).then_inc(ms_ready, 1)
            dve.wait_ge(rms_ready, 1)
            ch.link(dve.reciprocal(soft[:, 12:16], soft[:, 8:12]))
            for t in range(TT):
                ch.step(dve.tensor_scalar(low[:, t, 0:QR], low[:, t, 0:QR], soft[:, 12 + 2 * t:13 + 2 * t], None, ALU.mult))
                dve.tensor_scalar(low[:, t, QR:QR + KVR], low[:, t, QR:QR + KVR], soft[:, 13 + 2 * t:14 + 2 * t], None,
                                  ALU.mult).then_inc(lowrank_n, 1)
            dve.wait_ge(lowT_ps, 1)
            for k in range(3):
                ins = dve.tensor_scalar(lowT[:, k, :], PS[:, k // 2, 256 * (k % 2):256 * (k % 2) + 256],
                                        q_g[:, k:k + 1] if k < 2 else kv_g[:, 0:1], None, ALU.mult)
            ins.then_inc(lowT_ready, 1)
            for n in range(2 * KD, 3 * KD):
                ada_sum(n)
            dve.wait_ge(trig_ready, 1)
            dve.wait_ge(up_q_sb, 4)
            for t in range(TT):
                bc = lambda v: v.unsqueeze(1).broadcast_to((P, HEADS, ROPE // 2))
                view = lambda v: v[:, 128 * t:128 * t + 128].rearrange("p (h c) -> p h c", h=HEADS)
                ins = rope(dve, ch, q_sb[:, t], q_sb[:, t], NOPE, ROPE // 2, bc(trig_m[:, 0, t]), bc(trig_m[:, 1, t]), rope_t, view)
                if t < TT - 1:
                    ch.step(ins)
            ins.then_inc(qk_ready, 1)
            dve.wait_ge(qk_ready, 1)
            ins = rope(dve, ch, low[:, :, QR + KVR:], low[:, :, QR + KVR:], 0, ROPE // 2, trig_m[:, 0], trig_m[:, 1], rope_t,
                       lambda v: v[:, 0:32].rearrange("p (t c) -> p t c", t=TT))
            ch.link(ins)
            dve.wait_ge(up_k_sb, 8)
            for t in range(TT):
                ins = dve.tensor_copy(k_sb[:, t, :, NOPE:], low[:, t, QR + KVR:].unsqueeze(1).broadcast_to((P, HEADS, ROPE)))
            ins.then_inc(qk_ready, 1)

            for n in range(4):
                dve.wait_ge(qkT_ps, n + 1)
                dve.tensor_copy(qT0[:, 2 * n:2 * n + 2, :].rearrange("p h t -> p (h t)"), PS[0:QK, n, :]).then_inc(qT_ready, 1)

            def conv(i):
                c = i % CT
                half = PS[:, 4 + c % 2, 256 * (c // 2):256 * (c // 2) + 256]
                dve.wait_ge(conv_ps, CT + i + 1)
                if i < CT:
                    if i == 0:
                        dve.wait_ge(conv_x_sb, 2)
                    dve.tensor_tensor(conv_u[:, c, 2:], conv_x[:, c, :], half, ALU.mult).then_inc(conv_used, 1)
                    dve.wait_ge(conv_used, c + 1)
                    ch.link(dve.tensor_scalar(yT0[:, c, :], conv_u[:, c, 0:SEQ], conv_w[:, 0, c:c + 1], None, ALU.mult))
                    for j in (1, 2):
                        ch.step(dve.scalar_tensor_tensor(yT0[:, c, :], conv_u[:, c, j:SEQ + j], conv_w[:, j, c:c + 1],
                                                         yT0[:, c, :], ALU.mult, ALU.add))
                        if j == 1:
                            ch.hold()
                else:
                    ch.hold()
                    dve.tensor_tensor(yT0[:, c, :], yT0[:, c, :], half, ALU.mult).then_inc(conv_used, 1)

            def softmax_shift(h):
                b = h % 2
                dve.wait_ge(score_ps, h + 1)
                if h >= 2:
                    dve.wait_ge(prob_ready, 2 * (h - 1))
                ch.link(dve.tensor_tensor(score[:, b, :], PS[:, b, 0:3 * P], cst[:, C_MASK:C_MASK + 3 * P], ALU.add))
                at = 64 + 2 * h
                ch.step(dve.tensor_reduce(soft[:, at:at + 1], score[:, b, 0:P], AX.X, ALU.max))
                ch.link(dve.tensor_reduce(soft[:, at + 1:at + 2], score[:, b, P:3 * P], AX.X, ALU.max))
                dve.tensor_scalar(soft[:, 16 + 2 * h:18 + 2 * h], soft[:, at:at + 2], -MLA_SCALE, None, ALU.mult).then_inc(shift_ready, 1)

            softmax_shift(0)
            n = 3 * KD
            for h in range(HEADS):
                if h + 1 < HEADS:
                    softmax_shift(h + 1)
                dve.wait_ge(prob_ready, 2 * (h + 1))
                dve.reciprocal(soft[:, 96 + 2 * h:98 + 2 * h], soft[:, 32 + 2 * h:34 + 2 * h]).then_inc(psum_inv, 1)
                conv(h)
                for n in range(n, n + WITH_HEAD):
                    if n not in SHARED:
                        ada_sum(n)
                n += 1
                if h == 2:
                    third(2, 6)
                if h == 5:
                    third(3, 6)
            dve.wait_ge(oT_ps, 1)
            for k in range(4):
                ins = dve.tensor_copy(yT0[:, 4 + k, :], PS[:, 6 + k // 2, 256 * (k % 2):256 * (k % 2) + 256])
            ins.then_inc(oT_ready, 1)
            third(4, 4)
            for n in range(n, 7 * KD):
                ada_sum(n)
            third(5, 4)
            for n in range(7 * KD, 7 * KD + 4):
                ada_sum(n)
            residual(0, 0)
            variance(0, 0)
            for n in range(7 * KD + 4, LATE):
                ada_sum(n)
            residual(0, 1)
            normal(0, 0)
            variance(0, 1)
            normal(0, 1)

            h_banks(1)
            for m, bank in ((6, 6), (7, 7)):
                third(m, bank)
            router(0)
            experts(0)

            h_banks(2)
            for i in range(2):
                half = slice(D * i, D * (i + 1))
                dve.wait_ge(h_hi_ready, i + 1)
                dve.tensor_tensor(h_lo[:, half], hflat[:, half], h_hi[:, half].bitcast(F32), ALU.subtract).then_inc(h_lo_ready, 1)
            dve.wait_ge(h_lo_ready, 2)

            def ret_turned(u):
                for n in range(4):
                    dve.wait_ge(retT_ps, 4 * u + n + 1)
                    dve.tensor_copy(qkT1[u][:, 2 * n:2 * n + 2, :].rearrange("p h t -> p (h t)"), PS[:, 4 + n, :])\
                       .then_inc(retT_ready, 1)

            def decayed_scores(h):
                b = h % 2
                dve.wait_ge(rscore_ps, h + 1)
                if h >= 2:
                    dve.wait_ge(rhead_ps, h - 1)
                dve.tensor_tensor(sT1[:, b, 0:SEQ], PS[:, 4 + b, 0:SEQ], decay[:, h, :], ALU.mult)
                dve.tensor_tensor(sT1[:, b, SEQ:SEQ + P], PS[:, 4 + b, SEQ:SEQ + P], decay[:, h, 0:P], ALU.mult).then_inc(decayed, 1)

            def head_stats(h):
                dve.wait_ge(rhead_sb, 2 * (h + 1))
                for t in range(TT):
                    ch.step(dve.bn_stats(rstat[:, t, h, :], o1[:, t, DV * h:DV * (h + 1)]))

            def pair_var(p):
                head_stats(2 * p)
                head_stats(2 * p + 1)
                ch.hold()
                for t in range(TT):
                    for h in (2 * p, 2 * p + 1):
                        ch.step(dve.bn_aggr(rmv[:, t, h, :], rstat[:, t, h, :]))
                ch.hold()
                pair = slice(2 * p, 2 * p + 2)
                ch.link(dve.tensor_scalar(rrs[:, :, pair], rmv[:, :, pair, 1], LN_EPS, None, ALU.add))
                dve.reciprocal(rsd[:, :, pair], rrs[:, :, pair]).then_inc(rvar_ready, 1)

            def pair_norm(p):
                dve.wait_ge(rstd_ready, p + 1)
                for t in range(TT):
                    for h in (2 * p, 2 * p + 1):
                        o = o1[:, t, DV * h:DV * (h + 1)]
                        ch.step(dve.tensor_scalar(o, o, rmv[:, t, h, 0:1], rsd[:, t, h:h + 1], ALU.subtract, ALU.mult))
                ch.hold()
                dve.wait_ge(ret_sb, 2 * (8 + p + 1))
                for t in range(TT):
                    cut = slice(HALF * p, HALF * (p + 1))
                    ins = dve.tensor_tensor(o1[:, t, cut], o1[:, t, cut], g1[:, t, cut], ALU.mult)
                    if t < TT - 1:
                        ch.step(ins)
                ins.then_inc(ret_y, 1)

            def turned_y(n):
                dve.wait_ge(ryT_hi, 2 * n + 2)
                for k in (2 * n, 2 * n + 1):
                    dve.scalar_tensor_tensor(yT_lo[:, SEQ * k:SEQ * (k + 1)], PS[:, 4 + n % 4, 256 * (k % 2):256 * (k % 2) + 256],
                                             gn_g[:, k:k + 1], yT_hi[:, SEQ * k:SEQ * (k + 1)].bitcast(F32), ALU.mult, ALU.subtract)\
                       .then_inc(ryT_lo, 1)

            dve.wait_ge(w_lo_ready, 2)
            late = LATE
            for c in range(RET_CHUNKS):
                split_lo(dve, 2 * c + 2)
                if c >= 9:
                    pair_var(c - 9)
                ada_sum(late)
                split_lo(dve, 2 * c + 3)
                if c == RET_CHUNKS - 1:
                    turned_y(0)
                    turned_y(1)
                if c >= 9:
                    pair_norm(c - 9)
                if c == 3:
                    ret_turned(0)
                if c == 4:
                    third(8, 4)
                if c == 5:
                    ret_turned(1)
                    dve.wait_ge(decay_ld, 16)
                if c == 7:
                    third(9, 6)
                if 7 <= c < 11:
                    decayed_scores(2 * (c - 7))
                    decayed_scores(2 * (c - 7) + 1)
                for n in range(1, LATE_AT[c]):
                    ada_sum(late + n)
                late += LATE_AT[c]
            pair_var(RH // 2 - 1)
            pair_norm(RH // 2 - 1)
            turned_y(2)
            for n in range(3, RH + 1):
                split_lo(dve, RET_PARTS + n - 1)
                if n < RH:
                    turned_y(n)
            residual(2, 0)
            variance(2, 0)
            residual(2, 1)
            normal(2, 0)
            variance(2, 1)
            normal(2, 1)

            third(10, 4)
            third(11, 6)
            h_banks(3)
            router(1)
            experts(1)

        @block.gpsimd
        def _(pool):
            ch = Chain(pool, pool_chain)

            def x_with_gain(s):
                pool.wait_ge(xT_ps, 4 * (s + 2))
                if s % 2 == 0:
                    pool.wait_ge(x3_ready, s + 2)
                pool.wait_ge(ln_ld, 32 * (s + 1))
                for t in range(TT):
                    ch.link(pool.tensor_tensor(x[:, t, :], x[:, t, :], ln_g[:, :], ALU.mult))
                    ins = pool.tensor_tensor(x[:, t, :], x[:, t, :], ln_b[:, :], ALU.add)
                    if s % 2 == 0:
                        ch.link(ins)
                        ins = pool.tensor_scalar(x[:, t, :], x[:, t, :], ALPHA, None, ALU.mult)
                    ins.then_inc(x_full, 1)

            def residual_ahead(l):
                s = 2 * l + 1
                pool.wait_ge(third_ready, 3 * s + 3)
                pool.wait_ge(x_full, 2 * s)
                for c in range(4):
                    h, t = c // 2, c % 2
                    cut = slice(HALF * h, HALF * (h + 1))
                    y = y_acc[:, t, cut]
                    pool.wait_ge(acc_done, 4 * (PAIRS * (l + 1) - 2) + c + 1)
                    ch.link(pool.tensor_tensor(y, y, gates[:, s, cut], ALU.mult))
                    pool.tensor_tensor(y, y, x[:, t, cut], ALU.add).then_inc(ahead_ready, 1)

            def ret_rope(u):
                for t in range(TT):
                    pool.wait_ge(ret_sb, 4 * u + 2 + t + 1)
                    if u:
                        pool.wait_ge(retT_ps, 4)
                    cos, sin = (trig_r[:, v, t].unsqueeze(1).broadcast_to((P, RH, DK // 2)) for v in range(2))
                    if u or t:
                        pool.wait_ge(rope_ready, 2 * u + t)
                    ins = rope(pool, ch, raw1[:, t], turned1[:, t], 0, DK // 2, cos, sin, rope_r, lambda v: v)
                    ins.then_inc(rope_ready, 1)

            for i, n in enumerate(SHARED):
                acc = ada_acc(n // KD)
                pool.wait_ge(ada_scaled, i + 1)
                pool.wait_ge(ada_used, n)
                pool.tensor_tensor(acc, acc, ada_buf(n), ALU.add).then_inc(ada_used, 1)
            x_with_gain(0)
            residual_ahead(0)
            split_lo(pool, 0)
            split_lo(pool, 1)
            x_with_gain(1)
            ret_rope(0)
            ret_rope(1)
            x_with_gain(2)
            residual_ahead(1)


_INS = ['x', 'c', 'positions', 'ada_mix_w', 'ada_mix_b', 'ln_mix_g', 'ln_mix_b',
        'ab_w_in', 'ab_conv_w', 'ab_q_norm_g', 'ab_kv_norm_g', 'ab_w_uq', 'ab_w_ukv', 'ab_w_out',
        'ret_w_in', 'ret_gn_g', 'ret_w_out', 'ada_ffn_w', 'ada_ffn_b', 'ln_ffn_g', 'ln_ffn_b',
        'moe_rg_w', 'moe_rg_b', 'moe_re_w', 'moe_re_b', 'moe_w_gate', 'moe_w_up', 'moe_w_down']


def kernel(**inputs):
    import concourse.bacc as bacc
    from concourse.bass_utils import run_bass_kernel_spmd

    nc = bacc.Bacc("TRN2", target_bir_lowering=False, num_devices=1)
    arrays = {name: np.ascontiguousarray(inputs[name]) for name in _INS}
    arrays["table"], arrays["decay"] = shape_constants()
    aps = {name: nc.dram_tensor(f"in_{name}", v.shape, mybir.dt.from_np(v.dtype), kind="ExternalInput").ap()
           for name, v in arrays.items()}
    out = nc.dram_tensor("out_0", (1, SEQ, D), F32, kind="ExternalOutput").ap()
    build(nc, aps, out)
    got = run_bass_kernel_spmd(nc, [{f"in_{name}": v for name, v in arrays.items()}], core_ids=[0])
    return got.results[0]["out_0"]
```
